# Optimizing a Trainium2 kernel written in Bass

```python
import jax, jax.numpy as jnp
from jax import lax
import numpy as np

D_MODEL = 1024
BATCH = 1
SEQ = 1024
DEPTH = 1

CHUNK = 64
WINDOW = 128
WIN_CHUNKS = WINDOW // CHUNK
HEAD_DIM = 64
N_Q_HEADS = 8
N_KV_HEADS = 2
Q_PER_KV = N_Q_HEADS // N_KV_HEADS
ATTN_WIDTH = N_Q_HEADS * HEAD_DIM
KV_WIDTH = N_KV_HEADS * HEAD_DIM
ROPE_THETA = 10000.0
CONV_WIDTH = D_MODEL // 2
CONV_K = 3
D_FF = 2816
FFN_RES = 0.5
ALPHA = (2.0 * DEPTH) ** 0.25
BETA = (8.0 * DEPTH) ** -0.25
LN_EPS = 1e-5
N_COND = 9
MAX_OFFSET = 1 << 14
SPLIT_Q = ATTN_WIDTH
SPLIT_K = SPLIT_Q + KV_WIDTH
SPLIT_V = SPLIT_K + KV_WIDTH
SPLIT_CB = SPLIT_V + CONV_WIDTH
SPLIT_CC = SPLIT_CB + CONV_WIDTH
SPLIT_CX = SPLIT_CC + CONV_WIDTH
SPLIT_GA = SPLIT_CX + D_MODEL
IN_WIDTH = SPLIT_GA + D_MODEL

kernel_name = "hybrid_swa_shortconv_macaron_encoder"

def layer_norm(x, g, b):
    xf = x.astype(jnp.float32)
    mu = jnp.mean(xf, axis=-1, keepdims=True)
    var = jnp.mean(jnp.square(xf - mu), axis=-1, keepdims=True)
    y = (xf - mu) * lax.rsqrt(var + LN_EPS) * g.astype(jnp.float32) + b.astype(jnp.float32)
    return y.astype(x.dtype)

def swiglu(h, w1, w3, w2):
    return (jax.nn.silu(h @ w1) * (h @ w3)) @ w2

def rope(t, positions):
    half = HEAD_DIM // 2
    inv = ROPE_THETA ** (-jnp.arange(half, dtype=jnp.float32) / half)
    ang = positions.astype(jnp.float32)[..., None] * inv
    cos = jnp.cos(ang)[:, :, None, :]
    sin = jnp.sin(ang)[:, :, None, :]
    t1 = t[..., :half].astype(jnp.float32)
    t2 = t[..., half:].astype(jnp.float32)
    out = jnp.concatenate([t1 * cos - t2 * sin, t2 * cos + t1 * sin], axis=-1)
    return out.astype(t.dtype)

def banded_sink_attention(q, k, v, sinks):
    b, s = q.shape[0], q.shape[1]
    nc = s // CHUNK
    band_len = WIN_CHUNKS * CHUNK
    qc = q.reshape(b, nc, CHUNK, N_KV_HEADS, Q_PER_KV, HEAD_DIM)

    def band(t):
        tc = t.reshape(b, nc, CHUNK, N_KV_HEADS, HEAD_DIM)
        parts = [jnp.pad(tc, ((0, 0), (sh, 0), (0, 0), (0, 0), (0, 0)))[:, :nc]
                 for sh in range(WIN_CHUNKS - 1, -1, -1)]
        return jnp.concatenate(parts, axis=2)

    kb, vb = band(k), band(v)
    key_chunk = (jnp.arange(nc)[:, None] - (WIN_CHUNKS - 1)
                 + jnp.arange(band_len)[None, :] // CHUNK)
    valid = key_chunk >= 0
    scores = jnp.einsum('bnqgrd,bnkgd->bgrnqk', qc, kb).astype(jnp.float32) * (HEAD_DIM ** -0.5)
    scores = jnp.where(valid[:, None, :], scores, jnp.finfo(jnp.float32).min)
    sink = jnp.broadcast_to(sinks.astype(jnp.float32).reshape(1, N_KV_HEADS, Q_PER_KV, 1, 1, 1),
                            scores.shape[:-1] + (1,))
    probs = jax.nn.softmax(jnp.concatenate([scores, sink], axis=-1), axis=-1)[..., :-1]
    out = jnp.einsum('bgrnqk,bnkgd->bnqgrd', probs.astype(v.dtype), vb)
    return out.reshape(b, s, ATTN_WIDTH)

def causal_depthwise_conv(u, w):
    kern = w[:, None, :].astype(u.dtype)
    return lax.conv_general_dilated(u, kern, window_strides=(1,), padding=[(CONV_K - 1, 0)],
                                    dimension_numbers=('NWC', 'WIO', 'NWC'),
                                    feature_group_count=CONV_WIDTH)

def hybrid_mixer(h, positions, w_in, sinks, conv_w, w_branch_attn, w_branch_conv, w_out):
    b, s, _ = h.shape
    proj = h @ w_in
    q = proj[..., :SPLIT_Q].reshape(b, s, N_Q_HEADS, HEAD_DIM)
    k = proj[..., SPLIT_Q:SPLIT_K].reshape(b, s, N_KV_HEADS, HEAD_DIM)
    v = proj[..., SPLIT_K:SPLIT_V].reshape(b, s, N_KV_HEADS, HEAD_DIM)
    gate_b = proj[..., SPLIT_V:SPLIT_CB]
    gate_c = proj[..., SPLIT_CB:SPLIT_CC]
    conv_x = proj[..., SPLIT_CC:SPLIT_CX]
    merge_a = proj[..., SPLIT_CX:SPLIT_GA]
    merge_c = proj[..., SPLIT_GA:]
    attn = banded_sink_attention(rope(q, positions), rope(k, positions), v, sinks)
    conv = gate_b * causal_depthwise_conv(gate_c * conv_x, conv_w)
    merged = (jax.nn.sigmoid(merge_a) * (attn @ w_branch_attn)
              + jax.nn.sigmoid(merge_c) * (conv @ w_branch_conv))
    return merged @ w_out

def setup_inputs(seed: int = 0) -> dict:
    key = jax.random.key(seed)
    ks = jax.random.split(key, 24)
    f32 = jnp.float32

    def nrm(k, shape, scale):
        return jax.random.normal(k, shape, f32) * scale

    d = D_MODEL
    x = nrm(ks[0], (BATCH, SEQ, d), 1.0)
    c = nrm(ks[1], (BATCH, d), 1.0)
    offsets = jax.random.randint(ks[2], (BATCH, 1), 0, MAX_OFFSET, dtype=jnp.int32)
    positions = (offsets + jnp.arange(SEQ, dtype=jnp.int32)[None, :]).astype(jnp.int32)
    w_cond = nrm(ks[3], (DEPTH, d, N_COND * d), 0.5 * d ** -0.5)
    b_cond = nrm(ks[4], (DEPTH, N_COND * d), 0.02)
    ffn1_w1 = nrm(ks[5], (DEPTH, d, D_FF), d ** -0.5)
    ffn1_w3 = nrm(ks[6], (DEPTH, d, D_FF), d ** -0.5)
    ffn1_w2 = nrm(ks[7], (DEPTH, D_FF, d), BETA * D_FF ** -0.5)
    ln1_g = 1.0 + nrm(ks[8], (DEPTH, d), 0.02)
    ln1_b = nrm(ks[9], (DEPTH, d), 0.02)
    w_in = nrm(ks[10], (DEPTH, d, IN_WIDTH), d ** -0.5)
    w_in = w_in.at[..., SPLIT_K:SPLIT_V].multiply(BETA)
    w_in = w_in.at[..., SPLIT_CC:SPLIT_CX].multiply(BETA)
    attn_sinks = nrm(ks[11], (DEPTH, N_Q_HEADS), 1.0)
    conv_w = nrm(ks[12], (DEPTH, CONV_K, CONV_WIDTH), CONV_K ** -0.5)
    w_branch_attn = nrm(ks[13], (DEPTH, ATTN_WIDTH, d), ATTN_WIDTH ** -0.5)
    w_branch_conv = nrm(ks[14], (DEPTH, CONV_WIDTH, d), CONV_WIDTH ** -0.5)
    w_out = nrm(ks[15], (DEPTH, d, d), BETA * d ** -0.5)
    ln2_g = 1.0 + nrm(ks[16], (DEPTH, d), 0.02)
    ln2_b = nrm(ks[17], (DEPTH, d), 0.02)
    ffn2_w1 = nrm(ks[18], (DEPTH, d, D_FF), d ** -0.5)
    ffn2_w3 = nrm(ks[19], (DEPTH, d, D_FF), d ** -0.5)
    ffn2_w2 = nrm(ks[20], (DEPTH, D_FF, d), BETA * D_FF ** -0.5)
    ln3_g = 1.0 + nrm(ks[21], (DEPTH, d), 0.02)
    ln3_b = nrm(ks[22], (DEPTH, d), 0.02)
    return {"x": x, "c": c, "positions": positions, "w_cond": w_cond, "b_cond": b_cond,
            "ffn1_w1": ffn1_w1, "ffn1_w3": ffn1_w3, "ffn1_w2": ffn1_w2,
            "ln1_g": ln1_g, "ln1_b": ln1_b, "w_in": w_in, "attn_sinks": attn_sinks,
            "conv_w": conv_w, "w_branch_attn": w_branch_attn, "w_branch_conv": w_branch_conv,
            "w_out": w_out, "ln2_g": ln2_g, "ln2_b": ln2_b,
            "ffn2_w1": ffn2_w1, "ffn2_w3": ffn2_w3, "ffn2_w2": ffn2_w2,
            "ln3_g": ln3_g, "ln3_b": ln3_b}

def reference(x, c, positions, w_cond, b_cond, ffn1_w1, ffn1_w3, ffn1_w2, ln1_g, ln1_b,
              w_in, attn_sinks, conv_w, w_branch_attn, w_branch_conv, w_out, ln2_g, ln2_b,
              ffn2_w1, ffn2_w3, ffn2_w2, ln3_g, ln3_b):
    b, _, d = x.shape
    cs = jax.nn.silu(c)
    for l in range(DEPTH):
        mod = (cs @ w_cond[l] + b_cond[l]).reshape(b, N_COND, d)
        sh1, sc1, g1, sh2, sc2, g2, sh3, sc3, g3 = [mod[:, i, None, :] for i in range(N_COND)]
        h = x * (1.0 + sc1) + sh1
        x = layer_norm(ALPHA * x + FFN_RES * g1 * swiglu(h, ffn1_w1[l], ffn1_w3[l], ffn1_w2[l]),
                       ln1_g[l], ln1_b[l])
        h = x * (1.0 + sc2) + sh2
        mix = hybrid_mixer(h, positions, w_in[l], attn_sinks[l], conv_w[l],
                           w_branch_attn[l], w_branch_conv[l], w_out[l])
        x = layer_norm(ALPHA * x + g2 * mix, ln2_g[l], ln2_b[l])
        h = x * (1.0 + sc3) + sh3
        x = layer_norm(ALPHA * x + FFN_RES * g3 * swiglu(h, ffn2_w1[l], ffn2_w3[l], ffn2_w2[l]),
                       ln3_g[l], ln3_b[l])
    return x


_drawn_inputs = setup_inputs


def setup_inputs(seed=0):
    import zlib

    import numpy as np

    out = dict(_drawn_inputs(seed))
    spreads = {}
    factors = {'b_cond': 7.054,
     'ln1_g': 2.998,
     'ln1_b': 2.835,
     'attn_sinks': 64.0,
     'w_branch_attn': 3.487,
     'ln2_g': 8.16,
     'ln2_b': 8.095,
     'ln3_g': 7.619,
     'ln3_b': 7.795}
    for name, (base, spread) in spreads.items():
        noise = np.random.default_rng([zlib.crc32(name.encode()), seed]).standard_normal(out[name].shape)
        drawn = base * np.exp(spread * noise) if base else spread * noise
        out[name] = __import__('jax').numpy.asarray(drawn.astype(out[name].dtype))
    for name, factor in factors.items():
        out[name] = (out[name] * factor).astype(out[name].dtype)
    return out
```

```python
from contextlib import ExitStack

import concourse.bass as bass
from concourse import mybir
import numpy as np

F32 = mybir.dt.float32
F32R = mybir.dt.float32r
I32 = mybir.dt.int32
ALU = mybir.AluOpType
ACT = mybir.ActivationFunctionType
AX = mybir.AxisListType

P = 128
D = 1024
SEQ = 1024
HALF = SEQ // 2
KD = D // P
D_FF = 2816
FF_TILES = D_FF // P
CHUNK = 64
HEAD_DIM = 64
Q_HEADS = 8
Q_TILES = Q_HEADS * HEAD_DIM // P
CONV_WIDTH = D // 2
CONV_TILES = CONV_WIDTH // P
CONV_K = 3
N_COND = 9
ALPHA = 2.0 ** 0.25
FFN_RES = 0.5
LN_EPS = 1e-5
SCALE = HEAD_DIM ** -0.5
MASKED = -3.0e38
ROPE_THETA = 10000.0

GRAN = KD * P
FF_STEPS = FF_TILES // 2
UP_FFN = 2 * FF_TILES
PROJ = 2 + Q_TILES + 3 * CONV_TILES
MERGE = 3 * KD
UP_MIX = PROJ + MERGE
UP_ALL = 2 * UP_FFN + UP_MIX
MIX_STEPS = KD // 2
DOWN_ALL = 2 * FF_TILES + KD
UP_TOTAL = 2 * UP_FFN + 2 * UP_MIX

PC_BCOND = 0
PC_C = PC_BCOND + N_COND * KD
PC_LN = PC_C + KD
PC_CONV = PC_LN + 6 * KD
PC_SINK = PC_CONV + CONV_K * CONV_TILES
PC_INV = PC_SINK + Q_TILES
PC_SIGN = PC_INV + 1
PC_ONE = PC_SIGN + 1
PC_ALL = PC_ONE + 1

TWO_PI = 2.0 * np.pi
CW1 = 6.28125
CW2 = float(np.floor((TWO_PI - CW1) * 2.0 ** 19) / 2.0 ** 19)
CW3 = float(np.float32(TWO_PI - CW1 - CW2))
ROUND = float(1.5 * 2.0 ** 23)
PI_BELOW = float(np.nextafter(np.float32(np.pi), np.float32(0)))


def encoder_block(nc, x, pos, table, mean_w, w_cond, up_w, down_w, out):
    with ExitStack() as ctx:
        def sem(name):
            return ctx.enter_context(nc.semaphore(name))

        at = [nc.sbuf_base + (-nc.sbuf_base) % 32]

        def place(name, shape, dt=F32, offset=None):
            size = 4 * int(np.prod(shape[1:]))
            if offset is None:
                offset = at[0]
                at[0] = offset + size + (-size) % 32
            return nc.alloc_sbuf_tensor_at(name, shape, dt, offset=offset), offset + size + (-size) % 32

        res, _ = place("res", [P, KD, SEQ])
        h_hi, _ = place("h_hi", [P, KD, SEQ], F32R)
        h_lo, _ = place("h_lo", [P, KD, SEQ], F32R)
        up_raw, _ = place("up_raw", [P, 2, KD, P])
        up_hi, _ = place("up_hi", [P, 2, KD, P], F32R)
        up_lo, _ = place("up_lo", [P, 2, KD, P], F32R)
        dn_raw, _ = place("dn_raw", [P, 2, D])
        dn_hi, _ = place("dn_hi", [P, 2, D], F32R)
        dn_lo, _ = place("dn_lo", [P, 2, D], F32R)
        tmp, _ = place("tmp", [P, 4, HALF])
        cos_t, _ = place("cos_t", [P, SEQ])
        sin_t, _ = place("sin_t", [P, SEQ])
        mean_m, _ = place("mean_m", [P, P])
        eye, _ = place("eye", [P, P])
        par, _ = place("par", [P, PC_ALL])
        mod, _ = place("mod", [P, N_COND, KD])
        coef, _ = place("coef", [P, 16, KD])
        cs, _ = place("cs", [P, KD])
        negsink, _ = place("negsink", [P, Q_TILES])
        small, _ = place("small", [P, 2, 6, Q_TILES])
        ucarry, _ = place("ucarry", [P, CONV_TILES, CONV_K - 1])
        shared = at[0]
        g_hi, o = place("g_hi", [P, 2, SEQ], F32R, shared)
        g_lo, o = place("g_lo", [P, 2, SEQ], F32R, o)
        crow, o = place("crow", [P, 4, D], F32, o)
        cacc, o = place("cacc", [P, D], F32, o)
        pos_i, o = place("pos_i", [P, SEQ], I32, o)
        ang, o = place("ang", [P, SEQ], F32, o)
        turn, o = place("turn", [P, SEQ], F32, o)
        turns, o = place("turns", [P, SEQ], F32, o)
        attn_hi, o = place("attn_hi", [P, Q_TILES, HALF], F32R, shared)
        attn_lo, o = place("attn_lo", [P, Q_TILES, HALF], F32R, o)
        conv_hi, o = place("conv_hi", [P, CONV_TILES, HALF], F32R, o)
        conv_lo, o = place("conv_lo", [P, CONV_TILES, HALF], F32R, o)
        q_at = o
        qT, o = place("qT", [P, Q_TILES, HALF], F32, q_at)
        mg_hi, o2 = place("mg_hi", [P, 2, HALF], F32R, q_at)
        mg_lo, _ = place("mg_lo", [P, 2, HALF], F32R, o2)
        kT, o = place("kT", [P, CHUNK + HALF], F32, o)
        vT, o = place("vT", [P, CHUNK + HALF], F32, o)
        vband, o = place("vband", [P, HALF // CHUNK, P], F32, o)
        ubuf, o = place("ubuf", [P, CONV_K - 1 + HALF], F32, o)
        e_at = o
        prob, o = place("prob", [P, 2, Q_TILES, P], F32, e_at)
        probT, o = place("probT", [P, 2, Q_TILES, P], F32, o)
        presum, o2 = place("presum", [P, HALF], F32, e_at)
        rstd, _ = place("rstd", [P, HALF], F32, o2)

        ps = ctx.enter_context(nc.psum_tensor("ps", [P, 8, 512], F32))

        (C_SC0, C_H1S, C_H1B, C_R1S, C_R1B, C_H2S, C_H2B, C_R2S, C_R2B, C_G1, C_G3, C_ONE2,
         C_ONE3) = range(13)

        def col(v, k):
            return v[:, k:k + 1]

        tables_in = sem("tables_in")
        pos_in = sem("pos_in")
        x_in = [sem("x_in0"), sem("x_in1")]
        up_in = [sem("up_in0"), sem("up_in1")]
        dn_in = [sem("dn_in0"), sem("dn_in1")]
        crow_in = [sem(f"crow_in{i}") for i in range(4)]
        up_hi_done = sem("up_hi_done")
        up_lo_done = sem("up_lo_done")
        dn_hi_done = sem("dn_hi_done")
        dn_lo_done = sem("dn_lo_done")
        up_mm = sem("up_mm")
        dn_mm = sem("dn_mm")
        dn_acc = sem("dn_acc")
        gate_read = sem("gate_read")
        prod_done = sem("prod_done")
        g_hi_done = sem("g_hi_done")
        g_ready = sem("g_ready")
        cs_ready = sem("cs_ready")
        crow_used = sem("crow_used")
        mod_sum = sem("mod_sum")
        mod_ready = sem("mod_ready")
        coef_done = sem("coef_done")
        rope_steps = sem("rope_steps")
        trig_done = sem("trig_done")
        sin_ready = sem("sin_ready")
        ln_sum = sem("ln_sum")
        ln_mean = sem("ln_mean")
        ln_centred = sem("ln_centred")
        ln_sq = sem("ln_sq")
        ln_sqmm = sem("ln_sqmm")
        ln_var = sem("ln_var")
        ln_rcp = sem("ln_rcp")
        ln_rstd = sem("ln_rstd")
        ln_y = sem("ln_y")
        hf_done = sem("hf_done")
        hhi_done = sem("hhi_done")
        h_ready = sem("h_ready")
        r_scaled = sem("r_scaled")
        proj_read = sem("proj_read")
        dve_step = sem("dve_step")
        qkv_ready = sem("qkv_ready")
        carried = sem("carried")
        vband_mm = sem("vband_mm")
        vband_ready = sem("vband_ready")
        score_mm = sem("score_mm")
        negmax_done = sem("negmax_done")
        exp_done = sem("exp_done")
        probs_ready = sem("probs_ready")
        probT_mm = sem("probT_mm")
        probT_ready = sem("probT_ready")
        av_mm = sem("av_mm")
        attn_hi_done = sem("attn_hi_done")
        attn_ready = sem("attn_ready")
        conv_done = sem("conv_done")
        conv_hi_done = sem("conv_hi_done")
        conv_ready = sem("conv_ready")
        merge_parts = sem("merge_parts")
        y_ready = sem("y_ready")
        stored = sem("stored")

        UPB_MIX = [UP_FFN, UP_FFN + UP_MIX]
        UPB_FFN2 = UP_FFN + 2 * UP_MIX
        DNB_MIX = [FF_TILES, FF_TILES + KD]
        DNB_FFN2 = FF_TILES + 2 * KD
        TL_MIX = [FF_TILES, FF_TILES + KD]
        TL_FFN2 = FF_TILES + 2 * KD
        GR_MIX = [FF_TILES, FF_TILES + 2 * KD]
        GR_FFN2 = FF_TILES + 4 * KD
        CH_MIX = [FF_STEPS, FF_STEPS + MIX_STEPS]
        CH_FFN2 = FF_STEPS + 2 * MIX_STEPS
        N_CH = HALF // CHUNK
        LAG_T, LAG_V = 2, 3

        def halves(hf):
            return slice(hf * HALF, (hf + 1) * HALF)

        block = ctx.enter_context(nc.Block())

        @block.sync
        def _(sp):
            def load_up(u, slot, src):
                if not isinstance(u, int) or u >= 2:
                    sp.wait_ge(up_lo_done, u - 1)
                sp.dma_start(up_raw[:, slot, :, :].rearrange("p k f -> p (k f)"),
                             up_w[bass.ds(src, 1), :, :].rearrange("a p n -> (a p) n"))\
                    .then_inc(up_in[slot], 16)

            def load_down(d, slot, src):
                if not isinstance(d, int) or d >= 2:
                    sp.wait_ge(dn_lo_done, d - 1)
                sp.dma_start(dn_raw[:, slot, :],
                             down_w[bass.ds(src, 1), :, :].rearrange("a p n -> (a p) n"))\
                    .then_inc(dn_in[slot], 16)

            def load_cond(n, slot, v, k):
                if not isinstance(n, int) or n >= 4:
                    sp.wait_ge(crow_used, n - 3)
                sp.dma_start(crow[:, slot, :],
                             w_cond[bass.ds(v, 1), k, :, :].rearrange("a p n -> (a p) n"))\
                    .then_inc(crow_in[slot], 16)

            sp.dma_start(par[:, :], table).then_inc(tables_in, 16)
            sp.dma_start(mean_m[:, :], mean_w[0]).then_inc(tables_in, 16)
            sp.dma_start(eye[:, :], mean_w[1]).then_inc(tables_in, 16)
            for n in range(2 * KD):
                load_cond(n, n % 4, 1 - n // KD, n % KD)
                if n == KD:
                    sp.dma_start(res[:, :, 0:HALF], x[:, :, 0:HALF]).then_inc(x_in[0], 16)
            load_up(0, 0, 0)
            sp.dma_start(res[:, :, HALF:SEQ], x[:, :, HALF:SEQ]).then_inc(x_in[1], 16)
            load_up(1, 1, 1)
            sp.dma_start(pos_i[:, :], pos.to_broadcast([P, SEQ])).then_inc(pos_in, 16)

            def ffn_step(c, ub, sb, db, dsb, down, cond):
                if not (isinstance(c, int) and c == 0 and ub == 0):
                    load_up(c * 4 + ub, 0, c * 4 + sb)
                    load_up(c * 4 + (ub + 1), 1, c * 4 + (sb + 1))
                if down:
                    load_down(c * 2 + (db - 2), 0, c * 2 + (dsb - 2))
                    load_down(c * 2 + (db - 1), 1, c * 2 + (dsb - 1))
                if cond:
                    for k in range(KD):
                        load_cond(c * KD + (KD + k), k % 4, c + 1, k)
                load_up(c * 4 + (ub + 2), 0, c * 4 + (sb + 2))
                load_up(c * 4 + (ub + 3), 1, c * 4 + (sb + 3))

            ffn_step(0, 0, 0, 0, 0, False, False)
            ffn_step(1, 0, 0, 0, 0, True, True)
            with sp.Fori(2, N_COND - 1) as c:
                ffn_step(c, 0, 0, 0, 0, True, True)
            with sp.Fori(N_COND - 1, FF_STEPS) as c:
                ffn_step(c, 0, 0, 0, 0, True, False)
            load_down(FF_TILES - 2, 0, FF_TILES - 2)
            load_down(FF_TILES - 1, 1, FF_TILES - 1)
            for hf in range(2):
                ub, db = UPB_MIX[hf], DNB_MIX[hf]
                with sp.Fori(0, PROJ // 2) as i:
                    for s in range(2):
                        load_up(i * 2 + (ub + s), s, i * 2 + (UP_FFN + s))

                def merge_step(i, down):
                    for s in range(2):
                        load_up(i * 6 + (ub + PROJ + s), s, i * 6 + (UP_FFN + PROJ + s))
                    if down:
                        for s in range(2):
                            load_down(i * 2 + (db - 2 + s), s, i * 2 + (FF_TILES - 2 + s))
                    for s in range(2, 6):
                        load_up(i * 6 + (ub + PROJ + s), s % 2, i * 6 + (UP_FFN + PROJ + s))

                merge_step(0, False)
                with sp.Fori(1, MIX_STEPS) as i:
                    merge_step(i, True)
                load_down(db + KD - 2, 0, FF_TILES + KD - 2)
                load_down(db + KD - 1, 1, FF_TILES + KD - 1)
            ub, sb, db, dsb = UPB_FFN2, UP_FFN + UP_MIX, DNB_FFN2, FF_TILES + KD
            ffn_step(0, ub, sb, db, dsb, False, False)
            with sp.Fori(1, FF_STEPS) as c:
                ffn_step(c, ub, sb, db, dsb, True, False)
            load_down(db + FF_TILES - 2, 0, dsb + FF_TILES - 2)
            load_down(db + FF_TILES - 1, 1, dsb + FF_TILES - 1)
            for hf in range(2):
                for k in range(KD):
                    sp.wait_ge(y_ready, hf * KD + k + 1)
                    sp.dma_start(out[:, k, halves(hf)], res[:, k, halves(hf)]).then_inc(stored, 16)
            sp.wait_ge(stored, 16 * 2 * KD)

        @block.gpsimd
        def _(pool):
            with pool.Fori(0, UP_TOTAL // 2) as i:
                for s in range(2):
                    pool.wait_ge(up_hi_done, i * 2 + (s + 1))
                    pool.tensor_tensor(up_lo[:, s, :, :], up_raw[:, s, :, :],
                                       up_hi[:, s, :, :].bitcast(F32), ALU.subtract)\
                        .then_inc(up_lo_done, 1)

        @block.scalar
        def _(act):
            def split_up(u, slot, turn_of):
                act.wait_ge(up_in[slot], turn_of * 16 + 16)
                if not isinstance(u, int) or u >= 2:
                    act.wait_ge(up_mm, u - 1)
                act.activation(up_hi[:, slot, :, :], up_raw[:, slot, :, :], ACT.Copy)\
                    .then_inc(up_hi_done, 1)

            def split_down(chunk):
                for s in range(2):
                    act.wait_ge(dn_in[s], chunk * 16 + 16)
                    if not isinstance(chunk, int) or chunk >= 1:
                        act.wait_ge(dn_mm, chunk * KD)
                    act.activation(dn_hi[:, s, :], dn_raw[:, s, :], ACT.Copy)\
                        .then_inc(dn_hi_done, 1)

            def modulate(i, scale, bias, ready, ready_at):
                hf = i % 2
                for k in range(KD):
                    n = i * KD + k
                    act.wait_ge(ready, ready_at(k))
                    if n >= 4:
                        act.wait_ge(h_ready, n - 3)
                    act.activation(tmp[:, n % 4, :], res[:, k, halves(hf)], ACT.Identity,
                                   bias=bias[:, k:k + 1], scale=scale[:, k:k + 1])\
                        .then_inc(hf_done, 1)
                    act.wait_ge(hf_done, n + 1)
                    act.activation(h_hi[:, k, halves(hf)], tmp[:, n % 4, :], ACT.Copy)\
                        .then_inc(hhi_done, 1)

            def squares(i):
                for k in range(KD):
                    n = i * KD + k
                    act.wait_ge(ln_centred, n + 1)
                    if k >= 4:
                        act.wait_ge(ln_sqmm, n - 3)
                    act.activation(tmp[:, k % 4, :], res[:, k, halves(i % 2)], ACT.Square)\
                        .then_inc(ln_sq, 1)
                act.wait_ge(ln_rcp, i + 1)
                act.activation(rstd[:, :], presum[:, :], ACT.Sqrt).then_inc(ln_rstd, 1)

            def gate_tile(t, s, chunk, down, src_done, dst):
                act.wait_ge(prod_done, t + 1)
                if down and s == 0:
                    act.wait_ge(dn_mm, chunk * KD)
                act.activation(dst, src_done, ACT.Copy).then_inc(g_hi_done, 1)

            def ffn_step(c, ub, tb, cb, down, last=False):
                for s in range(2):
                    t = c * 2 + (tb + s)
                    if s == 0 or not last:
                        split_up(c * 4 + (ub + 2 + 2 * s), 0, c * 2 + (ub // 2 + 1 + s))
                    if not isinstance(t, int) or t >= 1:
                        act.wait_ge(prod_done, t)
                    act.wait_ge(up_mm, c * 4 + (ub + 1 + 2 * s))
                    act.activation(tmp[:, 0:2, :], ps[:, 0:2, :], ACT.Silu).then_inc(gate_read, 1)
                    if s == 0:
                        split_up(c * 4 + (ub + 3), 1, c * 2 + (ub // 2 + 1))
                    gate_tile(t, s, c + cb, down, tmp[:, 2:4, :],
                              g_hi[:, s, :].rearrange("p (a t) -> p a t", a=2))
                if not last:
                    split_up(c * 4 + (ub + 5), 1, c * 2 + (ub // 2 + 2))

            act.wait_ge(tables_in, 48)
            act.activation(cs[:, :], par[:, PC_C:PC_C + KD], ACT.Silu).then_inc(cs_ready, 1)
            split_up(0, 0, 0)
            split_up(1, 1, 0)
            act.wait_ge(coef_done, 1)
            for hf in range(2):
                act.wait_ge(x_in[hf], 16)
                modulate(hf, coef[:, C_SC0, :], mod[:, 0, :], coef_done, lambda k: 1)
            act.wait_ge(h_ready, 2 * KD)

            act.wait_ge(rope_steps, 9)
            act.activation(cos_t[:, :], turn[:, :], ACT.Sin).then_inc(trig_done, 1)
            act.wait_ge(rope_steps, 15)
            act.activation(sin_t[:, :], ang[:, :], ACT.Sin).then_inc(trig_done, 1)
            ffn_step(0, 0, 0, 0, False)
            split_down(0)
            with act.Fori(1, FF_STEPS) as c:
                ffn_step(c, 0, 0, 0, True)
                split_down(c)

            for hf in range(2):
                squares(hf)
                modulate(2 + hf, coef[:, C_H1S, :], coef[:, C_H1B, :], ln_y,
                         lambda k: hf * KD + k + 1)
            act.wait_ge(h_ready, 4 * KD)

            for hf in range(2):
                ub = UPB_MIX[hf]
                for p in range(PROJ):
                    u = ub + p
                    if p > 0:
                        split_up(u + 1, (u + 1) % 2, (u + 1) // 2)
                    m = p - 6
                    if 0 <= m - LAG_V < N_CH:
                        v = m - LAG_V
                        act.wait_ge(av_mm, hf * N_CH + v + 1)
                        act.activation(
                            attn_hi[:, :, v * CHUNK:(v + 1) * CHUNK],
                            ps[:, 7, 0:Q_TILES * CHUNK].rearrange("p (j t) -> p j t", j=Q_TILES),
                            ACT.Copy).then_inc(attn_hi_done, 1)
                    if 0 <= m - LAG_T < N_CH:
                        a = hf * N_CH + m - LAG_T
                        act.wait_ge(probT_mm, a + 1)
                        if a >= 2:
                            act.wait_ge(av_mm, a - 1)
                        act.activation(probT[:, a % 2, :, :],
                                       ps[:, 6, :].rearrange("p (j t) -> p j t", j=Q_TILES),
                                       ACT.Copy).then_inc(probT_ready, 1)
                    if 0 <= m < N_CH:
                        a = hf * N_CH + m
                        if a >= 2:
                            act.wait_ge(probT_mm, a - 1)
                        act.wait_ge(negmax_done, a + 1)
                        for j in range(Q_TILES):
                            act.activation(prob[:, a % 2, j, :], ps[:, 4 + a % 2, j * P:(j + 1) * P],
                                           ACT.Exp, bias=small[:, a % 2, 1, j:j + 1], scale=SCALE,
                                           accum_out=small[:, a % 2, 3, j:j + 1])
                        act.activation(small[:, a % 2, 4, :], small[:, a % 2, 2, :], ACT.Exp)\
                            .then_inc(exp_done, 1)
                    if m >= 3 and m % 3 == 0:
                        i = m // 3 - 1
                        act.wait_ge(conv_done, hf * CONV_TILES + i + 1)
                        act.activation(conv_hi[:, i, :], tmp[:, 2, :], ACT.Copy)\
                            .then_inc(conv_hi_done, 1)
                act.wait_ge(conv_done, (hf + 1) * CONV_TILES)
                act.activation(conv_hi[:, CONV_TILES - 1, :], tmp[:, 2, :], ACT.Copy)\
                    .then_inc(conv_hi_done, 1)
                act.wait_ge(conv_ready, (hf + 1) * CONV_TILES)

                mb, tb, cb = ub + PROJ, TL_MIX[hf], CH_MIX[hf]

                def merge_step(i, down, mb=mb, tb=tb, cb=cb):
                    def split(n):
                        split_up(i * 6 + (mb + n), n % 2, i * 3 + (mb + n) // 2)

                    for s in range(2):
                        t = i * 2 + (tb + s)
                        if s == 0:
                            split(1)
                        act.wait_ge(prod_done, t)
                        for b in range(2):
                            act.wait_ge(up_mm, i * 6 + (mb + 3 * s + b + 1))
                            act.activation(tmp[:, b, :], ps[:, b, :], ACT.Sigmoid)\
                                .then_inc(gate_read, 1)
                            split(2 + b if s == 0 else 5 + b)
                        if s == 0:
                            split(4)
                        gate_tile(t, s, i + cb, down, tmp[:, 2, :], mg_hi[:, s, :])

                merge_step(0, False)
                split_down(cb)
                with act.Fori(1, MIX_STEPS) as i:
                    merge_step(i, True)
                    split_down(i + cb)
                split_up(ub + UP_MIX + 1, 1, (ub + UP_MIX + 1) // 2)

            for hf in range(2):
                squares(2 + hf)
                modulate(4 + hf, coef[:, C_H2S, :], coef[:, C_H2B, :], ln_y,
                         lambda k: (2 + hf) * KD + k + 1)
            act.wait_ge(h_ready, 6 * KD)

            ffn_step(0, UPB_FFN2, TL_FFN2, CH_FFN2, False)
            split_down(CH_FFN2)
            with act.Fori(1, FF_STEPS - 1) as c:
                ffn_step(c, UPB_FFN2, TL_FFN2, CH_FFN2, True)
                split_down(c + CH_FFN2)
            ffn_step(FF_STEPS - 1, UPB_FFN2, TL_FFN2, CH_FFN2, True, last=True)
            split_down(CH_FFN2 + FF_STEPS - 1)
            for hf in range(2):
                squares(4 + hf)

        @block.vector
        def _(dve):
            def split_down(chunk):
                for s in range(2):
                    dve.wait_ge(dn_hi_done, chunk * 2 + (s + 1))
                    dve.tensor_tensor(dn_lo[:, s, :], dn_raw[:, s, :], dn_hi[:, s, :].bitcast(F32),
                                      ALU.subtract).then_inc(dn_lo_done, 1)

            def cond_rows(n, slot, turn_of, k, vectors):
                dve.wait_ge(crow_in[slot], turn_of * 16 + 16)
                if k == 0:
                    if not isinstance(vectors, int) or vectors >= 1:
                        dve.wait_ge(mod_sum, vectors)
                    dve.tensor_scalar(cacc[:, :], crow[:, slot, :], cs[:, 0:1], None, ALU.mult)\
                        .then_inc(crow_used, 1)
                else:
                    dve.wait_ge(crow_used, n)
                    dve.scalar_tensor_tensor(out=cacc[:, :], in0=crow[:, slot, :],
                                             scalar=cs[:, k:k + 1], in1=cacc[:, :], op0=ALU.mult,
                                             op1=ALU.add).then_inc(crow_used, 1)

            def cond_vector(v, vectors):
                dve.wait_ge(mod_sum, vectors + 1)
                dve.tensor_tensor(mod[:, bass.ds(v, 1), :].rearrange("p a k -> p (a k)"),
                                  ps[:, 6, 0:KD], par[:, bass.ds(v * KD + PC_BCOND, KD)], ALU.add)\
                    .then_inc(mod_ready, 1)

            def split_h(i, r_scale, r_bias):
                hf = i % 2
                for k in range(KD):
                    n = i * KD + k
                    dve.wait_ge(hhi_done, n + 1)
                    dve.tensor_tensor(h_lo[:, k, halves(hf)], tmp[:, n % 4, :],
                                      h_hi[:, k, halves(hf)].bitcast(F32), ALU.subtract)\
                        .then_inc(h_ready, 1)
                    r = res[:, k, halves(hf)]
                    if r_bias is None:
                        dve.tensor_scalar(r, r, r_scale, None, ALU.mult).then_inc(r_scaled, 1)
                    else:
                        dve.tensor_scalar(r, r, r_scale[:, k:k + 1], r_bias[:, k:k + 1], ALU.mult,
                                          ALU.add).then_inc(r_scaled, 1)

            def layer_norm(i, accs):
                r = res[:, :, halves(i % 2)]
                mean_b, var_b = 4 + 2 * (i % 2), 5 + 2 * (i % 2)
                dve.wait_ge(dn_acc, accs)
                dve.tensor_reduce(presum[:, :], r.rearrange("p k t -> p t k"), AX.X, ALU.add)\
                    .then_inc(ln_sum, 1)
                dve.wait_ge(ln_mean, i + 1)
                for k in range(KD):
                    dve.tensor_tensor(r[:, k, :], r[:, k, :], ps[:, mean_b, :], ALU.subtract)\
                        .then_inc(ln_centred, 1)
                dve.wait_ge(ln_sqmm, (i + 1) * KD)
                dve.tensor_scalar(presum[:, :], ps[:, var_b, :], LN_EPS, None, ALU.add)\
                    .then_inc(ln_var, 1)
                dve.wait_ge(ln_var, i + 1)
                dve.reciprocal(presum[:, :], presum[:, :]).then_inc(ln_rcp, 1)
                dve.wait_ge(ln_rstd, i + 1)
                for k in range(KD):
                    dve.tensor_tensor(r[:, k, :], r[:, k, :], rstd[:, :], ALU.mult)\
                        .then_inc(ln_y, 1)

            def ffn_step(c, tb, gb, ub, cb, gate, down, cond=False):
                if down:
                    split_down(c + (cb - 1))
                if cond:
                    for k in range(KD):
                        cond_rows(c * KD + (KD + k), k % 4, c * 2 + (2 + k // 4), k, c + 1)
                    cond_vector(c + 1, c + 1)
                    dve.wait_ge(mod_ready, c + 2)
                    dve.tensor_scalar(coef[:, C_G1, :], mod[:, 2, :], FFN_RES, None, ALU.mult)\
                        .then_inc(coef_done, 1)
                    dve.wait_ge(coef_done, c + 1)
                for s in range(2):
                    t = c * 2 + (tb + s)
                    dve.wait_ge(gate_read, c * 2 + (gb + s + 1))
                    dve.wait_ge(up_mm, c * 4 + (ub + 2 + 2 * s))
                    if not isinstance(t, int) or t >= 1:
                        dve.wait_ge(g_ready, t)
                    dve.tensor_tensor(tmp[:, 2:4, :], tmp[:, 0:2, :], ps[:, 2:4, :], ALU.mult)\
                        .then_inc(prod_done, 1)
                    if down and s == 0:
                        for m in range(KD):
                            dve.wait_ge(dn_mm, (c + (cb - 1)) * KD + (m + 1))
                            r = res[:, m, :].rearrange("p (a t) -> p a t", a=2)
                            b = 4 + 2 * (m % 2)
                            dve.scalar_tensor_tensor(out=r, in0=ps[:, b:b + 2, :],
                                                     scalar=gate[:, m:m + 1], in1=r, op0=ALU.mult,
                                                     op1=ALU.add).then_inc(dn_acc, 1)
                    dve.wait_ge(g_hi_done, t + 1)
                    dve.tensor_tensor(g_lo[:, s, :].rearrange("p (a t) -> p a t", a=2),
                                      tmp[:, 2:4, :],
                                      g_hi[:, s, :].bitcast(F32).rearrange("p (a t) -> p a t", a=2),
                                      ALU.subtract).then_inc(g_ready, 1)

            def ffn_last(chunk, gate):
                for m in range(KD):
                    dve.wait_ge(dn_mm, chunk * KD + (m + 1))
                    r = res[:, m, :].rearrange("p (a t) -> p a t", a=2)
                    b = 4 + 2 * (m % 2)
                    dve.scalar_tensor_tensor(out=r, in0=ps[:, b:b + 2, :], scalar=gate[:, m:m + 1],
                                             in1=r, op0=ALU.mult, op1=ALU.add).then_inc(dn_acc, 1)

            dve.wait_ge(tables_in, 48)
            dve.tensor_scalar(negsink[:, :], par[:, PC_SINK:PC_SINK + Q_TILES], -1.0, None,
                              ALU.mult).then_inc(dve_step, 1)
            steps = 1
            dve.wait_ge(cs_ready, 1)
            for n in range(2 * KD):
                cond_rows(n, n % 4, n // 4, n % KD, n // KD)
                if n % KD == KD - 1:
                    cond_vector(1 - n // KD, n // KD)
            dve.wait_ge(mod_ready, 2)
            dve.tensor_scalar(coef[:, C_SC0, :], mod[:, 1, :], 1.0, None, ALU.add)\
                .then_inc(coef_done, 1)
            for i in range(2):
                split_h(i, ALPHA, None)

            dve.wait_ge(pos_in, 16)
            dve.tensor_copy(ang[:, :], pos_i[:, :]).then_inc(rope_steps, 1)
            dve.wait_ge(rope_steps, 1)
            dve.tensor_scalar(ang[:, :], ang[:, :], par[:, PC_INV:PC_INV + 1], None, ALU.mult)\
                .then_inc(rope_steps, 1)
            step = 2
            for quarter, dst in ((0.25, turn), (0.0, ang)):
                dve.wait_ge(rope_steps, step)
                dve.tensor_scalar(turns[:, :], ang[:, :], 1.0 / TWO_PI, quarter, ALU.mult, ALU.add)\
                    .then_inc(rope_steps, 1)
                dve.wait_ge(rope_steps, step + 1)
                dve.tensor_scalar(turns[:, :], turns[:, :], ROUND, -ROUND, ALU.add, ALU.add)\
                    .then_inc(rope_steps, 1)
                src = ang
                for n, part in enumerate((CW1, CW2, CW3)):
                    dve.wait_ge(rope_steps, step + 2 + n)
                    dve.scalar_tensor_tensor(out=dst[:, :], in0=turns[:, :], scalar=-part,
                                             in1=src[:, :], op0=ALU.mult, op1=ALU.add)\
                        .then_inc(rope_steps, 1)
                    src = dst
                step += 5
                if quarter:
                    dve.wait_ge(rope_steps, step)
                    dve.tensor_scalar(dst[:, :], dst[:, :], quarter * TWO_PI, None, ALU.add)\
                        .then_inc(rope_steps, 1)
                    step += 1
                dve.wait_ge(rope_steps, step)
                dve.tensor_scalar(dst[:, :], dst[:, :], PI_BELOW, -PI_BELOW, ALU.min, ALU.max)\
                    .then_inc(rope_steps, 1)
                step += 1
            dve.wait_ge(trig_done, 2)
            dve.tensor_scalar(sin_t[:, :], sin_t[:, :], par[:, PC_SIGN:PC_SIGN + 1], None, ALU.mult)\
                .then_inc(sin_ready, 1)

            dve.wait_ge(r_scaled, 2 * KD)
            ffn_step(0, 0, 0, 0, 0, coef[:, C_G1, :], False)
            with dve.Fori(1, N_COND - 1) as c:
                ffn_step(c, 0, 0, 0, 0, coef[:, C_G1, :], True, cond=True)
            with dve.Fori(N_COND - 1, FF_STEPS) as c:
                ffn_step(c, 0, 0, 0, 0, coef[:, C_G1, :], True)
            split_down(FF_STEPS - 1)
            ffn_last(FF_STEPS - 1, coef[:, C_G1, :])

            coefs = N_COND - 1
            rows = ((4, 3, 0, C_ONE2, C_H1S, C_H1B, C_R1S, C_R1B),
                    (7, 6, 2, C_ONE3, C_H2S, C_H2B, C_R2S, C_R2B))
            for sc, sh, ln, one, hs, hb, rs, rb in rows:
                g = par[:, PC_LN + ln * KD:PC_LN + (ln + 1) * KD]
                b = par[:, PC_LN + (ln + 1) * KD:PC_LN + (ln + 2) * KD]
                dve.tensor_scalar(coef[:, one, :], mod[:, sc, :], 1.0, None, ALU.add)\
                    .then_inc(coef_done, 1)
                dve.wait_ge(coef_done, coefs + 1)
                dve.tensor_tensor(coef[:, hs, :], coef[:, one, :], g, ALU.mult)\
                    .then_inc(coef_done, 1)
                dve.tensor_tensor(coef[:, hb, :], coef[:, one, :], b, ALU.mult)\
                    .then_inc(coef_done, 1)
                dve.tensor_scalar(coef[:, rs, :], g, ALPHA, None, ALU.mult).then_inc(coef_done, 1)
                dve.tensor_scalar(coef[:, rb, :], b, ALPHA, None, ALU.mult).then_inc(coef_done, 1)
                dve.wait_ge(coef_done, coefs + 3)
                dve.tensor_tensor(coef[:, hb, :], coef[:, hb, :], mod[:, sh, :], ALU.add)\
                    .then_inc(coef_done, 1)
                coefs += 6
            dve.tensor_scalar(coef[:, C_G3, :], mod[:, 8, :], FFN_RES, None, ALU.mult)\
                .then_inc(coef_done, 1)
            coefs += 1
            dve.memset(kT[:, 0:CHUNK], 0.0).then_inc(carried, 1)
            dve.memset(vT[:, 0:CHUNK], 0.0).then_inc(carried, 1)
            dve.memset(ucarry[:, :, :], 0.0).then_inc(carried, 1)
            dve.wait_ge(coef_done, coefs)
            carries = 3

            for hf in range(2):
                layer_norm(hf, FF_STEPS * KD)
                dve.wait_ge(ln_y, (hf + 1) * KD)
                split_h(2 + hf, coef[:, C_R1S, :], coef[:, C_R1B, :])
            dve.wait_ge(r_scaled, 4 * KD)
            dve.wait_ge(sin_ready, 1)

            for hf in range(2):
                ub = UPB_MIX[hf]
                toks = halves(hf)

                def rope(bank, dst, slot):
                    for a in range(4):
                        b = a ^ 1
                        dve.tensor_tensor(tmp[32 * a:32 * a + 32, slot, :],
                                          ps[32 * b:32 * b + 32, bank, :],
                                          sin_t[32 * b:32 * b + 32, toks], ALU.mult)\
                            .then_inc(dve_step, 1)
                    dve.tensor_tensor(dst, ps[:, bank, :], cos_t[:, toks], ALU.mult)\
                        .then_inc(proj_read, 1)

                def add_rope(dst, slot, n, reads):
                    dve.wait_ge(dve_step, n)
                    dve.wait_ge(proj_read, reads)
                    dve.tensor_tensor(dst, dst, tmp[:, slot, :], ALU.add).then_inc(qkv_ready, 1)

                for p in range(PROJ):
                    u, bank, m = ub + p, p % 4, p - 6
                    reads = hf * PROJ + p
                    if p == 0 and hf == 1:
                        dve.wait_ge(up_mm, u + 1)
                        dve.tensor_copy(kT[:, 0:CHUNK], kT[:, HALF:HALF + CHUNK])\
                            .then_inc(carried, 1)
                        dve.tensor_copy(vT[:, 0:CHUNK], vT[:, HALF:HALF + CHUNK])\
                            .then_inc(carried, 1)
                        carries += 2
                    if p == 3:
                        dve.wait_ge(vband_mm, hf + 1)
                        dve.tensor_copy(vband[:, :, :],
                                        ps[:, 6:8, :].rearrange("p b (c t) -> p (b c) t", t=P))\
                            .then_inc(vband_ready, 1)
                    if 0 <= m - LAG_V < N_CH:
                        v = m - LAG_V
                        dve.wait_ge(attn_hi_done, hf * N_CH + v + 1)
                        dst = slice(v * CHUNK, (v + 1) * CHUNK)
                        dve.tensor_tensor(
                            attn_lo[:, :, dst],
                            ps[:, 7, 0:Q_TILES * CHUNK].rearrange("p (j t) -> p j t", j=Q_TILES),
                            attn_hi[:, :, dst].bitcast(F32), ALU.subtract).then_inc(attn_ready, 1)
                    if 0 <= m < N_CH:
                        a = hf * N_CH + m
                        sm = small[:, a % 2, :, :]
                        score = ps[:, 4 + a % 2, :].rearrange("p (j t) -> p j t", j=Q_TILES)
                        dve.wait_ge(score_mm, a + 1)
                        if a == 0:
                            dve.memset(score[:, :, 0:CHUNK], MASKED).then_inc(dve_step, 1)
                            steps += 1
                            dve.wait_ge(dve_step, steps)
                        dve.tensor_reduce(sm[:, 0, :], score, AX.X, ALU.max).then_inc(dve_step, 1)
                        steps += 1
                        dve.wait_ge(dve_step, steps)
                        dve.scalar_tensor_tensor(out=sm[:, 1, :], in0=sm[:, 0, :], scalar=-SCALE,
                                                 in1=negsink[:, :], op0=ALU.mult, op1=ALU.min)\
                            .then_inc(dve_step, 1)
                        steps += 1
                        dve.wait_ge(dve_step, steps)
                        dve.tensor_tensor(sm[:, 2, :], sm[:, 1, :], negsink[:, :], ALU.subtract)\
                            .then_inc(negmax_done, 1)
                        dve.wait_ge(exp_done, a + 1)
                        dve.tensor_tensor(sm[:, 5, :], sm[:, 3, :], sm[:, 4, :], ALU.add)\
                            .then_inc(dve_step, 1)
                        steps += 1
                        dve.wait_ge(dve_step, steps)
                        dve.reciprocal(sm[:, 5, :], sm[:, 5, :]).then_inc(dve_step, 1)
                        steps += 1
                        dve.wait_ge(dve_step, steps)
                        dve.tensor_tensor(
                            prob[:, a % 2, :, :], prob[:, a % 2, :, :],
                            sm[:, 5, :].rearrange("p (j o) -> p j o", o=1)
                            .to_broadcast([P, Q_TILES, P]), ALU.mult).then_inc(probs_ready, 1)
                    if m >= 3 and m % 3 == 0:
                        i = m // 3 - 1
                        dve.wait_ge(conv_hi_done, hf * CONV_TILES + i + 1)
                        dve.tensor_tensor(conv_lo[:, i, :], tmp[:, 2, :],
                                          conv_hi[:, i, :].bitcast(F32), ALU.subtract)\
                            .then_inc(conv_ready, 1)
                    dve.wait_ge(up_mm, u + 1)
                    if p == 0:
                        dve.wait_ge(carried, carries)
                        rope(bank, kT[:, CHUNK:CHUNK + HALF], p % 2)
                        steps += 4
                        add_rope(kT[:, CHUNK:CHUNK + HALF], p % 2, steps, reads + 1)
                    elif p == 1:
                        dve.tensor_copy(vT[:, CHUNK:CHUNK + HALF], ps[:, bank, :])\
                            .then_inc(proj_read, 1)
                    elif m < 0:
                        dve.wait_ge(qkv_ready, hf * (1 + Q_TILES) + p - 1)
                        rope(bank, qT[:, p - 2, :], p % 2)
                        steps += 4
                        add_rope(qT[:, p - 2, :], p % 2, steps, reads + 1)
                    elif m % 3 == 0:
                        dve.tensor_copy(tmp[:, 0, :], ps[:, bank, :]).then_inc(proj_read, 1)
                    elif m % 3 == 1:
                        i = m // 3
                        dve.wait_ge(proj_read, reads)
                        dve.tensor_copy(ubuf[:, 0:CONV_K - 1], ucarry[:, i, :])\
                            .then_inc(dve_step, 1)
                        dve.tensor_tensor(ubuf[:, CONV_K - 1:], ps[:, bank, :], tmp[:, 0, :],
                                          ALU.mult).then_inc(proj_read, 1)
                        dve.wait_ge(proj_read, reads + 1)
                        dve.tensor_copy(ucarry[:, i, :], ubuf[:, HALF:HALF + CONV_K - 1])\
                            .then_inc(dve_step, 1)
                        steps += 2
                        dve.wait_ge(dve_step, steps)
                        for j in range(CONV_K):
                            tap = CONV_K - 1 - j
                            w = par[:, PC_CONV + tap * CONV_TILES + i:
                                    PC_CONV + tap * CONV_TILES + i + 1]
                            if j == 0:
                                dve.tensor_scalar(tmp[:, 1, :], ubuf[:, tap:tap + HALF], w, None,
                                                  ALU.mult).then_inc(dve_step, 1)
                            else:
                                dve.wait_ge(dve_step, steps)
                                dve.scalar_tensor_tensor(out=tmp[:, 1, :],
                                                         in0=ubuf[:, tap:tap + HALF], scalar=w,
                                                         in1=tmp[:, 1, :], op0=ALU.mult,
                                                         op1=ALU.add).then_inc(dve_step, 1)
                            steps += 1
                    else:
                        dve.wait_ge(dve_step, steps)
                        i = m // 3
                        if i >= 1:
                            dve.wait_ge(conv_ready, hf * CONV_TILES + i)
                        dve.tensor_tensor(tmp[:, 2, :], ps[:, bank, :], tmp[:, 1, :], ALU.mult)\
                            .then_inc(proj_read, 1)
                        dve.wait_ge(proj_read, reads + 1)
                        dve.sem_inc(conv_done, 1)
                dve.wait_ge(conv_hi_done, (hf + 1) * CONV_TILES)
                dve.tensor_tensor(conv_lo[:, CONV_TILES - 1, :], tmp[:, 2, :],
                                  conv_hi[:, CONV_TILES - 1, :].bitcast(F32), ALU.subtract)\
                    .then_inc(conv_ready, 1)

                mb, tb, gb, cb = ub + PROJ, TL_MIX[hf], GR_MIX[hf], CH_MIX[hf]

                def add_down(chunk):
                    for m in range(KD):
                        dve.wait_ge(dn_mm, chunk * KD + (m + 1))
                        dve.scalar_tensor_tensor(out=res[:, m, toks], in0=ps[:, 4 + m % 4, :],
                                                 scalar=mod[:, 5, m:m + 1], in1=res[:, m, toks],
                                                 op0=ALU.mult, op1=ALU.add).then_inc(dn_acc, 1)

                def merge_step(i, down):
                    if down:
                        split_down(i + (cb - 1))
                    for s in range(2):
                        t = i * 2 + (tb + s)
                        dve.wait_ge(gate_read, i * 4 + (gb + 2 * s + 2))
                        dve.wait_ge(up_mm, i * 6 + (mb + 3 * s + 3))
                        dve.wait_ge(g_ready, t)
                        for b in range(2):
                            dve.tensor_tensor(tmp[:, 2 + b, :], tmp[:, b, :], ps[:, 2 + b, :],
                                              ALU.mult).then_inc(merge_parts, 1)
                        dve.wait_ge(merge_parts, (i * 2 + (tb + s - FF_TILES)) * 2 + 2)
                        dve.tensor_tensor(tmp[:, 2, :], tmp[:, 2, :], tmp[:, 3, :], ALU.add)\
                            .then_inc(prod_done, 1)
                        if s == 0 and down:
                            add_down(i + (cb - 1))
                        dve.wait_ge(g_hi_done, t + 1)
                        dve.tensor_tensor(mg_lo[:, s, :], tmp[:, 2, :], mg_hi[:, s, :].bitcast(F32),
                                          ALU.subtract).then_inc(g_ready, 1)

                merge_step(0, False)
                with dve.Fori(1, MIX_STEPS) as i:
                    merge_step(i, True)
                split_down(cb + MIX_STEPS - 1)
                add_down(cb + MIX_STEPS - 1)

            for hf in range(2):
                layer_norm(2 + hf, CH_FFN2 * KD)
                dve.wait_ge(ln_y, (3 + hf) * KD)
                split_h(4 + hf, coef[:, C_R2S, :], coef[:, C_R2B, :])
            dve.wait_ge(r_scaled, 6 * KD)

            gate = coef[:, C_G3, :]
            ffn_step(0, TL_FFN2, GR_FFN2, UPB_FFN2, CH_FFN2, gate, False)
            with dve.Fori(1, FF_STEPS) as c:
                ffn_step(c, TL_FFN2, GR_FFN2, UPB_FFN2, CH_FFN2, gate, True)
            split_down(CH_FFN2 + FF_STEPS - 1)
            ffn_last(CH_FFN2 + FF_STEPS - 1, gate)
            for hf in range(2):
                layer_norm(4 + hf, (CH_FFN2 + FF_STEPS) * KD)
                for k in range(KD):
                    dve.wait_ge(ln_y, (4 + hf) * KD + k + 1)
                    r = res[:, k, halves(hf)]
                    g, b = PC_LN + 4 * KD + k, PC_LN + 5 * KD + k
                    dve.tensor_scalar(r, r, par[:, g:g + 1], par[:, b:b + 1], ALU.mult, ALU.add)\
                        .then_inc(y_ready, 1)

        @block.tensor
        def _(pe):
            def passes(w_hi, w_lo, v_hi, v_lo):
                return ((w_hi, v_hi), (w_hi, v_lo), (w_lo, v_hi))

            def up_granule(u, slot, half_list, out_of, ks=range(KD), v_hi=h_hi, v_lo=h_lo,
                           last=True, tokens=None, ready=None, ready_at=None, k_of=None):
                for hf in half_list:
                    toks = halves(hf) if tokens is None else tokens
                    for k in ks:
                        if ready is not None:
                            pe.wait_ge(ready, ready_at(hf, k))
                        kv = k if k_of is None else k_of(k)
                        for n, (w, v) in enumerate(passes(up_hi, up_lo, v_hi, v_lo)):
                            mm = pe.matmul(out_of(hf), w[:, slot, k, :], v[:, kv, toks],
                                           start=(k == ks[0] and n == 0),
                                           stop=(k == ks[-1] and n == 2))
                if last:
                    mm.then_inc(up_mm, 1)

            def down_tile(m, half_list, out_of, v_hi, v_lo, toks_of):
                for hf in half_list:
                    for s in range(2):
                        for n, (w, v) in enumerate(passes(dn_hi, dn_lo, v_hi, v_lo)):
                            mm = pe.matmul(out_of(hf), w[:, s, m * P:(m + 1) * P],
                                           v[:, s, toks_of(hf)], start=(s == 0 and n == 0),
                                           stop=(s == 1 and n == 2))
                mm.then_inc(dn_mm, 1)

            def ffn_down(chunk):
                pe.wait_ge(dn_lo_done, chunk * 2 + 2)
                pe.wait_ge(g_ready, chunk * 2 + 2)
                for m in range(KD):
                    if not isinstance(chunk, int) or chunk > 0 or m >= 2:
                        pe.wait_ge(dn_acc, chunk * KD + (m - 1))
                    down_tile(m, range(2), lambda hf: ps[:, 4 + 2 * (m % 2) + hf, :], g_hi, g_lo,
                              halves)

            def cond_sum(vectors):
                pe.wait_ge(crow_used, vectors * KD + KD)
                for j in range(KD):
                    mm = pe.matmul(ps[:, 6, j:j + 1], cacc[:, j * P:(j + 1) * P],
                                   par[:, PC_ONE:PC_ONE + 1], start=True, stop=True)
                mm.then_inc(mod_sum, 1)

            def ffn_step(c, ub, tb, gb, cb, down, cond=False, h_from=None):
                for s in range(2):
                    t = c * 2 + (tb + s)
                    first = h_from is not None and s == 0
                    pe.wait_ge(up_lo_done, c * 4 + (ub + 2 * s + 1))
                    if not (isinstance(c, int) and c == 0 and s == 0):
                        pe.wait_ge(gate_read, c * 2 + (gb + s))
                    up_granule(None, 0, range(2), lambda hf: ps[:, hf, :],
                               ready=h_ready if first else None,
                               ready_at=(lambda hf, k: h_from + hf * KD + k + 1) if first else None)
                    pe.wait_ge(up_lo_done, c * 4 + (ub + 2 * s + 2))
                    if not isinstance(t, int) or t >= 1:
                        pe.wait_ge(prod_done, t)
                    up_granule(None, 1, range(2), lambda hf: ps[:, 2 + hf, :])
                    if s == 0 and cond:
                        if not isinstance(c, int) or c > 1:
                            pe.wait_ge(dn_acc, (c - 1) * KD)
                        cond_sum(c + 1)
                        pe.wait_ge(mod_ready, c + 2)
                    if s == 0 and down:
                        ffn_down(c + (cb - 1))

            def statistics(i):
                mean_b, var_b = 4 + 2 * (i % 2), 5 + 2 * (i % 2)
                pe.wait_ge(ln_sum, i + 1)
                pe.matmul(ps[:, mean_b, :], mean_m[:, :], presum[:, :], start=True, stop=True)\
                    .then_inc(ln_mean, 1)
                for k in range(KD):
                    pe.wait_ge(ln_sq, i * KD + k + 1)
                    pe.matmul(ps[:, var_b, :], mean_m[:, :], tmp[:, k % 4, :], start=(k == 0),
                              stop=(k == KD - 1)).then_inc(ln_sqmm, 1)

            pe.wait_ge(tables_in, 48)
            for vectors in range(2):
                if vectors:
                    pe.wait_ge(mod_ready, vectors)
                cond_sum(vectors)
            pe.wait_ge(mod_ready, 2)

            ffn_step(0, 0, 0, 0, 0, False, h_from=0)
            ffn_step(1, 0, 0, 0, 0, True, cond=True)
            with pe.Fori(2, N_COND - 1) as c:
                ffn_step(c, 0, 0, 0, 0, True, cond=True)
            with pe.Fori(N_COND - 1, FF_STEPS) as c:
                ffn_step(c, 0, 0, 0, 0, True)
            ffn_down(FF_STEPS - 1)
            for hf in range(2):
                statistics(hf)

            for hf in range(2):
                ub = UPB_MIX[hf]
                acc0 = CH_MIX[hf] * KD
                for p in range(PROJ):
                    u, m = ub + p, p - 6
                    if p == 3:
                        pe.wait_ge(proj_read, hf * PROJ + 2)
                        pe.wait_ge(dn_acc, acc0)
                        for n in range(N_CH):
                            mm = pe.transpose(ps[:, 6 + n // 4, (n % 4) * P:(n % 4 + 1) * P],
                                              vT[:, n * CHUNK:n * CHUNK + P], eye[:, :])
                        mm.then_inc(vband_mm, 1)
                    if 0 <= m - LAG_V < N_CH:
                        v = m - LAG_V
                        a = hf * N_CH + v
                        pe.wait_ge(probT_ready, a + 1)
                        pe.wait_ge(vband_ready, hf + 1)
                        if v >= 1:
                            pe.wait_ge(attn_ready, a)
                        for g in range(2):
                            rows = slice(g * HEAD_DIM, (g + 1) * HEAD_DIM)
                            mm = pe.matmul(ps[rows, 7, 0:Q_TILES * CHUNK], vband[:, v, rows],
                                           probT[:, a % 2, :, rows], start=True, stop=True)
                        mm.then_inc(av_mm, 1)
                    if 0 <= m - LAG_T < N_CH:
                        a = hf * N_CH + m - LAG_T
                        pe.wait_ge(probs_ready, a + 1)
                        pe.wait_ge(vband_ready, hf + 1)
                        if a >= 1:
                            pe.wait_ge(probT_ready, a)
                        for j in range(Q_TILES):
                            mm = pe.transpose(ps[:, 6, j * P:(j + 1) * P], prob[:, a % 2, j, :],
                                              eye[:, :])
                        mm.then_inc(probT_mm, 1)
                    if 0 <= m < N_CH:
                        a = hf * N_CH + m
                        pe.wait_ge(qkv_ready, (hf + 1) * (1 + Q_TILES))
                        if a >= 2:
                            pe.wait_ge(exp_done, a - 1)
                        for j in range(Q_TILES):
                            for g in range(2):
                                rows = slice(g * HEAD_DIM, (g + 1) * HEAD_DIM)
                                mm = pe.matmul(ps[rows, 4 + a % 2, j * P:(j + 1) * P],
                                               qT[rows, j, m * CHUNK:(m + 1) * CHUNK],
                                               kT[rows, m * CHUNK:m * CHUNK + P],
                                               start=True, stop=True)
                        mm.then_inc(score_mm, 1)
                    pe.wait_ge(up_lo_done, u + 1)
                    if p >= 4:
                        pe.wait_ge(proj_read, hf * PROJ + p - 3)
                    elif hf == 1:
                        pe.wait_ge(prod_done, TL_MIX[1])
                    first = hf == 0 and p == 0
                    up_granule(u, u % 2, [hf], lambda h: ps[:, p % 4, :],
                               ready=h_ready if p == 0 else None,
                               ready_at=lambda h, k: (2 + h) * KD + k + 1)

                mb, tb, gb, cb = ub + PROJ, TL_MIX[hf], GR_MIX[hf], CH_MIX[hf]
                pe.wait_ge(proj_read, (hf + 1) * PROJ)

                def merge_down(chunk):
                    pe.wait_ge(dn_lo_done, chunk * 2 + 2)
                    pe.wait_ge(g_ready, chunk * 2 + 2)
                    for m in range(KD):
                        pe.wait_ge(dn_acc, chunk * KD + (m - 3))
                        down_tile(m, [hf], lambda h: ps[:, 4 + m % 4, :], mg_hi, mg_lo,
                                  lambda h: slice(0, HALF))

                def merge_step(i, down):
                    for s in range(2):
                        t = i * 2 + (tb + s)
                        for b in range(2):
                            slot = (3 * s + b) % 2
                            pe.wait_ge(up_lo_done, i * 6 + (mb + 3 * s + b + 1))
                            pe.wait_ge(gate_read, i * 4 + (gb + 2 * s + b - 1))
                            up_granule(None, slot, [hf], lambda h: ps[:, b, :])
                        slot = (3 * s + 2) % 2
                        pe.wait_ge(up_lo_done, i * 6 + (mb + 3 * s + 3))
                        pe.wait_ge(prod_done, t)
                        if isinstance(i, int):
                            pe.wait_ge(attn_ready, (hf + 1) * N_CH)
                            pe.wait_ge(conv_ready, (hf + 1) * CONV_TILES)
                        up_granule(None, slot, [hf], lambda h: ps[:, 2, :], ks=range(0, 4),
                                   v_hi=conv_hi, v_lo=conv_lo, last=False, tokens=slice(0, HALF))
                        up_granule(None, slot, [hf], lambda h: ps[:, 3, :], ks=range(4, 8),
                                   v_hi=attn_hi, v_lo=attn_lo, tokens=slice(0, HALF),
                                   k_of=lambda k: k - 4)
                        if s == 0 and down:
                            merge_down(i + (cb - 1))

                merge_step(0, False)
                with pe.Fori(1, MIX_STEPS) as i:
                    merge_step(i, True)
                merge_down(cb + MIX_STEPS - 1)
            for hf in range(2):
                statistics(2 + hf)

            ffn_step(0, UPB_FFN2, TL_FFN2, GR_FFN2, CH_FFN2, False, h_from=4 * KD)
            with pe.Fori(1, FF_STEPS) as c:
                ffn_step(c, UPB_FFN2, TL_FFN2, GR_FFN2, CH_FFN2, True)
            ffn_down(CH_FFN2 + FF_STEPS - 1)
            for hf in range(2):
                statistics(4 + hf)


def tiles_of(w):
    n = w.shape[1] // P
    return w.reshape(-1, P, n, P).transpose(2, 1, 0, 3).reshape(n, P, -1)


def interleaved(*lists):
    return np.stack(lists, axis=1).reshape(-1, *lists[0].shape[1:])


def kernel(**inputs):
    import concourse.bacc as bacc
    from concourse.bass_utils import run_bass_kernel_spmd

    a = {k: np.asarray(v) for k, v in inputs.items()}
    w = {k: a[k][0] for k in a if k not in ("x", "c", "positions")}
    f32 = np.float32

    def columns(v):
        return v.reshape(-1, P).T

    pair = np.concatenate([np.arange(h * HEAD_DIM, (h + 1) * HEAD_DIM)
                           for j in range(Q_TILES) for h in (j, j + Q_TILES)])
    q_w, kv_w, conv_w3, merge_w = np.split(
        w["w_in"], [Q_HEADS * HEAD_DIM, Q_HEADS * HEAD_DIM + 2 * P,
                    Q_HEADS * HEAD_DIM + 2 * P + 3 * CONV_WIDTH], axis=1)
    gate_b, gate_c, conv_x = np.split(conv_w3, 3, axis=1)
    merge_a, merge_c = np.split(merge_w, 2, axis=1)
    branches = np.concatenate([tiles_of(w["w_branch_conv"]),
                               tiles_of(w["w_branch_attn"][pair])], axis=2)
    up_w = np.concatenate([
        interleaved(tiles_of(w["ffn1_w1"]), tiles_of(w["ffn1_w3"])),
        tiles_of(kv_w), tiles_of(q_w[:, pair]),
        interleaved(tiles_of(gate_c), tiles_of(conv_x), tiles_of(gate_b)),
        interleaved(tiles_of(merge_c), tiles_of(merge_a), branches),
        interleaved(tiles_of(w["ffn2_w1"]), tiles_of(w["ffn2_w3"]))])
    down_w = np.concatenate([w["ffn1_w2"], w["w_out"], w["ffn2_w2"]]).reshape(-1, P, D)
    w_cond = w["w_cond"].reshape(KD, P, N_COND, D).transpose(2, 0, 1, 3)
    sinks = np.repeat(w["attn_sinks"].reshape(2, Q_TILES), HEAD_DIM, axis=0)
    half = HEAD_DIM // 2
    freq = f32(ROPE_THETA) ** (-np.arange(half, dtype=f32) / f32(half))
    sign = np.where(np.arange(P) % HEAD_DIM < half, 1.0, -1.0)
    table = np.concatenate(
        [columns(w["b_cond"]), columns(a["c"][0])]
        + [columns(w[n]) for n in ("ln1_g", "ln1_b", "ln2_g", "ln2_b", "ln3_g", "ln3_b")]
        + [columns(w["conv_w"]), sinks, np.tile(freq, P // half)[:, None].astype(f32),
           sign[:, None].astype(f32), np.ones((P, 1), f32)], axis=1)
    mean_w = np.stack([np.full((P, P), 1.0 / D, f32), np.eye(P, dtype=f32)])
    arrays = {
        "x_t": a["x"][0].T.reshape(KD, P, SEQ).transpose(1, 0, 2),
        "positions": a["positions"], "table": table, "mean_w": mean_w, "w_cond": w_cond,
        "up_w": up_w, "down_w": down_w,
    }
    arrays = {n: np.ascontiguousarray(v) for n, v in arrays.items()}
    nc = bacc.Bacc("TRN2", target_bir_lowering=False, num_devices=1, dynamic_dma_scratch_size=1024)
    args = [nc.dram_tensor(n, v.shape, mybir.dt.from_np(v.dtype), kind="ExternalInput").ap()
            for n, v in arrays.items()]
    out = nc.dram_tensor("out_t", (P, KD, SEQ), F32, kind="ExternalOutput").ap()
    encoder_block(nc, *args, out)
    got = run_bass_kernel_spmd(nc, [arrays], core_ids=[0]).results[0]["out_t"]
    return got.transpose(2, 1, 0).reshape(1, SEQ, D)
```

```python
from contextlib import ExitStack

import concourse.bass as bass
from concourse import mybir
import numpy as np

F32 = mybir.dt.float32
F32R = mybir.dt.float32r
I32 = mybir.dt.int32
ALU = mybir.AluOpType
ACT = mybir.ActivationFunctionType
AX = mybir.AxisListType

P = 128
D = 1024
SEQ = 1024
HALF = SEQ // 2
KD = D // P
D_FF = 2816
FF_TILES = D_FF // P
CHUNK = 64
HEAD_DIM = 64
Q_HEADS = 8
Q_TILES = Q_HEADS * HEAD_DIM // P
CONV_WIDTH = D // 2
CONV_TILES = CONV_WIDTH // P
CONV_K = 3
N_COND = 9
ALPHA = 2.0 ** 0.25
FFN_RES = 0.5
LN_EPS = 1e-5
SCALE = HEAD_DIM ** -0.5
MASKED = -3.0e38
ROPE_THETA = 10000.0

GRAN = KD * P
FF_STEPS = FF_TILES // 2
UP_FFN = 2 * FF_TILES
PROJ = 2 + Q_TILES + 3 * CONV_TILES
MERGE = 3 * KD
UP_MIX = PROJ + MERGE
UP_ALL = 2 * UP_FFN + UP_MIX
MIX_STEPS = KD // 2
DOWN_ALL = 2 * FF_TILES + KD
UP_TOTAL = 2 * UP_FFN + 2 * UP_MIX

PC_BCOND = 0
PC_C = PC_BCOND + N_COND * KD
PC_LN = PC_C + KD
PC_CONV = PC_LN + 6 * KD
PC_SINK = PC_CONV + CONV_K * CONV_TILES
PC_INV = PC_SINK + Q_TILES
PC_SIGN = PC_INV + 1
PC_ONE = PC_SIGN + 1
PC_ALL = PC_ONE + 1

TWO_PI = 2.0 * np.pi
CW1 = 6.28125
CW2 = float(np.floor((TWO_PI - CW1) * 2.0 ** 19) / 2.0 ** 19)
CW3 = float(np.float32(TWO_PI - CW1 - CW2))
ROUND = float(1.5 * 2.0 ** 23)
PI_BELOW = float(np.nextafter(np.float32(np.pi), np.float32(0)))


def encoder_block(nc, x, pos, table, mean_w, w_cond, up_w, down_w, out):
    with ExitStack() as ctx:
        def sem(name):
            return ctx.enter_context(nc.semaphore(name))

        at = [nc.sbuf_base + (-nc.sbuf_base) % 32]

        def place(name, shape, dt=F32, offset=None):
            size = 4 * int(np.prod(shape[1:]))
            if offset is None:
                offset = at[0]
                at[0] = offset + size + (-size) % 32
            return nc.alloc_sbuf_tensor_at(name, shape, dt, offset=offset), offset + size + (-size) % 32

        res, _ = place("res", [P, KD, SEQ])
        h_hi, _ = place("h_hi", [P, KD, SEQ], F32R)
        h_lo, _ = place("h_lo", [P, KD, SEQ], F32R)
        up_raw, _ = place("up_raw", [P, 2, KD, P])
        up_hi, _ = place("up_hi", [P, 2, KD, P], F32R)
        up_lo, _ = place("up_lo", [P, 2, KD, P], F32R)
        dn_raw, _ = place("dn_raw", [P, 2, D])
        dn_hi, _ = place("dn_hi", [P, 2, D], F32R)
        dn_lo, _ = place("dn_lo", [P, 2, D], F32R)
        tmp, _ = place("tmp", [P, 4, HALF])
        cos_t, _ = place("cos_t", [P, SEQ])
        sin_t, _ = place("sin_t", [P, SEQ])
        mean_m, _ = place("mean_m", [P, P])
        eye, _ = place("eye", [P, P])
        par, _ = place("par", [P, PC_ALL])
        mod, _ = place("mod", [P, N_COND, KD])
        coef, _ = place("coef", [P, 16, KD])
        cs, _ = place("cs", [P, KD])
        negsink, _ = place("negsink", [P, Q_TILES])
        small, _ = place("small", [P, 2, 6, Q_TILES])
        ucarry, _ = place("ucarry", [P, CONV_TILES, CONV_K - 1])
        shared = at[0]
        g_hi, o = place("g_hi", [P, 2, SEQ], F32R, shared)
        g_lo, o = place("g_lo", [P, 2, SEQ], F32R, o)
        crow, o = place("crow", [P, 4, D], F32, o)
        cacc, o = place("cacc", [P, D], F32, o)
        pos_i, o = place("pos_i", [P, SEQ], I32, o)
        ang, o = place("ang", [P, SEQ], F32, o)
        turn, o = place("turn", [P, SEQ], F32, o)
        turns, o = place("turns", [P, SEQ], F32, o)
        attn_hi, o = place("attn_hi", [P, Q_TILES, HALF], F32R, shared)
        attn_lo, o = place("attn_lo", [P, Q_TILES, HALF], F32R, o)
        conv_hi, o = place("conv_hi", [P, CONV_TILES, HALF], F32R, o)
        conv_lo, o = place("conv_lo", [P, CONV_TILES, HALF], F32R, o)
        q_at = o
        qT, o = place("qT", [P, Q_TILES, HALF], F32, q_at)
        mg_hi, o2 = place("mg_hi", [P, 2, HALF], F32R, q_at)
        mg_lo, _ = place("mg_lo", [P, 2, HALF], F32R, o2)
        kT, o = place("kT", [P, CHUNK + HALF], F32, o)
        vT, o = place("vT", [P, CHUNK + HALF], F32, o)
        ln_at = o
        vband, o = place("vband", [P, HALF // CHUNK, P], F32, o)
        ubuf, o = place("ubuf", [P, CONV_K - 1 + HALF], F32, o)
        prob, o = place("prob", [P, 2, Q_TILES, P], F32, o)
        probT, o = place("probT", [P, 2, Q_TILES, P], F32, o)
        o2 = ln_at
        presum, o2 = place("presum", [P, 2, HALF], F32, o2)
        rstd, o2 = place("rstd", [P, HALF], F32, o2)
        ln_tmp, o2 = place("ln_tmp", [P, 4, HALF], F32, o2)
        assert max(o, o2) <= nc.sbuf_usable_end

        ps = ctx.enter_context(nc.psum_tensor("ps", [P, 8, 512], F32))

        (C_SC0, C_H1S, C_H1B, C_R1S, C_R1B, C_H2S, C_H2B, C_R2S, C_R2B, C_G1, C_G3, C_ONE2,
         C_ONE3) = range(13)

        def col(v, k):
            return v[:, k:k + 1]

        tables_in = sem("tables_in")
        pos_in = sem("pos_in")
        x_in = [sem("x_in0"), sem("x_in1")]
        up_in = [sem("up_in0"), sem("up_in1")]
        dn_in = [sem("dn_in0"), sem("dn_in1")]
        crow_in = [sem(f"crow_in{i}") for i in range(4)]
        up_hi_done = sem("up_hi_done")
        up_lo_done = sem("up_lo_done")
        dn_hi_done = sem("dn_hi_done")
        dn_lo_done = sem("dn_lo_done")
        up_mm = sem("up_mm")
        dn_mm = sem("dn_mm")
        dn_acc = sem("dn_acc")
        gate_read = sem("gate_read")
        prod_done = sem("prod_done")
        g_hi_done = sem("g_hi_done")
        g_ready = sem("g_ready")
        cs_ready = sem("cs_ready")
        crow_used = sem("crow_used")
        mod_sum = sem("mod_sum")
        mod_ready = sem("mod_ready")
        coef_done = sem("coef_done")
        rope_steps = sem("rope_steps")
        trig_done = sem("trig_done")
        sin_ready = sem("sin_ready")
        ln_sum = sem("ln_sum")
        ln_mean = sem("ln_mean")
        ln_centred = sem("ln_centred")
        ln_sq = sem("ln_sq")
        ln_sqmm = sem("ln_sqmm")
        ln_var = sem("ln_var")
        ln_rcp = sem("ln_rcp")
        ln_rstd = sem("ln_rstd")
        ln_y = sem("ln_y")
        pre_h = sem("pre_h")
        hhi_done = sem("hhi_done")
        h_ready = sem("h_ready")
        half_mm = sem("half_mm")
        half_acc = sem("half_acc")
        ln_part = sem("ln_part")
        ln_normed = sem("ln_normed")
        ln_scaled = sem("ln_scaled")
        r_scaled = sem("r_scaled")
        proj_read = sem("proj_read")
        dve_step = sem("dve_step")
        dve_scaled = sem("dve_scaled")
        qkv_ready = sem("qkv_ready")
        carried = sem("carried")
        vband_mm = sem("vband_mm")
        vband_ready = sem("vband_ready")
        score_mm = sem("score_mm")
        negmax_done = sem("negmax_done")
        exp_done = sem("exp_done")
        probs_ready = sem("probs_ready")
        probT_mm = sem("probT_mm")
        probT_ready = sem("probT_ready")
        av_mm = sem("av_mm")
        attn_hi_done = sem("attn_hi_done")
        attn_ready = sem("attn_ready")
        conv_done = sem("conv_done")
        conv_hi_done = sem("conv_hi_done")
        conv_ready = sem("conv_ready")
        merge_parts = sem("merge_parts")
        y_ready = sem("y_ready")
        stored = sem("stored")

        UPB_MIX = [UP_FFN, UP_FFN + UP_MIX]
        UPB_FFN2 = UP_FFN + 2 * UP_MIX
        DNB_MIX = [FF_TILES, FF_TILES + KD]
        DNB_FFN2 = FF_TILES + 2 * KD
        TL_MIX = [FF_TILES, FF_TILES + KD]
        TL_FFN2 = FF_TILES + 2 * KD
        GR_MIX = [FF_TILES, FF_TILES + 2 * KD]
        GR_FFN2 = FF_TILES + 4 * KD
        CH_MIX = [FF_STEPS, FF_STEPS + MIX_STEPS]
        CH_FFN2 = FF_STEPS + 2 * MIX_STEPS
        N_CH = HALF // CHUNK
        ATT_FIRST, LAG_T, LAG_V = 3 + Q_TILES, 2, 3
        assert ATT_FIRST + HALF // CHUNK - 1 + LAG_V < PROJ
        LN_BANKS = [(2, 3), (6, 7), (6, 7), (6, 7), (2, 3), (2, 3)]
        LAST_BANKS = (4, 5, 6, 7, 0, 1)

        def halves(hf):
            return slice(hf * HALF, (hf + 1) * HALF)

        block = ctx.enter_context(nc.Block())

        @block.sync
        def _(sp):
            def load_up(u, slot, src):
                if not isinstance(u, int) or u >= 2:
                    sp.wait_ge(up_lo_done, u - 1)
                sp.dma_start(up_raw[:, slot, :, :].rearrange("p k f -> p (k f)"),
                             up_w[bass.ds(src, 1), :, :].rearrange("a p n -> (a p) n"))\
                    .then_inc(up_in[slot], 16)

            def load_down(d, slot, src):
                if not isinstance(d, int) or d >= 2:
                    sp.wait_ge(dn_lo_done, d - 1)
                sp.dma_start(dn_raw[:, slot, :],
                             down_w[bass.ds(src, 1), :, :].rearrange("a p n -> (a p) n"))\
                    .then_inc(dn_in[slot], 16)

            def load_cond(n, slot, v, k):
                if not isinstance(n, int) or n >= 4:
                    sp.wait_ge(crow_used, n - 3)
                sp.dma_start(crow[:, slot, :],
                             w_cond[bass.ds(v, 1), k, :, :].rearrange("a p n -> (a p) n"))\
                    .then_inc(crow_in[slot], 16)

            sp.dma_start(par[:, :], table).then_inc(tables_in, 16)
            sp.dma_start(mean_m[:, :], mean_w[0]).then_inc(tables_in, 16)
            sp.dma_start(eye[:, :], mean_w[1]).then_inc(tables_in, 16)
            for n in range(2 * KD):
                load_cond(n, n % 4, 1 - n // KD, n % KD)
                if n == KD:
                    sp.dma_start(res[:, :, 0:HALF], x[:, :, 0:HALF]).then_inc(x_in[0], 16)
            load_up(0, 0, 0)
            sp.dma_start(res[:, :, HALF:SEQ], x[:, :, HALF:SEQ]).then_inc(x_in[1], 16)
            load_up(1, 1, 1)
            sp.dma_start(pos_i[:, :], pos.to_broadcast([P, SEQ])).then_inc(pos_in, 16)

            def ffn_step(c, ub, sb, db, dsb, cond=False, first=False):
                if not first:
                    load_up(c * 4 + ub, 0, c * 4 + sb)
                    load_up(c * 4 + (ub + 1), 1, c * 4 + (sb + 1))
                if cond:
                    for k in range(KD):
                        load_cond(c * KD + (KD + k), k % 4, c + 1, k)
                for s in range(2):
                    load_down(c * 2 + (db + s), s, c * 2 + (dsb + s))
                load_up(c * 4 + (ub + 2), 0, c * 4 + (sb + 2))
                load_up(c * 4 + (ub + 3), 1, c * 4 + (sb + 3))

            ffn_step(0, 0, 0, 0, 0, first=True)
            with sp.Fori(1, N_COND - 1) as c:
                ffn_step(c, 0, 0, 0, 0, cond=True)
            with sp.Fori(N_COND - 1, FF_STEPS) as c:
                ffn_step(c, 0, 0, 0, 0)
            for hf in range(2):
                ub, db = UPB_MIX[hf], DNB_MIX[hf]
                with sp.Fori(0, PROJ // 2) as i:
                    for s in range(2):
                        load_up(i * 2 + (ub + s), s, i * 2 + (UP_FFN + s))
                with sp.Fori(0, MIX_STEPS) as i:
                    for s in range(6):
                        load_up(i * 6 + (ub + PROJ + s), s % 2, i * 6 + (UP_FFN + PROJ + s))
                        if s == 1:
                            for d in range(2):
                                load_down(i * 2 + (db + d), d, i * 2 + (FF_TILES + d))
            with sp.Fori(0, FF_STEPS) as c:
                ffn_step(c, UPB_FFN2, UP_FFN + UP_MIX, DNB_FFN2, FF_TILES + KD)
            for hf in range(2):
                for k in range(KD):
                    sp.wait_ge(y_ready, hf * KD + k + 1)
                    sp.dma_start(out[:, k, halves(hf)], res[:, k, halves(hf)]).then_inc(stored, 16)
            sp.wait_ge(stored, 16 * 2 * KD)

        @block.gpsimd
        def _(pool):
            def split_ups(begin, end):
                with pool.Fori(begin // 2, end // 2) as i:
                    for s in range(2):
                        pool.wait_ge(up_hi_done, i * 2 + (s + 1))
                        pool.tensor_tensor(up_lo[:, s, :, :], up_raw[:, s, :, :],
                                           up_hi[:, s, :, :].bitcast(F32), ALU.subtract)\
                            .then_inc(up_lo_done, 1)

            parts = 0

            def sum_tiles(i, acc, before):
                nonlocal parts
                r, dst = res[:, :, halves(i % 2)], presum[:, i % 2, :]
                for k in range(1, KD):
                    pool.wait_ge(acc, before + k + 1)
                    if k > 1:
                        pool.wait_ge(ln_part, parts)
                    ins = pool.tensor_tensor(dst, r[:, 0, :] if k == 1 else dst, r[:, k, :],
                                             ALU.add)
                    ins.then_inc(ln_sum if k == KD - 1 else ln_part, 1)
                    parts += k < KD - 1

            def normalise(i):
                r = res[:, :, halves(i % 2)]
                for k in range(KD):
                    pool.wait_ge(pre_h, (i + 2) * KD + k + 1)
                    pool.tensor_tensor(r[:, k, :], r[:, k, :], rstd[:, :], ALU.mult)\
                        .then_inc(ln_normed, 1)

            split_ups(0, UP_FFN + 2)
            sum_tiles(0, half_acc, 0)
            normalise(0)
            split_ups(UP_FFN + 2, UPB_FFN2 + 2)
            sum_tiles(3, dn_acc, (CH_FFN2 - 1) * KD)
            normalise(3)
            split_ups(UPB_FFN2 + 2, UP_TOTAL)
            sum_tiles(4, half_acc, KD)
            sum_tiles(5, dn_acc, (CH_FFN2 + FF_STEPS - 1) * KD)

        @block.scalar
        def _(act):
            def split_up(u, slot, turn_of):
                act.wait_ge(up_in[slot], turn_of * 16 + 16)
                if not isinstance(u, int) or u >= 2:
                    act.wait_ge(up_mm, u - 1)
                act.activation(up_hi[:, slot, :, :], up_raw[:, slot, :, :], ACT.Copy)\
                    .then_inc(up_hi_done, 1)

            def split_down(chunk):
                for s in range(2):
                    act.wait_ge(dn_in[s], chunk * 16 + 16)
                    if not isinstance(chunk, int) or chunk >= 1:
                        act.wait_ge(dn_mm, chunk * KD)
                    act.activation(dn_hi[:, s, :], dn_raw[:, s, :], ACT.Copy)\
                        .then_inc(dn_hi_done, 1)

            def high_h(i, ks, bias=None):
                for k in ks:
                    act.wait_ge(pre_h, i * KD + k + 1)
                    src, dst = ln_tmp[:, k % 4, :], h_hi[:, k, halves(i % 2)]
                    if bias is None:
                        act.activation(dst, src, ACT.Copy).then_inc(hhi_done, 1)
                    else:
                        act.activation(dst, src, ACT.Identity, bias=bias[:, k:k + 1])\
                            .then_inc(hhi_done, 1)

            def squares(i):
                for k in range(KD):
                    act.wait_ge(ln_centred, i * KD + k + 1)
                    if k >= 4:
                        act.wait_ge(ln_sqmm, i * KD + k - 3)
                    act.activation(ln_tmp[:, k % 4, :], res[:, k, halves(i % 2)], ACT.Square)\
                        .then_inc(ln_sq, 1)

            def root(i):
                act.wait_ge(ln_rcp, i + 1)
                act.activation(rstd[:, :], presum[:, i % 2, :], ACT.Sqrt).then_inc(ln_rstd, 1)

            def gate_tile(t, s, chunk, down, src_done, dst):
                act.wait_ge(prod_done, t + 1)
                if down and s == 0:
                    act.wait_ge(dn_mm, chunk * KD)
                act.activation(dst, src_done, ACT.Copy).then_inc(g_hi_done, 1)

            def ffn_step(c, ub, tb, cb, down, last=False):
                for s in range(2):
                    t = c * 2 + (tb + s)
                    if s == 0 or not last:
                        split_up(c * 4 + (ub + 2 + 2 * s), 0, c * 2 + (ub // 2 + 1 + s))
                    if not isinstance(t, int) or t >= 1:
                        act.wait_ge(prod_done, t)
                    act.wait_ge(up_mm, c * 4 + (ub + 1 + 2 * s))
                    act.activation(tmp[:, 0:2, :], ps[:, 0:2, :], ACT.Silu).then_inc(gate_read, 1)
                    if s == 0:
                        split_up(c * 4 + (ub + 3), 1, c * 2 + (ub // 2 + 1))
                    gate_tile(t, s, c + cb, down, tmp[:, 2:4, :],
                              g_hi[:, s, :].rearrange("p (a t) -> p a t", a=2))
                    if s == 0:
                        split_down(c + cb)
                if not last:
                    split_up(c * 4 + (ub + 5), 1, c * 2 + (ub // 2 + 2))

            act.wait_ge(tables_in, 48)
            act.activation(cs[:, :], par[:, PC_C:PC_C + KD], ACT.Silu).then_inc(cs_ready, 1)
            split_up(0, 0, 0)
            split_up(1, 1, 0)
            for i in range(2):
                high_h(i, range(KD))

            ffn_step(0, 0, 0, 0, False)
            act.wait_ge(rope_steps, 9)
            act.activation(cos_t[:, :], turn[:, :], ACT.Sin).then_inc(trig_done, 1)
            act.wait_ge(rope_steps, 15)
            act.activation(sin_t[:, :], ang[:, :], ACT.Sin).then_inc(trig_done, 1)
            with act.Fori(1, FF_STEPS) as c:
                ffn_step(c, 0, 0, 0, True)

            squares(0)
            root(0)
            high_h(2, range(KD), coef[:, C_H1B, :])

            for hf in range(2):
                ub = UPB_MIX[hf]
                for p in range(PROJ):
                    u = ub + p
                    if p > 0:
                        split_up(u + 1, (u + 1) % 2, (u + 1) // 2)
                    m = p - ATT_FIRST
                    if 0 <= m - LAG_V < N_CH:
                        v = m - LAG_V
                        act.wait_ge(av_mm, hf * N_CH + v + 1)
                        act.activation(
                            attn_hi[:, :, v * CHUNK:(v + 1) * CHUNK],
                            ps[:, 7, 0:Q_TILES * CHUNK].rearrange("p (j t) -> p j t", j=Q_TILES),
                            ACT.Copy).then_inc(attn_hi_done, 1)
                    if 0 <= m - LAG_T < N_CH:
                        a = hf * N_CH + m - LAG_T
                        act.wait_ge(probT_mm, a + 1)
                        if a >= 2:
                            act.wait_ge(av_mm, a - 1)
                        act.activation(probT[:, a % 2, :, :],
                                       ps[:, 6, :].rearrange("p (j t) -> p j t", j=Q_TILES),
                                       ACT.Copy).then_inc(probT_ready, 1)
                    if 0 <= m < N_CH:
                        a = hf * N_CH + m
                        if a >= 2:
                            act.wait_ge(probT_mm, a - 1)
                        act.wait_ge(negmax_done, a + 1)
                        for j in range(Q_TILES):
                            act.activation(prob[:, a % 2, j, :], ps[:, 4 + a % 2, j * P:(j + 1) * P],
                                           ACT.Exp, bias=small[:, a % 2, 1, j:j + 1], scale=SCALE,
                                           accum_out=small[:, a % 2, 3, j:j + 1])
                        act.activation(small[:, a % 2, 4, :], small[:, a % 2, 2, :], ACT.Exp)\
                            .then_inc(exp_done, 1)
                    if p >= 9 and p % 3 == 0:
                        i = p // 3 - 3
                        act.wait_ge(conv_done, hf * CONV_TILES + i + 1)
                        act.activation(conv_hi[:, i, :], tmp[:, 2, :], ACT.Copy)\
                            .then_inc(conv_hi_done, 1)
                act.wait_ge(conv_done, (hf + 1) * CONV_TILES)
                act.activation(conv_hi[:, CONV_TILES - 1, :], tmp[:, 2, :], ACT.Copy)\
                    .then_inc(conv_hi_done, 1)
                act.wait_ge(conv_ready, (hf + 1) * CONV_TILES)

                mb, tb, cb = ub + PROJ, TL_MIX[hf], CH_MIX[hf]
                ln = 1 + hf

                def split(i, n):
                    split_up(i * 6 + (mb + n), n % 2, i * 3 + (mb + n) // 2)

                def sigmoid(i, s, b):
                    if b == 0:
                        act.wait_ge(prod_done, i * 2 + (tb + s))
                    act.wait_ge(up_mm, i * 6 + (mb + 3 * s + b + 1))
                    act.activation(tmp[:, b, :], ps[:, b, :], ACT.Sigmoid).then_inc(gate_read, 1)

                def merge_step(i, first=False):
                    sigmoid(i, 0, 0)
                    split(i, 2)
                    if first:
                        squares(ln)
                    sigmoid(i, 0, 1)
                    split(i, 3)
                    split(i, 4)
                    gate_tile(i * 2 + tb, 0, i + cb, not first, tmp[:, 2, :], mg_hi[:, 0, :])
                    split_down(i + cb)
                    sigmoid(i, 1, 0)
                    split(i, 5)
                    if first:
                        bias = coef[:, (C_H1B, C_H2B)[hf], :]
                        root(ln)
                        high_h(2 + ln, range(0, 2), bias)
                        split(i, 6)
                        high_h(2 + ln, range(2, 4), bias)
                        sigmoid(i, 1, 1)
                        split(i, 7)
                        high_h(2 + ln, range(4, KD), bias)
                    else:
                        sigmoid(i, 1, 1)
                        split(i, 6)
                        split(i, 7)
                    gate_tile(i * 2 + (tb + 1), 1, i + cb, not first, tmp[:, 2, :], mg_hi[:, 1, :])

                split(0, 1)
                merge_step(0, first=True)
                with act.Fori(1, MIX_STEPS) as i:
                    merge_step(i)

            squares(3)
            root(3)
            high_h(5, range(KD), coef[:, C_H2B, :])

            ffn_step(0, UPB_FFN2, TL_FFN2, CH_FFN2, False)
            with act.Fori(1, FF_STEPS - 1) as c:
                ffn_step(c, UPB_FFN2, TL_FFN2, CH_FFN2, True)
            ffn_step(FF_STEPS - 1, UPB_FFN2, TL_FFN2, CH_FFN2, True, last=True)

            def add_bias(i):
                for k in range(KD):
                    act.wait_ge(ln_scaled, (i - 4) * KD + k + 1)
                    r = res[:, k, halves(i % 2)]
                    b = PC_LN + 5 * KD + k
                    act.activation(r, r, ACT.Identity, bias=par[:, b:b + 1]).then_inc(y_ready, 1)

            squares(4)
            root(4)
            squares(5)
            add_bias(4)
            root(5)
            add_bias(5)

        @block.vector
        def _(dve):
            def split_down(chunk):
                for s in range(2):
                    dve.wait_ge(dn_hi_done, chunk * 2 + (s + 1))
                    dve.tensor_tensor(dn_lo[:, s, :], dn_raw[:, s, :], dn_hi[:, s, :].bitcast(F32),
                                      ALU.subtract).then_inc(dn_lo_done, 1)

            def cond_rows(n, slot, turn_of, k, vectors):
                dve.wait_ge(crow_in[slot], turn_of * 16 + 16)
                if k == 0:
                    if not isinstance(vectors, int) or vectors >= 1:
                        dve.wait_ge(mod_sum, vectors)
                    dve.tensor_scalar(cacc[:, :], crow[:, slot, :], cs[:, 0:1], None, ALU.mult)\
                        .then_inc(crow_used, 1)
                else:
                    dve.wait_ge(crow_used, n)
                    dve.scalar_tensor_tensor(out=cacc[:, :], in0=crow[:, slot, :],
                                             scalar=cs[:, k:k + 1], in1=cacc[:, :], op0=ALU.mult,
                                             op1=ALU.add).then_inc(crow_used, 1)

            def cond_vector(v, vectors):
                dve.wait_ge(mod_sum, vectors + 1)
                dve.tensor_tensor(mod[:, bass.ds(v, 1), :].rearrange("p a k -> p (a k)"),
                                  ps[:, 6, 0:KD], par[:, bass.ds(v * KD + PC_BCOND, KD)], ALU.add)\
                    .then_inc(mod_ready, 1)

            def block_input(i, pre, post):
                for k in range(KD + 1):
                    if k < KD:
                        if i or k >= 4:
                            dve.wait_ge(h_ready, i * KD + k - 3)
                        pre(k).then_inc(pre_h, 1)
                    if k >= 1:
                        dve.wait_ge(hhi_done, i * KD + k)
                        post(k - 1).then_inc(h_ready, 1)

            def first_input(hf):
                dve.wait_ge(x_in[hf], 16)
                block_input(
                    hf,
                    lambda k: dve.tensor_scalar(ln_tmp[:, k % 4, :], res[:, k, halves(hf)],
                                                coef[:, C_SC0, k:k + 1], mod[:, 0, k:k + 1],
                                                ALU.mult, ALU.add),
                    lambda k: dve.tensor_tensor(h_lo[:, k, halves(hf)], ln_tmp[:, k % 4, :],
                                                h_hi[:, k, halves(hf)].bitcast(F32),
                                                ALU.subtract))

            def ln_input(i, scale, bias):
                hf = i % 2
                dve.wait_ge(ln_rstd, i + 1)
                block_input(
                    i + 2,
                    lambda k: dve.scalar_tensor_tensor(
                        out=ln_tmp[:, k % 4, :], in0=res[:, k, halves(hf)],
                        scalar=scale[:, k:k + 1], in1=rstd[:, :], op0=ALU.mult, op1=ALU.mult),
                    lambda k: dve.scalar_tensor_tensor(
                        out=h_lo[:, k, halves(hf)], in0=ln_tmp[:, k % 4, :],
                        scalar=bias[:, k:k + 1], in1=h_hi[:, k, halves(hf)].bitcast(F32),
                        op0=ALU.add, op1=ALU.subtract))

            def scale_residual(i, scale, bias, normalised):
                for k in range(KD):
                    r = res[:, k, halves(i % 2)]
                    if normalised is not None:
                        dve.wait_ge(ln_normed, normalised + k + 1)
                    else:
                        dve.scalar_tensor_tensor(out=r, in0=r, scalar=scale[:, k:k + 1],
                                                 in1=rstd[:, :], op0=ALU.mult, op1=ALU.mult)\
                            .then_inc(dve_scaled, 1)
                if normalised is None:
                    scaled[0] += KD
                for k in range(KD):
                    r = res[:, k, halves(i % 2)]
                    if normalised is not None:
                        dve.tensor_scalar(r, r, scale[:, k:k + 1], bias[:, k:k + 1], ALU.mult,
                                          ALU.add).then_inc(r_scaled, 1)
                    else:
                        dve.wait_ge(dve_scaled, scaled[0] - KD + k + 1)
                        dve.tensor_scalar(r, r, bias[:, k:k + 1], None, ALU.add)\
                            .then_inc(r_scaled, 1)

            scaled = [0]

            def centre(i, k):
                r = res[:, k, halves(i % 2)]
                if k == 0:
                    dve.wait_ge(ln_mean, i + 1)
                dve.tensor_tensor(r, r, ps[:, LN_BANKS[i][0], :], ALU.subtract)\
                    .then_inc(ln_centred, 1)

            def variance(i):
                dve.wait_ge(ln_sqmm, (i + 1) * KD)
                dve.tensor_scalar(presum[:, i % 2, :], ps[:, LN_BANKS[i][1], :], LN_EPS, None,
                                  ALU.add).then_inc(ln_var, 1)
                dve.wait_ge(ln_var, i + 1)
                dve.reciprocal(presum[:, i % 2, :], presum[:, i % 2, :]).then_inc(ln_rcp, 1)

            def ffn_step(c, tb, gb, ub, cb, gate, down, cond=False):
                if cond:
                    for k in range(KD):
                        cond_rows(c * KD + (KD + k), k % 4, c * 2 + (2 + k // 4), k, c + 1)
                    cond_vector(c + 1, c + 1)
                    dve.wait_ge(mod_ready, c + 2)
                    dve.tensor_scalar(coef[:, C_G1, :], mod[:, 2, :], FFN_RES, None, ALU.mult)\
                        .then_inc(coef_done, 1)
                    dve.wait_ge(coef_done, c + 1)
                for s in range(2):
                    t = c * 2 + (tb + s)
                    dve.wait_ge(gate_read, c * 2 + (gb + s + 1))
                    dve.wait_ge(up_mm, c * 4 + (ub + 2 + 2 * s))
                    if not isinstance(t, int) or t >= 1:
                        dve.wait_ge(g_ready, t)
                    dve.tensor_tensor(tmp[:, 2:4, :], tmp[:, 0:2, :], ps[:, 2:4, :], ALU.mult)\
                        .then_inc(prod_done, 1)
                    if down and s == 0:
                        for m in range(KD):
                            dve.wait_ge(dn_mm, (c + (cb - 1)) * KD + (m + 1))
                            r = res[:, m, :].rearrange("p (a t) -> p a t", a=2)
                            b = 4 + 2 * (m % 2)
                            dve.scalar_tensor_tensor(out=r, in0=ps[:, b:b + 2, :],
                                                     scalar=gate[:, m:m + 1], in1=r, op0=ALU.mult,
                                                     op1=ALU.add).then_inc(dn_acc, 1)
                    dve.wait_ge(g_hi_done, t + 1)
                    dve.tensor_tensor(g_lo[:, s, :].rearrange("p (a t) -> p a t", a=2),
                                      tmp[:, 2:4, :],
                                      g_hi[:, s, :].bitcast(F32).rearrange("p (a t) -> p a t", a=2),
                                      ALU.subtract).then_inc(g_ready, 1)
                    if s == 0:
                        split_down(c + cb)

            def ffn_last(chunk, gate, halves_before, i):
                for n in range(2 * KD):
                    hf, m = n // KD, n % KD
                    if hf == 0:
                        dve.wait_ge(half_mm, halves_before + m + 1)
                    else:
                        dve.wait_ge(dn_mm, chunk * KD + m + 1)
                    r = res[:, m, halves(hf)]
                    dve.scalar_tensor_tensor(out=r, in0=ps[:, LAST_BANKS[n % 6], :],
                                             scalar=gate[:, m:m + 1], in1=r, op0=ALU.mult,
                                             op1=ALU.add).then_inc(dn_acc if hf else half_acc, 1)
                    if n > KD:
                        centre(i, n - KD - 1)
                centre(i, KD - 1)

            dve.wait_ge(tables_in, 48)
            dve.tensor_scalar(negsink[:, :], par[:, PC_SINK:PC_SINK + Q_TILES], -1.0, None,
                              ALU.mult).then_inc(dve_step, 1)
            steps = 1
            dve.wait_ge(cs_ready, 1)
            for n in range(2 * KD):
                cond_rows(n, n % 4, n // 4, n % KD, n // KD)
                if n % KD == KD - 1:
                    cond_vector(1 - n // KD, n // KD)
            dve.wait_ge(mod_ready, 2)
            dve.tensor_scalar(coef[:, C_SC0, :], mod[:, 1, :], 1.0, None, ALU.add)\
                .then_inc(coef_done, 1)
            dve.wait_ge(coef_done, 1)
            for hf in range(2):
                first_input(hf)
            for n in range(2 * KD):
                dve.wait_ge(hhi_done, n + 1)
                r = res[:, n % KD, halves(n // KD)]
                dve.tensor_scalar(r, r, ALPHA, None, ALU.mult).then_inc(r_scaled, 1)

            dve.wait_ge(pos_in, 16)
            dve.tensor_copy(ang[:, :], pos_i[:, :]).then_inc(rope_steps, 1)
            dve.wait_ge(rope_steps, 1)
            dve.tensor_scalar(ang[:, :], ang[:, :], par[:, PC_INV:PC_INV + 1], None, ALU.mult)\
                .then_inc(rope_steps, 1)
            step = 2
            for quarter, dst in ((0.25, turn), (0.0, ang)):
                dve.wait_ge(rope_steps, step)
                dve.tensor_scalar(turns[:, :], ang[:, :], 1.0 / TWO_PI, quarter, ALU.mult, ALU.add)\
                    .then_inc(rope_steps, 1)
                dve.wait_ge(rope_steps, step + 1)
                dve.tensor_scalar(turns[:, :], turns[:, :], ROUND, -ROUND, ALU.add, ALU.add)\
                    .then_inc(rope_steps, 1)
                src = ang
                for n, part in enumerate((CW1, CW2, CW3)):
                    dve.wait_ge(rope_steps, step + 2 + n)
                    dve.scalar_tensor_tensor(out=dst[:, :], in0=turns[:, :], scalar=-part,
                                             in1=src[:, :], op0=ALU.mult, op1=ALU.add)\
                        .then_inc(rope_steps, 1)
                    src = dst
                step += 5
                if quarter:
                    dve.wait_ge(rope_steps, step)
                    dve.tensor_scalar(dst[:, :], dst[:, :], quarter * TWO_PI, None, ALU.add)\
                        .then_inc(rope_steps, 1)
                    step += 1
                dve.wait_ge(rope_steps, step)
                dve.tensor_scalar(dst[:, :], dst[:, :], PI_BELOW, -PI_BELOW, ALU.min, ALU.max)\
                    .then_inc(rope_steps, 1)
                step += 1
            dve.wait_ge(r_scaled, 2 * KD)
            ffn_step(0, 0, 0, 0, 0, coef[:, C_G1, :], False)
            with dve.Fori(1, N_COND - 1) as c:
                ffn_step(c, 0, 0, 0, 0, coef[:, C_G1, :], True, cond=True)
            with dve.Fori(N_COND - 1, FF_STEPS) as c:
                ffn_step(c, 0, 0, 0, 0, coef[:, C_G1, :], True)
            dve.wait_ge(trig_done, 2)
            dve.tensor_scalar(sin_t[:, :], sin_t[:, :], par[:, PC_SIGN:PC_SIGN + 1], None, ALU.mult)\
                .then_inc(sin_ready, 1)
            coefs = N_COND - 1
            rows = ((4, 3, 0, C_ONE2, C_H1S, C_H1B, C_R1S, C_R1B),
                    (7, 6, 2, C_ONE3, C_H2S, C_H2B, C_R2S, C_R2B))
            for sc, sh, ln, one, hs, hb, rs, rb in rows:
                g = par[:, PC_LN + ln * KD:PC_LN + (ln + 1) * KD]
                b = par[:, PC_LN + (ln + 1) * KD:PC_LN + (ln + 2) * KD]
                dve.tensor_scalar(coef[:, one, :], mod[:, sc, :], 1.0, None, ALU.add)\
                    .then_inc(coef_done, 1)
                dve.wait_ge(coef_done, coefs + 1)
                dve.tensor_tensor(coef[:, hs, :], coef[:, one, :], g, ALU.mult)\
                    .then_inc(coef_done, 1)
                dve.tensor_tensor(coef[:, hb, :], coef[:, one, :], b, ALU.mult)\
                    .then_inc(coef_done, 1)
                dve.tensor_scalar(coef[:, rs, :], g, ALPHA, None, ALU.mult).then_inc(coef_done, 1)
                dve.tensor_scalar(coef[:, rb, :], b, ALPHA, None, ALU.mult).then_inc(coef_done, 1)
                dve.wait_ge(coef_done, coefs + 3)
                dve.tensor_tensor(coef[:, hb, :], coef[:, hb, :], mod[:, sh, :], ALU.add)\
                    .then_inc(coef_done, 1)
                coefs += 6
            dve.tensor_scalar(coef[:, C_G3, :], mod[:, 8, :], FFN_RES, None, ALU.mult)\
                .then_inc(coef_done, 1)
            coefs += 1
            dve.memset(kT[:, 0:CHUNK], 0.0).then_inc(carried, 1)
            dve.memset(vT[:, 0:CHUNK], 0.0).then_inc(carried, 1)
            dve.memset(ucarry[:, :, :], 0.0).then_inc(carried, 1)
            dve.wait_ge(coef_done, coefs)
            carries = 3

            ffn_last(FF_STEPS - 1, coef[:, C_G1, :], 0, 0)
            variance(0)
            ln_input(0, coef[:, C_H1S, :], coef[:, C_H1B, :])
            dve.wait_ge(sin_ready, 1)

            for hf in range(2):
                ub = UPB_MIX[hf]
                toks = halves(hf)

                def rope(bank, dst, slot):
                    for a in range(4):
                        b = a ^ 1
                        dve.tensor_tensor(tmp[32 * a:32 * a + 32, slot, :],
                                          ps[32 * b:32 * b + 32, bank, :],
                                          sin_t[32 * b:32 * b + 32, toks], ALU.mult)\
                            .then_inc(dve_step, 1)
                    dve.tensor_tensor(dst, ps[:, bank, :], cos_t[:, toks], ALU.mult)\
                        .then_inc(proj_read, 1)

                def add_rope(dst, slot, n, reads):
                    dve.wait_ge(dve_step, n)
                    dve.wait_ge(proj_read, reads)
                    dve.tensor_tensor(dst, dst, tmp[:, slot, :], ALU.add).then_inc(qkv_ready, 1)

                for p in range(PROJ):
                    u, bank, m = ub + p, p % 4, p - ATT_FIRST
                    reads = hf * PROJ + p
                    if p == 0 and hf == 1:
                        dve.wait_ge(up_mm, u + 1)
                        dve.tensor_copy(kT[:, 0:CHUNK], kT[:, HALF:HALF + CHUNK])\
                            .then_inc(carried, 1)
                        dve.tensor_copy(vT[:, 0:CHUNK], vT[:, HALF:HALF + CHUNK])\
                            .then_inc(carried, 1)
                        carries += 2
                    if p == 3:
                        dve.wait_ge(vband_mm, hf + 1)
                        dve.tensor_copy(vband[:, :, :],
                                        ps[:, 6:8, :].rearrange("p b (c t) -> p (b c) t", t=P))\
                            .then_inc(vband_ready, 1)
                    if 0 <= m - LAG_V < N_CH:
                        v = m - LAG_V
                        dve.wait_ge(attn_hi_done, hf * N_CH + v + 1)
                        dst = slice(v * CHUNK, (v + 1) * CHUNK)
                        dve.tensor_tensor(
                            attn_lo[:, :, dst],
                            ps[:, 7, 0:Q_TILES * CHUNK].rearrange("p (j t) -> p j t", j=Q_TILES),
                            attn_hi[:, :, dst].bitcast(F32), ALU.subtract).then_inc(attn_ready, 1)
                    if 0 <= m < N_CH:
                        a = hf * N_CH + m
                        sm = small[:, a % 2, :, :]
                        score = ps[:, 4 + a % 2, :].rearrange("p (j t) -> p j t", j=Q_TILES)
                        dve.wait_ge(score_mm, a + 1)
                        if a == 0:
                            dve.memset(score[:, :, 0:CHUNK], MASKED).then_inc(dve_step, 1)
                            steps += 1
                            dve.wait_ge(dve_step, steps)
                        dve.tensor_reduce(sm[:, 0, :], score, AX.X, ALU.max).then_inc(dve_step, 1)
                        steps += 1
                        dve.wait_ge(dve_step, steps)
                        dve.scalar_tensor_tensor(out=sm[:, 1, :], in0=sm[:, 0, :], scalar=-SCALE,
                                                 in1=negsink[:, :], op0=ALU.mult, op1=ALU.min)\
                            .then_inc(dve_step, 1)
                        steps += 1
                        dve.wait_ge(dve_step, steps)
                        dve.tensor_tensor(sm[:, 2, :], sm[:, 1, :], negsink[:, :], ALU.subtract)\
                            .then_inc(negmax_done, 1)
                        dve.wait_ge(exp_done, a + 1)
                        dve.tensor_tensor(sm[:, 5, :], sm[:, 3, :], sm[:, 4, :], ALU.add)\
                            .then_inc(dve_step, 1)
                        steps += 1
                        dve.wait_ge(dve_step, steps)
                        dve.reciprocal(sm[:, 5, :], sm[:, 5, :]).then_inc(dve_step, 1)
                        steps += 1
                        dve.wait_ge(dve_step, steps)
                        dve.tensor_tensor(
                            prob[:, a % 2, :, :], prob[:, a % 2, :, :],
                            sm[:, 5, :].rearrange("p (j o) -> p j o", o=1)
                            .to_broadcast([P, Q_TILES, P]), ALU.mult).then_inc(probs_ready, 1)
                    if p >= 9 and p % 3 == 0:
                        i = p // 3 - 3
                        dve.wait_ge(conv_hi_done, hf * CONV_TILES + i + 1)
                        dve.tensor_tensor(conv_lo[:, i, :], tmp[:, 2, :],
                                          conv_hi[:, i, :].bitcast(F32), ALU.subtract)\
                            .then_inc(conv_ready, 1)
                    dve.wait_ge(up_mm, u + 1)
                    if p == 0:
                        dve.wait_ge(carried, carries)
                        rope(bank, kT[:, CHUNK:CHUNK + HALF], p % 2)
                        steps += 4
                        add_rope(kT[:, CHUNK:CHUNK + HALF], p % 2, steps, reads + 1)
                    elif p == 1:
                        dve.tensor_copy(vT[:, CHUNK:CHUNK + HALF], ps[:, bank, :])\
                            .then_inc(proj_read, 1)
                    elif p < 2 + Q_TILES:
                        dve.wait_ge(qkv_ready, hf * (1 + Q_TILES) + p - 1)
                        rope(bank, qT[:, p - 2, :], p % 2)
                        steps += 4
                        add_rope(qT[:, p - 2, :], p % 2, steps, reads + 1)
                    elif p % 3 == 0:
                        dve.tensor_copy(tmp[:, 0, :], ps[:, bank, :]).then_inc(proj_read, 1)
                    elif p % 3 == 1:
                        i = p // 3 - 2
                        dve.wait_ge(proj_read, reads)
                        dve.tensor_copy(ubuf[:, 0:CONV_K - 1], ucarry[:, i, :])\
                            .then_inc(dve_step, 1)
                        dve.tensor_tensor(ubuf[:, CONV_K - 1:], ps[:, bank, :], tmp[:, 0, :],
                                          ALU.mult).then_inc(proj_read, 1)
                        dve.wait_ge(proj_read, reads + 1)
                        dve.tensor_copy(ucarry[:, i, :], ubuf[:, HALF:HALF + CONV_K - 1])\
                            .then_inc(dve_step, 1)
                        steps += 2
                        dve.wait_ge(dve_step, steps)
                        for j in range(CONV_K):
                            tap = CONV_K - 1 - j
                            w = par[:, PC_CONV + tap * CONV_TILES + i:
                                    PC_CONV + tap * CONV_TILES + i + 1]
                            if j == 0:
                                dve.tensor_scalar(tmp[:, 1, :], ubuf[:, tap:tap + HALF], w, None,
                                                  ALU.mult).then_inc(dve_step, 1)
                            else:
                                dve.wait_ge(dve_step, steps)
                                dve.scalar_tensor_tensor(out=tmp[:, 1, :],
                                                         in0=ubuf[:, tap:tap + HALF], scalar=w,
                                                         in1=tmp[:, 1, :], op0=ALU.mult,
                                                         op1=ALU.add).then_inc(dve_step, 1)
                            steps += 1
                    else:
                        dve.wait_ge(dve_step, steps)
                        i = p // 3 - 2
                        if i >= 1:
                            dve.wait_ge(conv_ready, hf * CONV_TILES + i)
                        dve.tensor_tensor(tmp[:, 2, :], ps[:, bank, :], tmp[:, 1, :], ALU.mult)\
                            .then_inc(proj_read, 1)
                        dve.wait_ge(proj_read, reads + 1)
                        dve.sem_inc(conv_done, 1)
                dve.wait_ge(conv_hi_done, (hf + 1) * CONV_TILES)
                dve.tensor_tensor(conv_lo[:, CONV_TILES - 1, :], tmp[:, 2, :],
                                  conv_hi[:, CONV_TILES - 1, :].bitcast(F32), ALU.subtract)\
                    .then_inc(conv_ready, 1)

                mb, tb, gb, cb = ub + PROJ, TL_MIX[hf], GR_MIX[hf], CH_MIX[hf]

                def add_down(chunk):
                    for m in range(KD):
                        dve.wait_ge(dn_mm, chunk * KD + (m + 1))
                        dve.scalar_tensor_tensor(out=res[:, m, toks], in0=ps[:, 4 + m % 4, :],
                                                 scalar=mod[:, 5, m:m + 1], in1=res[:, m, toks],
                                                 op0=ALU.mult, op1=ALU.add).then_inc(dn_acc, 1)

                def merge_step(i, down):
                    for s in range(2):
                        t = i * 2 + (tb + s)
                        dve.wait_ge(gate_read, i * 4 + (gb + 2 * s + 2))
                        dve.wait_ge(up_mm, i * 6 + (mb + 3 * s + 3))
                        dve.wait_ge(g_ready, t)
                        for b in range(2):
                            dve.tensor_tensor(tmp[:, 2 + b, :], tmp[:, b, :], ps[:, 2 + b, :],
                                              ALU.mult).then_inc(merge_parts, 1)
                        dve.wait_ge(merge_parts, i * 4 + ((tb + s - FF_TILES) * 2 + 2))
                        dve.tensor_tensor(tmp[:, 2, :], tmp[:, 2, :], tmp[:, 3, :], ALU.add)\
                            .then_inc(prod_done, 1)
                        if s == 0 and down:
                            add_down(i + (cb - 1))
                        dve.wait_ge(g_hi_done, t + 1)
                        dve.tensor_tensor(mg_lo[:, s, :], tmp[:, 2, :], mg_hi[:, s, :].bitcast(F32),
                                          ALU.subtract).then_inc(g_ready, 1)
                        if s == 0:
                            split_down(i + cb)
                        if s == 0 and not down:
                            variance(ln)
                            ln_input(ln, *(coef[:, c, :] for c in ((C_H1S, C_H1B),
                                                                   (C_H2S, C_H2B))[hf]))

                ln = 1 + hf
                dve.wait_ge(attn_ready, (hf + 1) * N_CH)
                dve.tensor_reduce(presum[:, ln % 2, :],
                                  res[:, :, halves(ln % 2)].rearrange("p k t -> p t k"), AX.X,
                                  ALU.add).then_inc(ln_sum, 1)
                for k in range(KD):
                    centre(ln, k)
                merge_step(0, False)
                if hf == 0:
                    scale_residual(0, coef[:, C_R1S, :], coef[:, C_R1B, :], 0)
                    scale_residual(1, coef[:, C_R1S, :], coef[:, C_R1B, :], None)
                else:
                    scale_residual(2, coef[:, C_R2S, :], coef[:, C_R2B, :], None)
                dve.wait_ge(r_scaled, (4, 5)[hf] * KD)
                with dve.Fori(1, MIX_STEPS) as i:
                    merge_step(i, True)
                add_down(cb + MIX_STEPS - 1)

            for k in range(KD):
                centre(3, k)
            variance(3)
            ln_input(3, coef[:, C_H2S, :], coef[:, C_H2B, :])

            gate = coef[:, C_G3, :]
            ffn_step(0, TL_FFN2, GR_FFN2, UPB_FFN2, CH_FFN2, gate, False)
            scale_residual(3, coef[:, C_R2S, :], coef[:, C_R2B, :], KD)
            dve.wait_ge(r_scaled, 6 * KD)
            with dve.Fori(1, FF_STEPS) as c:
                ffn_step(c, TL_FFN2, GR_FFN2, UPB_FFN2, CH_FFN2, gate, True)

            def scale_output(i):
                dve.wait_ge(ln_rstd, i + 1)
                for k in range(KD):
                    r = res[:, k, halves(i % 2)]
                    g = PC_LN + 4 * KD + k
                    dve.scalar_tensor_tensor(out=r, in0=r, scalar=par[:, g:g + 1], in1=rstd[:, :],
                                             op0=ALU.mult, op1=ALU.mult).then_inc(ln_scaled, 1)

            ffn_last(CH_FFN2 + FF_STEPS - 1, gate, KD, 4)
            variance(4)
            for k in range(KD):
                centre(5, k)
            scale_output(4)
            variance(5)
            scale_output(5)

        @block.tensor
        def _(pe):
            def passes(w_hi, w_lo, v_hi, v_lo):
                return ((w_hi, v_hi), (w_hi, v_lo), (w_lo, v_hi))

            def up_granule(u, slot, half_list, out_of, ks=range(KD), v_hi=h_hi, v_lo=h_lo,
                           last=True, tokens=None, ready=None, ready_at=None, k_of=None,
                           begin=0, end=KD - 1):
                for hf in half_list:
                    toks = halves(hf) if tokens is None else tokens
                    for k in ks:
                        if ready is not None:
                            pe.wait_ge(ready, ready_at(hf, k))
                        kv = k if k_of is None else k_of(k)
                        for n, (w, v) in enumerate(passes(up_hi, up_lo, v_hi, v_lo)):
                            mm = pe.matmul(out_of(hf), w[:, slot, k, :], v[:, kv, toks],
                                           start=(k == begin and n == 0),
                                           stop=(k == end and n == 2))
                if last:
                    mm.then_inc(up_mm, 1)

            def down_tile(m, half_list, out_of, v_hi, v_lo, toks_of):
                for hf in half_list:
                    for s in range(2):
                        for n, (w, v) in enumerate(passes(dn_hi, dn_lo, v_hi, v_lo)):
                            mm = pe.matmul(out_of(hf), w[:, s, m * P:(m + 1) * P],
                                           v[:, s, toks_of(hf)], start=(s == 0 and n == 0),
                                           stop=(s == 1 and n == 2))
                mm.then_inc(dn_mm, 1)

            def ffn_down(chunk, vectors=None):
                pe.wait_ge(dn_lo_done, chunk * 2 + 2)
                pe.wait_ge(g_ready, chunk * 2 + 2)
                for m in range(KD):
                    if not isinstance(chunk, int) or chunk > 0 or m >= 2:
                        pe.wait_ge(dn_acc, chunk * KD + (m - 1))
                    if m == 1 and vectors is not None:
                        pe.wait_ge(mod_ready, vectors)
                    down_tile(m, range(2), lambda hf: ps[:, 4 + 2 * (m % 2) + hf, :], g_hi, g_lo,
                              halves)

            def cond_sum(vectors):
                pe.wait_ge(crow_used, vectors * KD + KD)
                for j in range(KD):
                    mm = pe.matmul(ps[:, 6, j:j + 1], cacc[:, j * P:(j + 1) * P],
                                   par[:, PC_ONE:PC_ONE + 1], start=True, stop=True)
                mm.then_inc(mod_sum, 1)

            def ffn_last(chunk, halves_before, i, gates):
                def tile(n, ss):
                    m, hf = n % KD, n // KD
                    for s in ss:
                        for j, (w, v) in enumerate(passes(dn_hi, dn_lo, g_hi, g_lo)):
                            mm = pe.matmul(ps[:, LAST_BANKS[n % 6], :], w[:, s, m * P:(m + 1) * P],
                                           v[:, s, halves(hf)], start=(s == 0 and j == 0),
                                           stop=(s == 1 and j == 2))
                    if ss[-1] == 1:
                        mm.then_inc(dn_mm if hf else half_mm, 1)

                pe.wait_ge(dn_lo_done, chunk * 2 + 2)
                pe.wait_ge(g_ready, chunk * 2 + 1)
                pe.wait_ge(dn_acc, chunk * KD)
                for n in range(6):
                    if n == 4:
                        pe.wait_ge(gate_read, gates)
                    tile(n, (0,))
                pe.wait_ge(g_ready, chunk * 2 + 2)
                for n in range(2 * KD):
                    if n >= 6:
                        if n - 6 < KD:
                            pe.wait_ge(half_acc, halves_before + n - 5)
                        else:
                            pe.wait_ge(dn_acc, chunk * KD + n - 5 - KD)
                    tile(n, (1,) if n < 6 else (0, 1))
                    if n == KD + 1:
                        mean(i)
                    if n >= KD + 3:
                        mean_square(i, n - KD - 3)
                for k in range(KD - 3, KD):
                    mean_square(i, k)

            def ffn_step(c, ub, tb, gb, cb, down, cond=False, begun=None, h_from=0):
                for s in range(2):
                    t = c * 2 + (tb + s)
                    if begun is None or s == 1:
                        pe.wait_ge(up_lo_done, c * 4 + (ub + 2 * s + 1))
                        pe.wait_ge(gate_read, c * 2 + (gb + s))
                        up_granule(None, 0, range(2), lambda hf: ps[:, hf, :])
                        pe.wait_ge(up_lo_done, c * 4 + (ub + 2 * s + 2))
                        pe.wait_ge(prod_done, t)
                        up_granule(None, 1, range(2), lambda hf: ps[:, 2 + hf, :])
                    else:
                        up_granule(None, 0, [1], lambda hf: ps[:, hf, :], ready=h_ready,
                                   ready_at=lambda hf, k: h_from + k + 1)
                        up_granule(None, 1, [1], lambda hf: ps[:, 2 + hf, :])
                    if s == 0 and cond:
                        if not isinstance(c, int) or c > 1:
                            pe.wait_ge(dn_acc, (c - 1) * KD)
                        cond_sum(c + 1)
                    if s == 0 and down:
                        ffn_down(c + (cb - 1), c + 2 if cond else None)

            def mean(i):
                pe.wait_ge(ln_sum, i + 1)
                if i == 5:
                    pe.wait_ge(ln_centred, i * KD)
                pe.matmul(ps[:, LN_BANKS[i][0], :], mean_m[:, :], presum[:, i % 2, :], start=True,
                          stop=True).then_inc(ln_mean, 1)

            def mean_square(i, k):
                pe.wait_ge(ln_sq, i * KD + k + 1)
                if k == 0 and i > 0:
                    pe.wait_ge(ln_var, i)
                pe.matmul(ps[:, LN_BANKS[i][1], :], mean_m[:, :], ln_tmp[:, k % 4, :],
                          start=(k == 0), stop=(k == KD - 1)).then_inc(ln_sqmm, 1)

            pe.wait_ge(tables_in, 48)
            for vectors in range(2):
                if vectors:
                    pe.wait_ge(mod_ready, vectors)
                cond_sum(vectors)
            pe.wait_ge(mod_ready, 2)

            pe.wait_ge(up_lo_done, 1)
            up_granule(None, 0, [0], lambda hf: ps[:, 0, :], ready=h_ready,
                       ready_at=lambda hf, k: k + 1, last=False)
            pe.wait_ge(up_lo_done, 2)
            up_granule(None, 1, [0], lambda hf: ps[:, 2, :], last=False)
            ffn_step(0, 0, 0, 0, 0, False, begun=True, h_from=KD)
            ffn_step(1, 0, 0, 0, 0, True, cond=True)
            with pe.Fori(2, N_COND - 1) as c:
                ffn_step(c, 0, 0, 0, 0, True, cond=True)
            with pe.Fori(N_COND - 1, FF_STEPS) as c:
                ffn_step(c, 0, 0, 0, 0, True)
            ffn_last(FF_STEPS - 1, 0, 0, FF_TILES)

            for hf in range(2):
                ub = UPB_MIX[hf]
                acc0 = CH_MIX[hf] * KD

                def project(hf, p):
                    u = UPB_MIX[hf] + p
                    pe.wait_ge(up_lo_done, u + 1)
                    if p >= 4:
                        pe.wait_ge(proj_read, hf * PROJ + p - 3)
                    elif hf == 1:
                        pe.wait_ge(prod_done, TL_MIX[1])
                    elif p == 2:
                        pe.wait_ge(ln_var, 1)
                    up_granule(u, u % 2, [hf], lambda h: ps[:, p % 4, :],
                               ready=h_ready if p == 0 else None,
                               ready_at=lambda h, k: (2 + h) * KD + k + 1)

                for p in range(PROJ):
                    m = p - ATT_FIRST
                    if p == 3:
                        pe.wait_ge(proj_read, hf * PROJ + 2)
                        pe.wait_ge(dn_acc, acc0)
                        for n in range(N_CH):
                            mm = pe.transpose(ps[:, 6 + n // 4, (n % 4) * P:(n % 4 + 1) * P],
                                              vT[:, n * CHUNK:n * CHUNK + P], eye[:, :])
                        mm.then_inc(vband_mm, 1)
                    if 0 <= m - LAG_V < N_CH:
                        v = m - LAG_V
                        a = hf * N_CH + v
                        pe.wait_ge(probT_ready, a + 1)
                        pe.wait_ge(vband_ready, hf + 1)
                        if v >= 1:
                            pe.wait_ge(attn_ready, a)
                        for g in range(2):
                            rows = slice(g * HEAD_DIM, (g + 1) * HEAD_DIM)
                            mm = pe.matmul(ps[rows, 7, 0:Q_TILES * CHUNK], vband[:, v, rows],
                                           probT[:, a % 2, :, rows], start=True, stop=True)
                        mm.then_inc(av_mm, 1)
                    if 0 <= m - LAG_T < N_CH:
                        a = hf * N_CH + m - LAG_T
                        pe.wait_ge(probs_ready, a + 1)
                        pe.wait_ge(vband_ready, hf + 1)
                        if a >= 1:
                            pe.wait_ge(probT_ready, a)
                        for j in range(Q_TILES):
                            mm = pe.transpose(ps[:, 6, j * P:(j + 1) * P], prob[:, a % 2, j, :],
                                              eye[:, :])
                        mm.then_inc(probT_mm, 1)
                    if 0 <= m < N_CH:
                        a = hf * N_CH + m
                        pe.wait_ge(qkv_ready, (hf + 1) * (1 + Q_TILES))
                        if a >= 2:
                            pe.wait_ge(exp_done, a - 1)
                        for j in range(Q_TILES):
                            for g in range(2):
                                rows = slice(g * HEAD_DIM, (g + 1) * HEAD_DIM)
                                mm = pe.matmul(ps[rows, 4 + a % 2, j * P:(j + 1) * P],
                                               qT[rows, j, m * CHUNK:(m + 1) * CHUNK],
                                               kT[rows, m * CHUNK:m * CHUNK + P],
                                               start=True, stop=True)
                        mm.then_inc(score_mm, 1)
                    if p > 0 or hf == 0:
                        project(hf, p)

                mb, tb, gb, cb = ub + PROJ, TL_MIX[hf], GR_MIX[hf], CH_MIX[hf]
                pe.wait_ge(proj_read, (hf + 1) * PROJ)

                def merge_down(chunk):
                    pe.wait_ge(dn_lo_done, chunk * 2 + 2)
                    pe.wait_ge(g_ready, chunk * 2 + 2)
                    for m in range(KD):
                        pe.wait_ge(dn_acc, chunk * KD + (m - 3))
                        down_tile(m, [hf], lambda h: ps[:, 4 + m % 4, :], mg_hi, mg_lo,
                                  lambda h: slice(0, HALF))

                def merge_step(i, down):
                    for s in range(2):
                        t = i * 2 + (tb + s)
                        for b in range(2):
                            slot = (3 * s + b) % 2
                            pe.wait_ge(up_lo_done, i * 6 + (mb + 3 * s + b + 1))
                            pe.wait_ge(gate_read, i * 4 + (gb + 2 * s + b - 1))
                            up_granule(None, slot, [hf], lambda h: ps[:, b, :])
                            if s == 0 and b == 0 and not down:
                                mean(1 + hf)
                        slot = (3 * s + 2) % 2
                        pe.wait_ge(up_lo_done, i * 6 + (mb + 3 * s + 3))
                        pe.wait_ge(prod_done, t)
                        if isinstance(i, int):
                            pe.wait_ge(attn_ready, (hf + 1) * N_CH)
                            pe.wait_ge(conv_ready, (hf + 1) * CONV_TILES)
                        up_granule(None, slot, [hf], lambda h: ps[:, 2, :], ks=range(0, 4),
                                   v_hi=conv_hi, v_lo=conv_lo, last=False, tokens=slice(0, HALF),
                                   end=3)
                        up_granule(None, slot, [hf], lambda h: ps[:, 3, :], ks=range(4, 8),
                                   v_hi=attn_hi, v_lo=attn_lo, tokens=slice(0, HALF),
                                   k_of=lambda k: k - 4, begin=4)
                        if s == 0 and not down:
                            for k in range(KD):
                                mean_square(1 + hf, k)
                        if s == 0 and down:
                            merge_down(i + (cb - 1))

                merge_step(0, False)
                pe.wait_ge(ln_var, 2 + hf)
                with pe.Fori(1, MIX_STEPS) as i:
                    merge_step(i, True)
                if hf == 0:
                    project(1, 0)
                    merge_down(cb + MIX_STEPS - 1)

            pe.wait_ge(up_lo_done, UPB_FFN2 + 1)
            pe.wait_ge(gate_read, GR_FFN2)
            up_granule(None, 0, [0], lambda hf: ps[:, 0, :], ready=h_ready,
                       ready_at=lambda hf, k: 4 * KD + k + 1, last=False)
            merge_down(CH_FFN2 - 1)
            pe.wait_ge(up_lo_done, UPB_FFN2 + 2)
            pe.wait_ge(prod_done, TL_FFN2)
            up_granule(None, 1, [0], lambda hf: ps[:, 2, :], ks=range(0, 4), last=False)
            pe.wait_ge(dn_acc, CH_FFN2 * KD)
            mean(3)
            up_granule(None, 1, [0], lambda hf: ps[:, 2, :], ks=range(4, KD), last=False)
            for k in range(KD):
                mean_square(3, k)

            ffn_step(0, UPB_FFN2, TL_FFN2, GR_FFN2, CH_FFN2, False, begun=True, h_from=5 * KD)
            with pe.Fori(1, FF_STEPS) as c:
                ffn_step(c, UPB_FFN2, TL_FFN2, GR_FFN2, CH_FFN2, True)
            ffn_last(CH_FFN2 + FF_STEPS - 1, KD, 4, GR_FFN2 + FF_TILES)
            mean(5)
            for k in range(KD):
                mean_square(5, k)


def tiles_of(w):
    n = w.shape[1] // P
    return w.reshape(-1, P, n, P).transpose(2, 1, 0, 3).reshape(n, P, -1)


def interleaved(*lists):
    return np.stack(lists, axis=1).reshape(-1, *lists[0].shape[1:])


def kernel(**inputs):
    import concourse.bacc as bacc
    from concourse.bass_utils import run_bass_kernel_spmd

    a = {k: np.asarray(v) for k, v in inputs.items()}
    w = {k: a[k][0] for k in a if k not in ("x", "c", "positions")}
    f32 = np.float32

    def columns(v):
        return v.reshape(-1, P).T

    pair = np.concatenate([np.arange(h * HEAD_DIM, (h + 1) * HEAD_DIM)
                           for j in range(Q_TILES) for h in (j, j + Q_TILES)])
    q_w, kv_w, conv_w3, merge_w = np.split(
        w["w_in"], [Q_HEADS * HEAD_DIM, Q_HEADS * HEAD_DIM + 2 * P,
                    Q_HEADS * HEAD_DIM + 2 * P + 3 * CONV_WIDTH], axis=1)
    gate_b, gate_c, conv_x = np.split(conv_w3, 3, axis=1)
    merge_a, merge_c = np.split(merge_w, 2, axis=1)
    branches = np.concatenate([tiles_of(w["w_branch_conv"]),
                               tiles_of(w["w_branch_attn"][pair])], axis=2)
    up_w = np.concatenate([
        interleaved(tiles_of(w["ffn1_w1"]), tiles_of(w["ffn1_w3"])),
        tiles_of(kv_w), tiles_of(q_w[:, pair]),
        interleaved(tiles_of(gate_c), tiles_of(conv_x), tiles_of(gate_b)),
        interleaved(tiles_of(merge_c), tiles_of(merge_a), branches),
        interleaved(tiles_of(w["ffn2_w1"]), tiles_of(w["ffn2_w3"]))])
    down_w = np.concatenate([w["ffn1_w2"], w["w_out"], w["ffn2_w2"]]).reshape(-1, P, D)
    w_cond = w["w_cond"].reshape(KD, P, N_COND, D).transpose(2, 0, 1, 3)
    sinks = np.repeat(w["attn_sinks"].reshape(2, Q_TILES), HEAD_DIM, axis=0)
    half = HEAD_DIM // 2
    freq = (ROPE_THETA ** (-np.arange(half) / half)).astype(f32)
    sign = np.where(np.arange(P) % HEAD_DIM < half, 1.0, -1.0)
    table = np.concatenate(
        [columns(w["b_cond"]), columns(a["c"][0])]
        + [columns(w[n]) for n in ("ln1_g", "ln1_b", "ln2_g", "ln2_b", "ln3_g", "ln3_b")]
        + [columns(w["conv_w"]), sinks, np.tile(freq, P // half)[:, None],
           sign[:, None].astype(f32), np.ones((P, 1), f32)], axis=1)
    mean_w = np.stack([np.full((P, P), 1.0 / D, f32), np.eye(P, dtype=f32)])
    arrays = {
        "x_t": a["x"][0].T.reshape(KD, P, SEQ).transpose(1, 0, 2),
        "positions": a["positions"], "table": table, "mean_w": mean_w, "w_cond": w_cond,
        "up_w": up_w, "down_w": down_w,
    }
    arrays = {n: np.ascontiguousarray(v) for n, v in arrays.items()}
    nc = bacc.Bacc("TRN2", target_bir_lowering=False, num_devices=1, dynamic_dma_scratch_size=1024)
    args = [nc.dram_tensor(n, v.shape, mybir.dt.from_np(v.dtype), kind="ExternalInput").ap()
            for n, v in arrays.items()]
    out = nc.dram_tensor("out_t", (P, KD, SEQ), F32, kind="ExternalOutput").ap()
    encoder_block(nc, *args, out)
    got = run_bass_kernel_spmd(nc, [arrays], core_ids=[0]).results[0]["out_t"]
    return got.transpose(2, 1, 0).reshape(1, SEQ, D)
```

```python
from contextlib import ExitStack

import concourse.bass as bass
from concourse import mybir
import numpy as np

F32 = mybir.dt.float32
F32R = mybir.dt.float32r
I32 = mybir.dt.int32
ALU = mybir.AluOpType
ACT = mybir.ActivationFunctionType
AX = mybir.AxisListType

P = 128
D = 1024
SEQ = 1024
HALF = SEQ // 2
KD = D // P
D_FF = 2816
FF_TILES = D_FF // P
CHUNK = 64
HEAD_DIM = 64
Q_HEADS = 8
Q_TILES = Q_HEADS * HEAD_DIM // P
CONV_WIDTH = D // 2
CONV_TILES = CONV_WIDTH // P
CONV_K = 3
N_COND = 9
ALPHA = 2.0 ** 0.25
FFN_RES = 0.5
LN_EPS = 1e-5
SCALE = HEAD_DIM ** -0.5
MASKED = -3.0e38
ROPE_THETA = 10000.0

FF_STEPS = FF_TILES // 2
UP_FFN = 2 * FF_TILES
PROJ = 2 + Q_TILES + 3 * CONV_TILES
UP_MIX = PROJ + 3 * KD
MIX_STEPS = KD // 2
HALF_STEP = 8
UPB_MIX = [UP_FFN + 4, UP_FFN + 4 + UP_MIX]
UPB_FFN2 = UP_FFN + 4 + 2 * UP_MIX
UP_TOTAL = UPB_FFN2 + UP_FFN + 8
TL_FFN = FF_TILES + 2

PC_BCOND = 0
PC_LN = PC_BCOND + N_COND * KD
PC_CONV = PC_LN + 6 * KD
PC_SINK = PC_CONV + CONV_K * CONV_TILES
PC_INV = PC_SINK + Q_TILES
PC_SIGN = PC_INV + 1
PC_ONE = PC_SIGN + 1
PC_EPS = PC_ONE + 1
PC_ALL = PC_EPS + 1

TWO_PI = 2.0 * np.pi
CW1 = 6.28125
CW2 = float(np.floor((TWO_PI - CW1) * 2.0 ** 19) / 2.0 ** 19)
CW3 = float(np.float32(TWO_PI - CW1 - CW2))
ROUND = float(1.5 * 2.0 ** 23)
PI_BELOW = float(np.nextafter(np.float32(np.pi), np.float32(0)))


def encoder_block(nc, x, c_row, pos, table, mean_w, w_cond, up_w, down_w, out):
    with ExitStack() as ctx:
        def sem(name):
            return ctx.enter_context(nc.semaphore(name))

        at = [nc.sbuf_base + (-nc.sbuf_base) % 32]

        def place(name, shape, dt=F32, offset=None):
            size = 4 * int(np.prod(shape[1:]))
            if offset is None:
                offset = at[0]
                at[0] = offset + size + (-size) % 32
            end = offset + size + (-size) % 32
            return nc.alloc_sbuf_tensor_at(name, shape, dt, offset=offset), end

        res, _ = place("res", [P, KD, SEQ])
        h_hi, _ = place("h_hi", [P, KD, SEQ], F32R)
        h_lo, _ = place("h_lo", [P, KD, SEQ], F32R)
        up_raw, _ = place("up_raw", [P, 2, KD, P])
        up_hi, _ = place("up_hi", [P, 2, KD, P], F32R)
        up_lo, _ = place("up_lo", [P, 2, KD, P], F32R)
        dn_raw, _ = place("dn_raw", [P, 2, D])
        dn_hi, _ = place("dn_hi", [P, 2, D], F32R)
        dn_lo, _ = place("dn_lo", [P, 2, D], F32R)
        tmp, _ = place("tmp", [P, 4, HALF])
        cos_t, _ = place("cos_t", [P, SEQ])
        sin_t, _ = place("sin_t", [P, SEQ])
        mean_m, _ = place("mean_m", [P, P])
        eye, _ = place("eye", [P, P])
        par, _ = place("par", [P, PC_ALL])
        mod, _ = place("mod", [P, N_COND, KD])
        coef, _ = place("coef", [P, 16, KD])
        negsink, _ = place("negsink", [P, Q_TILES])
        small, _ = place("small", [P, 2, 6, Q_TILES])
        root_warm, _ = place("root_warm", [P, 1])
        ucarry, _ = place("ucarry", [P, CONV_TILES, CONV_K - 1])
        shared = at[0]
        g_hi, o = place("g_hi", [P, 2, SEQ], F32R, shared)
        g_lo, o = place("g_lo", [P, 2, SEQ], F32R, o)
        crow, o = place("crow", [P, 4, D], F32, o)
        silu_c, o = place("silu_c", [P, D], F32, o)
        pos_i, o = place("pos_i", [P, SEQ], I32, o)
        ang, o = place("ang", [P, SEQ], F32, o)
        turn, o = place("turn", [P, SEQ], F32, o)
        turns, o = place("turns", [P, SEQ], F32, o)
        attn_hi, o = place("attn_hi", [P, Q_TILES, HALF], F32R, shared)
        attn_lo, o = place("attn_lo", [P, Q_TILES, HALF], F32R, o)
        conv_hi, o = place("conv_hi", [P, CONV_TILES, HALF], F32R, o)
        conv_lo, o = place("conv_lo", [P, CONV_TILES, HALF], F32R, o)
        q_at = o
        qT, o = place("qT", [P, Q_TILES, HALF], F32, q_at)
        mg_hi, o2 = place("mg_hi", [P, 2, HALF], F32R, q_at)
        mg_lo, _ = place("mg_lo", [P, 2, HALF], F32R, o2)
        kT, o = place("kT", [P, CHUNK + HALF], F32, o)
        vT, o = place("vT", [P, CHUNK + HALF], F32, o)
        ln_at = o
        vband, o = place("vband", [P, HALF // CHUNK, P], F32, o)
        ubuf, o = place("ubuf", [P, CONV_K - 1 + HALF], F32, o)
        prob, o = place("prob", [P, 2, Q_TILES, P], F32, o)
        probT, o = place("probT", [P, 2, Q_TILES, P], F32, o)
        o2 = ln_at
        presum, o2 = place("presum", [P, 2, HALF], F32, o2)
        rstd, o2 = place("rstd", [P, HALF], F32, o2)
        ln_tmp, o2 = place("ln_tmp", [P, 4, HALF], F32, o2)
        assert max(o, o2) <= nc.sbuf_usable_end

        ps = ctx.enter_context(nc.psum_tensor("ps", [P, 8, 512], F32))

        (C_SH0, C_SC0, C_H1S, C_H1B, C_R1S, C_R1B, C_H2S, C_H2B, C_R2S, C_R2B, C_G1, C_G3, C_ONE2,
         C_ONE3, C_BASE, _) = range(16)

        tables_in = sem("tables_in")
        pos_in = sem("pos_in")
        c_in = sem("c_in")
        x_in = [sem(f"x_in{i}") for i in range(4)]
        up_in = [sem("up_in0"), sem("up_in1")]
        dn_in = [sem("dn_in0"), sem("dn_in1")]
        crow_in = [sem(f"crow_in{i}") for i in range(4)]
        up_hi_done = sem("up_hi_done")
        up_lo_done = sem("up_lo_done")
        dn_hi_done = sem("dn_hi_done")
        dn_lo_done = sem("dn_lo_done")
        up_mm = sem("up_mm")
        dn_mm = sem("dn_mm")
        dn_acc = sem("dn_acc")
        gate_read = sem("gate_read")
        prod_done = sem("prod_done")
        g_hi_done = sem("g_hi_done")
        g_ready = sem("g_ready")
        cs_ready = sem("cs_ready")
        crow_used = sem("crow_used")
        mod_ready = sem("mod_ready")
        coef_done = sem("coef_done")
        rope_steps = sem("rope_steps")
        trig_done = sem("trig_done")
        sin_ready = sem("sin_ready")
        ln_sum = sem("ln_sum")
        ln_mean = sem("ln_mean")
        ln_centred = sem("ln_centred")
        ln_sq = sem("ln_sq")
        ln_sqadd = sem("ln_sqadd")
        ln_sqmm = sem("ln_sqmm")
        ln_std = sem("ln_std")
        ln_rstd_part = sem("ln_rstd_part")
        ln_rstd = sem("ln_rstd")
        pre_h = sem("pre_h")
        hhi_done = sem("hhi_done")
        h_ready = sem("h_ready")
        half_mm = sem("half_mm")
        half_acc = sem("half_acc")
        ln_part = sem("ln_part")
        ln_normed = sem("ln_normed")
        ln_scaled = sem("ln_scaled")
        r_alpha = sem("r_alpha")
        ln_pair = sem("ln_pair")
        r_scaled = sem("r_scaled")
        proj_read = sem("proj_read")
        dve_step = sem("dve_step")
        qkv_ready = sem("qkv_ready")
        carried = sem("carried")
        vband_mm = sem("vband_mm")
        vband_ready = sem("vband_ready")
        score_mm = sem("score_mm")
        negmax_done = sem("negmax_done")
        exp_done = sem("exp_done")
        probs_ready = sem("probs_ready")
        probT_mm = sem("probT_mm")
        probT_ready = sem("probT_ready")
        av_mm = sem("av_mm")
        attn_hi_done = sem("attn_hi_done")
        attn_ready = sem("attn_ready")
        conv_done = sem("conv_done")
        conv_hi_done = sem("conv_hi_done")
        conv_ready = sem("conv_ready")
        merge_parts = sem("merge_parts")
        y_ready = sem("y_ready")
        stored = sem("stored")

        DNB_MIX = [FF_TILES, FF_TILES + KD]
        DNB_FFN2 = FF_TILES + 2 * KD
        TL_MIX = [TL_FFN, TL_FFN + KD]
        TL_FFN2 = TL_FFN + 2 * KD
        GR_MIX = [TL_FFN, TL_FFN + 2 * KD]
        GR_FFN2 = TL_FFN + 4 * KD
        CH_MIX = [FF_STEPS, FF_STEPS + MIX_STEPS]
        CH_FFN2 = FF_STEPS + 2 * MIX_STEPS
        N_CH = HALF // CHUNK
        ATT_FIRST, LAG_T, LAG_V = 3 + Q_TILES, 2, 3
        assert ATT_FIRST + HALF // CHUNK - 1 + LAG_V < PROJ
        SQ_MM = np.cumsum([0, 1, 1, 1, 1, 1, KD - 1]).tolist()
        LN_BANKS = [(2, 3), (6, 7), (6, 7), (2, 3), (2, 3), (2, 3)]
        LAST_BANKS = (4, 5, 6, 7, 0, 1)
        LEAD = 5
        PAIR_ORDER = [(0, k) for k in range(LEAD)]
        for k in range(KD):
            PAIR_ORDER += [(1, k)] + ([(0, k + LEAD)] if k + LEAD < KD else [])

        def inv_row(i):
            return tmp[:, 3, :] if i == 5 else rstd[:, :]

        def halves(hf):
            return slice(hf * HALF, (hf + 1) * HALF)

        block = ctx.enter_context(nc.Block())

        @block.sync
        def _(sp):
            def load_up(u, slot, src):
                if not isinstance(u, int) or u >= 2:
                    sp.wait_ge(up_lo_done, u - 1)
                sp.dma_start(up_raw[:, slot, :, :].rearrange("p k f -> p (k f)"),
                             up_w[bass.ds(src, 1), :, :].rearrange("a p n -> (a p) n"))\
                    .then_inc(up_in[slot], 16)

            def load_down(d, slot, src):
                if not isinstance(d, int) or d >= 2:
                    sp.wait_ge(dn_lo_done, d - 1)
                sp.dma_start(dn_raw[:, slot, :],
                             down_w[bass.ds(src, 1), :, :].rearrange("a p n -> (a p) n"))\
                    .then_inc(dn_in[slot], 16)

            def load_cond(n, slot, v, k):
                if not isinstance(n, int) or n >= 4:
                    sp.wait_ge(crow_used, n - 3)
                sp.dma_start(crow[:, slot, :],
                             w_cond[bass.ds(v, 1), k, :, :].rearrange("a p n -> (a p) n"))\
                    .then_inc(crow_in[slot], 16)

            sp.dma_start(par[:, :], table).then_inc(tables_in, 16)
            sp.dma_start(silu_c[:, :], c_row.to_broadcast([P, D])).then_inc(c_in, 16)
            load_up(0, 0, 0)
            for k in range(KD):
                load_cond(2 * k, 2 * k % 4, 1, k)
                load_cond(2 * k + 1, (2 * k + 1) % 4, 0, k)
                sp.dma_start(res[:, k, :], x[:, k, :]).then_inc(x_in[k % 4], 16)
                if k == 1:
                    load_up(1, 1, 1)
            sp.dma_start(mean_m[:, :], mean_w[0]).then_inc(tables_in, 16)
            sp.dma_start(eye[:, :], mean_w[1]).then_inc(tables_in, 16)
            sp.dma_start(pos_i[:, :], pos.to_broadcast([P, SEQ])).then_inc(pos_in, 16)

            def ffn_step(c, ub, sb, db, dsb, cond=False, first=False):
                if not first:
                    load_up(c * 4 + ub, 0, c * 4 + sb)
                    load_up(c * 4 + (ub + 1), 1, c * 4 + (sb + 1))
                for s in range(2):
                    load_down(c * 2 + (db + s), s, c * 2 + (dsb + s))
                for s in range(2):
                    if cond:
                        for k in range(4 * s, 4 * s + 4):
                            load_cond(c * KD + (KD + k), k % 4, c + 1, k)
                    load_up(c * 4 + (ub + 2 + s), s, c * 4 + (sb + 2 + s))

            def half_step(u, src, down, down_src):
                for n in range(HALF_STEP):
                    load_up(u + n, n % 2, src + n % 4)
                    if n == 1:
                        for s in range(2):
                            load_down(down + s, s, down_src + s)

            LAST = FF_STEPS - 1
            ffn_step(0, 0, 0, 0, 0, first=True)
            with sp.Fori(1, N_COND - 1) as c:
                ffn_step(c, 0, 0, 0, 0, cond=True)
            with sp.Fori(N_COND - 1, LAST) as c:
                ffn_step(c, 0, 0, 0, 0)
            half_step(4 * LAST, 4 * LAST, 2 * LAST, 2 * LAST)
            for hf in range(2):
                ub, db = UPB_MIX[hf], DNB_MIX[hf]
                with sp.Fori(0, PROJ // 2) as i:
                    for s in range(2):
                        load_up(i * 2 + (ub + s), s, i * 2 + (UP_FFN + s))
                with sp.Fori(0, MIX_STEPS) as i:
                    for s in range(6):
                        load_up(i * 6 + (ub + PROJ + s), s % 2, i * 6 + (UP_FFN + PROJ + s))
                        if s == 1:
                            for d in range(2):
                                load_down(i * 2 + (db + d), d, i * 2 + (FF_TILES + d))
            src, down_src = UP_FFN + UP_MIX, FF_TILES + KD
            half_step(UPB_FFN2, src, DNB_FFN2, down_src)
            with sp.Fori(1, LAST) as c:
                ffn_step(c, UPB_FFN2 + 4, src, DNB_FFN2, down_src)
            half_step(UPB_FFN2 + 4 + 4 * LAST, src + 4 * LAST, DNB_FFN2 + 2 * LAST,
                      down_src + 2 * LAST)
            for hf in range(2):
                for k in range(KD):
                    sp.wait_ge(y_ready, hf * KD + k + 1)
                    sp.dma_start(out[:, k, halves(hf)], res[:, k, halves(hf)]).then_inc(stored, 16)
            sp.wait_ge(stored, 16 * 2 * KD)

        @block.gpsimd
        def _(pool):
            def split_one(u):
                pool.wait_ge(up_hi_done, u + 1)
                pool.tensor_tensor(up_lo[:, u % 2, :, :], up_raw[:, u % 2, :, :],
                                   up_hi[:, u % 2, :, :].bitcast(F32), ALU.subtract)\
                    .then_inc(up_lo_done, 1)

            def split_ups(begin, end):
                with pool.Fori(begin // 2, end // 2) as i:
                    for s in range(2):
                        pool.wait_ge(up_hi_done, i * 2 + (s + 1))
                        pool.tensor_tensor(up_lo[:, s, :, :], up_raw[:, s, :, :],
                                           up_hi[:, s, :, :].bitcast(F32), ALU.subtract)\
                            .then_inc(up_lo_done, 1)

            parts = 0

            def sum_tiles(i, acc, before, tiles=KD, beside=None, dst=None):
                nonlocal parts
                r, dst = res[:, :, halves(i % 2)], presum[:, i % 2, :] if dst is None else dst
                for k in range(1, tiles):
                    if beside is not None:
                        split_one(beside + k - 1)
                    pool.wait_ge(acc, before + k + 1)
                    if k > 1:
                        pool.wait_ge(ln_part, parts)
                    ins = pool.tensor_tensor(dst, r[:, 0, :] if k == 1 else dst, r[:, k, :],
                                             ALU.add)
                    ins.then_inc(ln_sum if k == tiles - 1 else ln_part, 1)
                    parts += k < tiles - 1

            def normalise(i):
                r = res[:, :, halves(i % 2)]
                if i == 4:
                    pool.wait_ge(ln_rstd_part, 1)
                pool.wait_ge(ln_rstd, i + 1)
                for k in range(KD):
                    pool.tensor_tensor(r[:, k, :], r[:, k, :], rstd[:, :], ALU.mult)\
                        .then_inc(ln_normed, 1)

            split_one(0)
            split_one(1)
            for k in range(KD):
                pool.wait_ge(pre_h, 2 * k + 1)
                r = res[:, k, 0:HALF]
                pool.tensor_scalar(r, r, ALPHA, None, ALU.mult).then_inc(r_alpha, 1)
            split_ups(2, UPB_MIX[0])
            sum_tiles(0, half_acc, 0)
            split_one(UPB_MIX[0])
            split_one(UPB_MIX[0] + 1)
            normalise(0)
            split_ups(UPB_MIX[0] + 2, UPB_MIX[0] + 6)
            for i, ub, chunks in ((1, UPB_MIX[0], CH_MIX[0]), (2, UPB_MIX[1], CH_MIX[1])):
                sum_tiles(i, dn_acc, chunks * KD - KD, beside=ub + 6, dst=tmp[:, 3, :])
                split_one(ub + 6 + KD - 1)
                split_ups(ub + 6 + KD, (UPB_MIX[1] + 6, UPB_FFN2 + 2)[i - 1])
            split_one(UPB_FFN2 + 2)
            sum_tiles(3, dn_acc, (CH_FFN2 - 1) * KD)
            split_one(UPB_FFN2 + 3)
            split_one(UPB_FFN2 + 4)
            normalise(3)
            split_one(UPB_FFN2 + 5)
            split_ups(UPB_FFN2 + 6, UP_TOTAL)
            sum_tiles(4, half_acc, 2 * KD)
            sum_tiles(5, dn_acc, (CH_FFN2 + FF_STEPS - 1) * KD, KD // 2)
            normalise(4)

        @block.scalar
        def _(act):
            def split_up(u, slot, turn_of):
                act.wait_ge(up_in[slot], turn_of * 16 + 16)
                if not isinstance(u, int) or u >= 2:
                    act.wait_ge(up_mm, u - 1)
                act.activation(up_hi[:, slot, :, :], up_raw[:, slot, :, :], ACT.Copy)\
                    .then_inc(up_hi_done, 1)

            def split_down(chunk):
                for s in range(2):
                    act.wait_ge(dn_in[s], chunk * 16 + 16)
                    if not isinstance(chunk, int) or chunk >= 1:
                        act.wait_ge(dn_mm, chunk * KD)
                    act.activation(dn_hi[:, s, :], dn_raw[:, s, :], ACT.Copy)\
                        .then_inc(dn_hi_done, 1)

            def high_h(i, ks):
                for k in ks:
                    act.wait_ge(pre_h, i * KD + k + 1)
                    act.activation(h_hi[:, k, halves(i % 2)], ln_tmp[:, k % 4, :], ACT.Copy)\
                        .then_inc(hhi_done, 1)

            def first_high_h(k):
                act.wait_ge(x_in[k % 4], 16 * (k // 4) + 16)
                act.wait_ge(coef_done, 3 + k)
                for hf in range(2):
                    n = 2 * k + hf
                    if n >= 4:
                        act.wait_ge(h_ready, n - 3)
                    act.activation(ln_tmp[:, n % 4, :], res[:, k, halves(hf)], ACT.Identity,
                                   bias=coef[:, C_SH0, k:k + 1], scale=coef[:, C_SC0, k:k + 1])\
                        .then_inc(pre_h, 1)
                for hf in range(2):
                    n = 2 * k + hf
                    act.wait_ge(pre_h, n + 1)
                    act.activation(h_hi[:, k, halves(hf)], ln_tmp[:, n % 4, :], ACT.Copy)\
                        .then_inc(hhi_done, 1)

            def ln_high_h(i, ks, scale, bias):
                for k in ks:
                    act.wait_ge(ln_normed, i * KD + k + 1)
                    if k < 4:
                        act.wait_ge(h_ready, (i + 2) * KD)
                    else:
                        act.wait_ge(h_ready, (i + 2) * KD + k - 3)
                    act.activation(ln_tmp[:, k % 4, :], res[:, k, halves(i % 2)], ACT.Identity,
                                   bias=bias[:, k:k + 1], scale=scale[:, k:k + 1])\
                        .then_inc(pre_h, 1)
                    if k > ks[0]:
                        high_h(i + 2, [k - 1])
                high_h(i + 2, [ks[-1]])

            def squares(i, ks=range(KD)):
                for k in ks:
                    act.wait_ge(ln_centred, i * KD + k + 1)
                    if k >= 4 and i == 5:
                        act.wait_ge(ln_sqmm, SQ_MM[i] + k - 3)
                    elif k >= 4:
                        act.wait_ge(ln_sqadd, i * (KD - 1) + max(k - 4, 1))
                    act.activation(ln_tmp[:, k % 4, :], res[:, k, halves(i % 2)], ACT.Square)\
                        .then_inc(ln_sq, 1)

            def root(i):
                act.wait_ge(ln_sqmm, SQ_MM[i + 1])
                act.activation(inv_row(i), ps[:, LN_BANKS[i][1], :], ACT.Sqrt,
                               bias=par[:, PC_EPS:PC_EPS + 1]).then_inc(ln_std, 1)

            def load_root_table():
                act.activation(root_warm[:, :], par[:, PC_ONE:PC_ONE + 1], ACT.Sqrt)


            def gate_tile(t, s, chunk, down, src_done, dst):
                act.wait_ge(prod_done, t + 1)
                if down and s == 0:
                    act.wait_ge(dn_mm, chunk * KD)
                act.activation(dst, src_done, ACT.Copy).then_inc(g_hi_done, 1)

            def ffn_step(c, ub, tb, cb, down):
                for s in range(2):
                    t = c * 2 + (tb + s)
                    split_up(c * 4 + (ub + 2 + 2 * s), 0, c * 2 + (ub // 2 + 1 + s))
                    if not isinstance(t, int) or t >= 1:
                        act.wait_ge(prod_done, t)
                    act.wait_ge(up_mm, c * 4 + (ub + 1 + 2 * s))
                    act.activation(tmp[:, 0:2, :], ps[:, 0:2, :], ACT.Silu).then_inc(gate_read, 1)
                    if s == 0:
                        split_up(c * 4 + (ub + 3), 1, c * 2 + (ub // 2 + 1))
                    gate_tile(t, s, c + cb, down, tmp[:, 2:4, :],
                              g_hi[:, s, :].rearrange("p (a t) -> p a t", a=2))
                    if s == 0:
                        split_down(c + cb)
                split_up(c * 4 + (ub + 5), 1, c * 2 + (ub // 2 + 2))

            def half_silu(u, t):
                act.wait_ge(prod_done, t)
                act.wait_ge(up_mm, u + 1)
                act.activation(tmp[:, 0, :], ps[:, 0, :], ACT.Silu).then_inc(gate_read, 1)

            def half_gate(n, t, chunk, down=True):
                gate_tile(t, n, chunk, down, tmp[:, 2, :], g_hi[:, n % 2, halves(n // 2)])

            def split(u):
                split_up(u, u % 2, u // 2)

            def last_step(u, t, chunk, i, more):
                for n in range(3):
                    split(u + 2 * n + 2)
                    half_silu(u + 2 * n, t + n)
                    split(u + 2 * n + 3)
                    half_gate(n, t + n, chunk)
                    if n == 0:
                        split_down(chunk)
                squares(i)
                half_silu(u + 6, t + 3)
                load_root_table()
                if more:
                    split(u + 8)
                half_gate(3, t + 3, chunk)
                root(i)
                if more:
                    split(u + 9)

            act.wait_ge(c_in, 16)
            act.activation(silu_c[:, :], silu_c[:, :], ACT.Silu).then_inc(cs_ready, 1)
            split_up(0, 0, 0)
            first_high_h(0)
            split_up(1, 1, 0)
            for k in range(1, KD):
                first_high_h(k)
            act.wait_ge(tables_in, 48)

            ffn_step(0, 0, 0, 0, False)
            ffn_step(1, 0, 0, 0, True)
            act.wait_ge(rope_steps, 9)
            act.activation(cos_t[:, :], turn[:, :], ACT.Sin).then_inc(trig_done, 1)
            ffn_step(2, 0, 0, 0, True)
            act.wait_ge(rope_steps, 15)
            act.activation(sin_t[:, :], ang[:, :], ACT.Sin).then_inc(trig_done, 1)
            LAST = FF_STEPS - 1
            with act.Fori(3, LAST) as c:
                ffn_step(c, 0, 0, 0, True)
            last_step(4 * LAST, 2 * LAST, LAST, 0, True)
            ln_high_h(0, range(KD), coef[:, C_H1S, :], coef[:, C_H1B, :])

            for hf in range(2):
                ub = UPB_MIX[hf]
                for p in range(PROJ):
                    u = ub + p
                    if p > 0:
                        split_up(u + 1, (u + 1) % 2, (u + 1) // 2)
                    m = p - ATT_FIRST
                    if 0 <= m - LAG_V < N_CH:
                        v = m - LAG_V
                        act.wait_ge(av_mm, hf * N_CH + v + 1)
                        act.activation(
                            attn_hi[:, :, v * CHUNK:(v + 1) * CHUNK],
                            ps[:, 7, 0:Q_TILES * CHUNK].rearrange("p (j t) -> p j t", j=Q_TILES),
                            ACT.Copy).then_inc(attn_hi_done, 1)
                    if 0 <= m - LAG_T < N_CH:
                        a = hf * N_CH + m - LAG_T
                        act.wait_ge(probT_mm, a + 1)
                        if a >= 2:
                            act.wait_ge(av_mm, a - 1)
                        act.activation(probT[:, a % 2, :, :],
                                       ps[:, 6, :].rearrange("p (j t) -> p j t", j=Q_TILES),
                                       ACT.Copy).then_inc(probT_ready, 1)
                    if 0 <= m < N_CH:
                        a = hf * N_CH + m
                        if a >= 2:
                            act.wait_ge(probT_mm, a - 1)
                        act.wait_ge(negmax_done, a + 1)
                        for j in range(Q_TILES):
                            act.activation(prob[:, a % 2, j, :], ps[:, 4 + a % 2, j * P:(j + 1) * P],
                                           ACT.Exp, bias=small[:, a % 2, 1, j:j + 1], scale=SCALE,
                                           accum_out=small[:, a % 2, 3, j:j + 1])
                        act.activation(small[:, a % 2, 4, :], small[:, a % 2, 2, :], ACT.Exp)\
                            .then_inc(exp_done, 1)
                    if p >= 9 and p % 3 == 0:
                        i = p // 3 - 3
                        act.wait_ge(conv_done, hf * CONV_TILES + i + 1)
                        act.activation(conv_hi[:, i, :], tmp[:, 2, :], ACT.Copy)\
                            .then_inc(conv_hi_done, 1)
                act.wait_ge(conv_done, (hf + 1) * CONV_TILES)
                act.activation(conv_hi[:, CONV_TILES - 1, :], tmp[:, 2, :], ACT.Copy)\
                    .then_inc(conv_hi_done, 1)
                act.wait_ge(conv_ready, (hf + 1) * CONV_TILES)

                mb, tb, cb = ub + PROJ, TL_MIX[hf], CH_MIX[hf]
                ln = 1 + hf

                def mix_split(i, n):
                    split_up(i * 6 + (mb + n), n % 2, i * 3 + (mb + n) // 2)

                def sigmoid(i, s, b):
                    if b == 0:
                        act.wait_ge(prod_done, i * 2 + (tb + s))
                    act.wait_ge(up_mm, i * 6 + (mb + 3 * s + b + 1))
                    act.activation(tmp[:, b, :], ps[:, b, :], ACT.Sigmoid).then_inc(gate_read, 1)

                def merge_step(i, more=True):
                    sigmoid(i, 0, 0)
                    sigmoid(i, 0, 1)
                    mix_split(i, 3)
                    mix_split(i, 4)
                    gate_tile(i * 2 + tb, 0, i + cb, True, tmp[:, 2, :], mg_hi[:, 0, :])
                    split_down(i + cb)
                    sigmoid(i, 1, 0)
                    mix_split(i, 5)
                    sigmoid(i, 1, 1)
                    mix_split(i, 6)
                    mix_split(i, 7)
                    gate_tile(i * 2 + (tb + 1), 1, i + cb, True, tmp[:, 2, :], mg_hi[:, 1, :])
                    if more:
                        mix_split(i, 8)

                def first_merge_step():
                    sb = [coef[:, c, :] for c in ((C_H1S, C_H1B), (C_H2S, C_H2B))[hf]]
                    squares(ln, range(0, 4))
                    sigmoid(0, 0, 0)
                    mix_split(0, 2)
                    squares(ln, range(4, KD))
                    sigmoid(0, 0, 1)
                    mix_split(0, 3)
                    root(ln)
                    mix_split(0, 4)
                    gate_tile(tb, 0, cb, False, tmp[:, 2, :], mg_hi[:, 0, :])
                    ln_high_h(ln, range(0, 2), *sb)
                    mix_split(0, 5)
                    split_down(cb)
                    sigmoid(0, 1, 0)
                    mix_split(0, 6)
                    sigmoid(0, 1, 1)
                    ln_high_h(ln, range(2, 5), *sb)
                    mix_split(0, 7)
                    gate_tile(tb + 1, 1, cb, False, tmp[:, 2, :], mg_hi[:, 1, :])
                    ln_high_h(ln, range(5, 6), *sb)
                    mix_split(0, 8)
                    ln_high_h(ln, range(6, KD), *sb)

                mix_split(0, 1)
                first_merge_step()
                with act.Fori(1, MIX_STEPS - 1) as i:
                    merge_step(i)
                merge_step(MIX_STEPS - 1, more=False)

            u, t = UPB_FFN2, TL_FFN2
            split(u + 2)
            half_silu(u, t)
            squares(3, range(0, 4))
            split(u + 3)
            squares(3, range(4, KD))
            half_gate(0, t, CH_FFN2, False)
            split_down(CH_FFN2)
            load_root_table()
            root(3)
            split(u + 4)
            half_silu(u + 2, t + 1)
            split(u + 5)
            half_gate(1, t + 1, CH_FFN2, False)
            ln_high_h(3, range(KD), coef[:, C_H2S, :], coef[:, C_H2B, :])
            for n in range(2, 4):
                split(u + 2 * n + 2)
                half_silu(u + 2 * n, t + n)
                split(u + 2 * n + 3)
                half_gate(n, t + n, CH_FFN2, False)
            with act.Fori(1, LAST) as c:
                ffn_step(c, UPB_FFN2 + 4, TL_FFN2 + 2, CH_FFN2, True)
            last_step(UPB_FFN2 + 4 + 4 * LAST, TL_FFN2 + 2 + 2 * LAST, CH_FFN2 + LAST, 4, False)

            def store_tile(i, k):
                r = res[:, k, halves(i % 2)]
                b = PC_LN + 5 * KD + k
                if i == 4:
                    act.wait_ge(ln_normed, 2 * KD + 2 * KD + k + 1)
                    act.activation(r, r, ACT.Identity, bias=par[:, b:b + 1],
                                   scale=par[:, b - KD:b - KD + 1]).then_inc(y_ready, 1)
                else:
                    act.wait_ge(ln_scaled, k + 1)
                    act.activation(r, r, ACT.Identity, bias=par[:, b:b + 1]).then_inc(y_ready, 1)

            squares(5)
            for k in range(0, 3):
                store_tile(4, k)
            root(5)
            for k in range(3, KD):
                store_tile(4, k)
            for k in range(KD):
                store_tile(5, k)

        @block.vector
        def _(dve):
            def split_down(chunk):
                for s in range(2):
                    dve.wait_ge(dn_hi_done, chunk * 2 + (s + 1))
                    dve.tensor_tensor(dn_lo[:, s, :], dn_raw[:, s, :], dn_hi[:, s, :].bitcast(F32),
                                      ALU.subtract).then_inc(dn_lo_done, 1)

            def cond_block(slot, turn_of, v, k):
                dve.wait_ge(crow_in[slot], turn_of * 16 + 16)
                dve.scalar_tensor_tensor(
                    out=crow[:, slot, :], in0=crow[:, slot, :], scalar=1.0, in1=silu_c[:, :],
                    op0=ALU.mult, op1=ALU.mult,
                    accum_out=mod[:, bass.ds(v, 1), k:k + 1].rearrange("p a k -> p (a k)"))\
                    .then_inc(crow_used, 1)

            def cond_vector(v):
                for k in range(KD):
                    cond_block(k % 4, v * 2 + k // 4, v, k)
                dve.wait_ge(crow_used, v * KD + KD)
                row = mod[:, bass.ds(v, 1), :].rearrange("p a k -> p (a k)")
                dve.tensor_tensor(row, row, par[:, bass.ds(v * KD + PC_BCOND, KD)], ALU.add)\
                    .then_inc(mod_ready, 1)

            def first_low(k):
                for n in (2 * k, 2 * k + 1):
                    dve.wait_ge(hhi_done, n + 1)
                    at = halves(n % 2)
                    dve.tensor_tensor(h_lo[:, k, at], ln_tmp[:, n % 4, :],
                                      h_hi[:, k, at].bitcast(F32), ALU.subtract)\
                        .then_inc(h_ready, 1)

            def low_h(i, k):
                return dve.tensor_tensor(h_lo[:, k, halves(i % 2)], ln_tmp[:, k % 4, :],
                                         h_hi[:, k, halves(i % 2)].bitcast(F32), ALU.subtract)

            def ln_low_h(i, k):
                dve.wait_ge(hhi_done, (i + 2) * KD + k + 1)
                low_h(i, k).then_inc(h_ready, 1)

            def ln_input(i, begin, end):
                for k in range(begin, end):
                    if k < KD:
                        r = res[:, k, halves(i % 2)]
                        dve.tensor_tensor(r, r, rstd[:, :], ALU.mult).then_inc(ln_normed, 1)
                    if k >= 2:
                        ln_low_h(i, k - 2)

            def scale_residual(i, scale, bias):
                for k in range(KD):
                    r = res[:, k, halves(i % 2)]
                    dve.wait_ge(pre_h, (i + 2) * KD + k + 1)
                    dve.tensor_scalar(r, r, scale[:, k:k + 1], bias[:, k:k + 1], ALU.mult,
                                      ALU.add).then_inc(r_scaled, 1)

            def centre(i, k):
                r = res[:, k, halves(i % 2)]
                if k == 0:
                    dve.wait_ge(ln_mean, i + 1)
                dve.tensor_tensor(r, r, ps[:, LN_BANKS[i][0], :], ALU.subtract)\
                    .then_inc(ln_centred, 1)

            def add_square(i, k):
                dve.wait_ge(ln_sq, i * KD + k + 1)
                if k > 1:
                    dve.wait_ge(ln_sqadd, i * (KD - 1) + k - 1)
                dst = presum[:, 1 - i % 2, :]
                dve.tensor_tensor(dst, ln_tmp[:, 0, :] if k == 1 else dst, ln_tmp[:, k % 4, :],
                                  ALU.add).then_inc(ln_sqadd, 1)

            def centre_and_square(i, begin, end):
                for k in range(begin, end):
                    if k < KD:
                        centre(i, k)
                    if k >= 3:
                        add_square(i, k - 2)

            def inverse(i, part=None):
                if not part:
                    dve.wait_ge(ln_std, i + 1)
                n = HALF if part is None else HALF // 2
                at = slice((part or 0) * n, (part or 0) * n + n)
                dve.reciprocal(inv_row(i)[:, at], inv_row(i)[:, at]).then_inc(ln_rstd_part if part == 0
                                                                  else ln_rstd, 1)

            def ffn_step(c, tb, gb, ub, cb, gate, down, cond=False):
                if cond:
                    cond_vector(c + 1)
                    dve.wait_ge(mod_ready, c)
                    dve.tensor_scalar(coef[:, C_G1, :], mod[:, 2, :], FFN_RES, None, ALU.mult)\
                        .then_inc(coef_done, 1)
                    dve.wait_ge(coef_done, c + (2 + KD))
                for s in range(2):
                    t = c * 2 + (tb + s)
                    dve.wait_ge(gate_read, c * 2 + (gb + s + 1))
                    dve.wait_ge(up_mm, c * 4 + (ub + 2 + 2 * s))
                    if not isinstance(t, int) or t >= 1:
                        dve.wait_ge(g_ready, t)
                    dve.tensor_tensor(tmp[:, 2:4, :], tmp[:, 0:2, :], ps[:, 2:4, :], ALU.mult)\
                        .then_inc(prod_done, 1)
                    if down and s == 0:
                        if down == "half":
                            for m in range(KD):
                                add_half(m, 1, 4 + m % 4, dn_mm, (c + (cb - 1)) * KD, gate, dn_acc)
                        else:
                            add_down(c + (cb - 1), gate)
                    dve.wait_ge(g_hi_done, t + 1)
                    dve.tensor_tensor(g_lo[:, s, :].rearrange("p (a t) -> p a t", a=2),
                                      tmp[:, 2:4, :],
                                      g_hi[:, s, :].bitcast(F32).rearrange("p (a t) -> p a t", a=2),
                                      ALU.subtract).then_inc(g_ready, 1)
                    if s == 0:
                        split_down(c + cb)

            def half_product(u, t, g):
                dve.wait_ge(gate_read, g + 1)
                dve.wait_ge(up_mm, u + 2)
                dve.wait_ge(g_ready, t)
                dve.tensor_tensor(tmp[:, 2, :], tmp[:, 0, :], ps[:, 1, :], ALU.mult)\
                    .then_inc(prod_done, 1)

            def half_low(n, t):
                dve.wait_ge(g_hi_done, t + 1)
                at = halves(n // 2)
                dve.tensor_tensor(g_lo[:, n % 2, at], tmp[:, 2, :],
                                  g_hi[:, n % 2, at].bitcast(F32), ALU.subtract)\
                    .then_inc(g_ready, 1)

            def add_down(chunk, gate):
                for m in range(KD):
                    dve.wait_ge(dn_mm, chunk * KD + (m + 1))
                    r = res[:, m, :].rearrange("p (a t) -> p a t", a=2)
                    b = 4 + 2 * (m % 2)
                    dve.scalar_tensor_tensor(out=r, in0=ps[:, b:b + 2, :], scalar=gate[:, m:m + 1],
                                             in1=r, op0=ALU.mult, op1=ALU.add).then_inc(dn_acc, 1)

            def add_half(m, hf, bank, mm, before, gate, acc):
                dve.wait_ge(mm, before + m + 1)
                r = res[:, m, halves(hf)]
                dve.scalar_tensor_tensor(out=r, in0=ps[:, bank, :], scalar=gate[:, m:m + 1], in1=r,
                                         op0=ALU.mult, op1=ALU.add).then_inc(acc, 1)

            def last_step(u, t, g, chunk, gate, halves_before, i, low):
                half_product(u, t, g)
                add_down(chunk - 1, gate)
                half_low(0, t)
                split_down(chunk)
                for n in range(1, 3):
                    half_product(u + 2 * n, t + n, g + n)
                    half_low(n, t + n)
                for m in range(KD):
                    add_half(m, 0, 4 + m % 4, half_mm, halves_before, gate, half_acc)
                centre_and_square(i, 0, KD + 2)
                half_product(u + 6, t + 3, g + 3)
                half_low(3, t + 3)
                inverse(i, None if i == 0 else 0)
                for m in range(KD):
                    add_half(m, 1, LAST_BANKS[m % 6], dn_mm, chunk * KD, gate, dn_acc)
                    low(m)

            dve.wait_ge(tables_in, 16)
            dve.tensor_scalar(negsink[:, :], par[:, PC_SINK:PC_SINK + Q_TILES], -1.0, None,
                              ALU.mult).then_inc(dve_step, 1)
            steps = 1
            dve.tensor_copy(coef[:, C_BASE, :], par[:, PC_BCOND:PC_BCOND + KD])\
                .then_inc(coef_done, 1)
            dve.tensor_scalar(coef[:, C_BASE + 1, :], par[:, PC_BCOND + KD:PC_BCOND + 2 * KD], 1.0,
                              None, ALU.add).then_inc(coef_done, 1)
            dve.wait_ge(coef_done, 2)
            dve.wait_ge(cs_ready, 1)
            for k in range(KD):
                cond_block(2 * k % 4, k // 2, 1, k)
                cond_block((2 * k + 1) % 4, k // 2, 0, k)
                dve.wait_ge(crow_used, 2 * k + 2)
                dve.tensor_tensor(coef[:, C_SH0:C_SC0 + 1, k:k + 1], mod[:, 0:2, k:k + 1],
                                  coef[:, C_BASE:C_BASE + 2, k:k + 1], ALU.add)\
                    .then_inc(coef_done, 1)
                if k > 0:
                    first_low(k - 1)
            first_low(KD - 1)
            for k in range(KD):
                r = res[:, k, HALF:SEQ]
                dve.wait_ge(pre_h, 2 * k + 2)
                dve.tensor_scalar(r, r, ALPHA, None, ALU.mult).then_inc(r_scaled, 1)
            ffn_step(0, 0, 0, 0, 0, coef[:, C_G1, :], False)

            dve.wait_ge(pos_in, 16)
            dve.tensor_copy(ang[:, :], pos_i[:, :]).then_inc(rope_steps, 1)
            dve.wait_ge(rope_steps, 1)
            dve.tensor_scalar(ang[:, :], ang[:, :], par[:, PC_INV:PC_INV + 1], None, ALU.mult)\
                .then_inc(rope_steps, 1)
            step = 2
            for quarter, dst in ((0.25, turn), (0.0, ang)):
                dve.wait_ge(rope_steps, step)
                dve.tensor_scalar(turns[:, :], ang[:, :], 1.0 / TWO_PI, quarter, ALU.mult, ALU.add)\
                    .then_inc(rope_steps, 1)
                dve.wait_ge(rope_steps, step + 1)
                dve.tensor_scalar(turns[:, :], turns[:, :], ROUND, -ROUND, ALU.add, ALU.add)\
                    .then_inc(rope_steps, 1)
                src = ang
                for n, part in enumerate((CW1, CW2, CW3)):
                    dve.wait_ge(rope_steps, step + 2 + n)
                    dve.scalar_tensor_tensor(out=dst[:, :], in0=turns[:, :], scalar=-part,
                                             in1=src[:, :], op0=ALU.mult, op1=ALU.add)\
                        .then_inc(rope_steps, 1)
                    src = dst
                step += 5
                if quarter:
                    dve.wait_ge(rope_steps, step)
                    dve.tensor_scalar(dst[:, :], dst[:, :], quarter * TWO_PI, None, ALU.add)\
                        .then_inc(rope_steps, 1)
                    step += 1
                dve.wait_ge(rope_steps, step)
                dve.tensor_scalar(dst[:, :], dst[:, :], PI_BELOW, -PI_BELOW, ALU.min, ALU.max)\
                    .then_inc(rope_steps, 1)
                step += 1
                if quarter:
                    dve.wait_ge(r_scaled, KD)
                    dve.wait_ge(r_alpha, KD)
                    ffn_step(1, 0, 0, 0, 0, coef[:, C_G1, :], True, cond=True)
            with dve.Fori(2, N_COND - 1) as c:
                ffn_step(c, 0, 0, 0, 0, coef[:, C_G1, :], True, cond=True)
            LAST = FF_STEPS - 1
            with dve.Fori(N_COND - 1, LAST) as c:
                ffn_step(c, 0, 0, 0, 0, coef[:, C_G1, :], True)
            dve.wait_ge(trig_done, 2)
            dve.tensor_scalar(sin_t[:, :], sin_t[:, :], par[:, PC_SIGN:PC_SIGN + 1], None, ALU.mult)\
                .then_inc(sin_ready, 1)
            coefs = 2 + KD + N_COND - 2
            rows = ((4, 3, 0, C_ONE2, C_H1S, C_H1B, C_R1S, C_R1B),
                    (7, 6, 2, C_ONE3, C_H2S, C_H2B, C_R2S, C_R2B))
            for sc, sh, ln, one, hs, hb, rs, rb in rows:
                g = par[:, PC_LN + ln * KD:PC_LN + (ln + 1) * KD]
                b = par[:, PC_LN + (ln + 1) * KD:PC_LN + (ln + 2) * KD]
                dve.tensor_scalar(coef[:, one, :], mod[:, sc, :], 1.0, None, ALU.add)\
                    .then_inc(coef_done, 1)
                dve.wait_ge(coef_done, coefs + 1)
                dve.tensor_tensor(coef[:, hs, :], coef[:, one, :], g, ALU.mult)\
                    .then_inc(coef_done, 1)
                dve.tensor_tensor(coef[:, hb, :], coef[:, one, :], b, ALU.mult)\
                    .then_inc(coef_done, 1)
                dve.tensor_scalar(coef[:, rs, :], g, ALPHA, None, ALU.mult).then_inc(coef_done, 1)
                dve.tensor_scalar(coef[:, rb, :], b, ALPHA, None, ALU.mult).then_inc(coef_done, 1)
                dve.wait_ge(coef_done, coefs + 3)
                dve.tensor_tensor(coef[:, hb, :], coef[:, hb, :], mod[:, sh, :], ALU.add)\
                    .then_inc(coef_done, 1)
                coefs += 6
            dve.tensor_scalar(coef[:, C_G3, :], mod[:, 8, :], FFN_RES, None, ALU.mult)\
                .then_inc(coef_done, 1)
            coefs += 1
            dve.memset(kT[:, 0:CHUNK], 0.0).then_inc(carried, 1)
            dve.memset(vT[:, 0:CHUNK], 0.0).then_inc(carried, 1)
            dve.memset(ucarry[:, :, :], 0.0).then_inc(carried, 1)
            dve.wait_ge(coef_done, coefs)
            carries = 3

            last_step(4 * LAST, 2 * LAST, 2 * LAST, LAST, coef[:, C_G1, :], 0, 0,
                      lambda m: ln_low_h(0, m - 5) if m >= 5 else None)
            for k in range(3, KD):
                ln_low_h(0, k)
            dve.wait_ge(sin_ready, 1)

            for hf in range(2):
                ub = UPB_MIX[hf]
                toks = halves(hf)

                def rope(bank, dst, slot):
                    for a in range(4):
                        b = a ^ 1
                        dve.tensor_tensor(tmp[32 * a:32 * a + 32, slot, :],
                                          ps[32 * b:32 * b + 32, bank, :],
                                          sin_t[32 * b:32 * b + 32, toks], ALU.mult)\
                            .then_inc(dve_step, 1)
                    dve.tensor_tensor(dst, ps[:, bank, :], cos_t[:, toks], ALU.mult)\
                        .then_inc(proj_read, 1)

                def add_rope(dst, slot, n, reads):
                    dve.wait_ge(dve_step, n)
                    dve.wait_ge(proj_read, reads)
                    dve.tensor_tensor(dst, dst, tmp[:, slot, :], ALU.add).then_inc(qkv_ready, 1)

                for p in range(PROJ):
                    u, bank, m = ub + p, p % 4, p - ATT_FIRST
                    reads = hf * PROJ + p
                    if p == 0 and hf == 1:
                        dve.wait_ge(up_mm, u + 1)
                        dve.tensor_copy(kT[:, 0:CHUNK], kT[:, HALF:HALF + CHUNK])\
                            .then_inc(carried, 1)
                        dve.tensor_copy(vT[:, 0:CHUNK], vT[:, HALF:HALF + CHUNK])\
                            .then_inc(carried, 1)
                        carries += 2
                    if p == 3:
                        dve.wait_ge(vband_mm, hf + 1)
                        dve.tensor_copy(vband[:, :, :],
                                        ps[:, 6:8, :].rearrange("p b (c t) -> p (b c) t", t=P))\
                            .then_inc(vband_ready, 1)
                    if 0 <= m - LAG_V < N_CH:
                        v = m - LAG_V
                        dve.wait_ge(attn_hi_done, hf * N_CH + v + 1)
                        dst = slice(v * CHUNK, (v + 1) * CHUNK)
                        dve.tensor_tensor(
                            attn_lo[:, :, dst],
                            ps[:, 7, 0:Q_TILES * CHUNK].rearrange("p (j t) -> p j t", j=Q_TILES),
                            attn_hi[:, :, dst].bitcast(F32), ALU.subtract).then_inc(attn_ready, 1)
                    if 0 <= m < N_CH:
                        a = hf * N_CH + m
                        sm = small[:, a % 2, :, :]
                        score = ps[:, 4 + a % 2, :].rearrange("p (j t) -> p j t", j=Q_TILES)
                        dve.wait_ge(score_mm, a + 1)
                        if a == 0:
                            dve.memset(score[:, :, 0:CHUNK], MASKED).then_inc(dve_step, 1)
                            steps += 1
                            dve.wait_ge(dve_step, steps)
                        dve.tensor_reduce(sm[:, 0, :], score, AX.X, ALU.max).then_inc(dve_step, 1)
                        steps += 1
                        dve.wait_ge(dve_step, steps)
                        dve.scalar_tensor_tensor(out=sm[:, 1, :], in0=sm[:, 0, :], scalar=-SCALE,
                                                 in1=negsink[:, :], op0=ALU.mult, op1=ALU.min)\
                            .then_inc(dve_step, 1)
                        steps += 1
                        dve.wait_ge(dve_step, steps)
                        dve.tensor_tensor(sm[:, 2, :], sm[:, 1, :], negsink[:, :], ALU.subtract)\
                            .then_inc(negmax_done, 1)
                        dve.wait_ge(exp_done, a + 1)
                        dve.tensor_tensor(sm[:, 5, :], sm[:, 3, :], sm[:, 4, :], ALU.add)\
                            .then_inc(dve_step, 1)
                        steps += 1
                        dve.wait_ge(dve_step, steps)
                        dve.reciprocal(sm[:, 5, :], sm[:, 5, :]).then_inc(dve_step, 1)
                        steps += 1
                        dve.wait_ge(dve_step, steps)
                        dve.tensor_tensor(
                            prob[:, a % 2, :, :], prob[:, a % 2, :, :],
                            sm[:, 5, :].rearrange("p (j o) -> p j o", o=1)
                            .to_broadcast([P, Q_TILES, P]), ALU.mult).then_inc(probs_ready, 1)
                    if p >= 9 and p % 3 == 0:
                        i = p // 3 - 3
                        dve.wait_ge(conv_hi_done, hf * CONV_TILES + i + 1)
                        dve.tensor_tensor(conv_lo[:, i, :], tmp[:, 2, :],
                                          conv_hi[:, i, :].bitcast(F32), ALU.subtract)\
                            .then_inc(conv_ready, 1)
                    dve.wait_ge(up_mm, u + 1)
                    if p == 0:
                        dve.wait_ge(carried, carries)
                        rope(bank, kT[:, CHUNK:CHUNK + HALF], p % 2)
                        steps += 4
                        add_rope(kT[:, CHUNK:CHUNK + HALF], p % 2, steps, reads + 1)
                    elif p == 1:
                        dve.tensor_copy(vT[:, CHUNK:CHUNK + HALF], ps[:, bank, :])\
                            .then_inc(proj_read, 1)
                    elif p < 2 + Q_TILES:
                        dve.wait_ge(qkv_ready, hf * (1 + Q_TILES) + p - 1)
                        rope(bank, qT[:, p - 2, :], p % 2)
                        steps += 4
                        add_rope(qT[:, p - 2, :], p % 2, steps, reads + 1)
                    elif p % 3 == 0:
                        dve.tensor_copy(tmp[:, 0, :], ps[:, bank, :]).then_inc(proj_read, 1)
                    elif p % 3 == 1:
                        i = p // 3 - 2
                        dve.wait_ge(proj_read, reads)
                        dve.tensor_copy(ubuf[:, 0:CONV_K - 1], ucarry[:, i, :])\
                            .then_inc(dve_step, 1)
                        dve.tensor_tensor(ubuf[:, CONV_K - 1:], ps[:, bank, :], tmp[:, 0, :],
                                          ALU.mult).then_inc(proj_read, 1)
                        dve.wait_ge(proj_read, reads + 1)
                        dve.tensor_copy(ucarry[:, i, :], ubuf[:, HALF:HALF + CONV_K - 1])\
                            .then_inc(dve_step, 1)
                        steps += 2
                        dve.wait_ge(dve_step, steps)
                        for j in range(CONV_K):
                            tap = CONV_K - 1 - j
                            w = par[:, PC_CONV + tap * CONV_TILES + i:
                                    PC_CONV + tap * CONV_TILES + i + 1]
                            if j == 0:
                                dve.tensor_scalar(tmp[:, 1, :], ubuf[:, tap:tap + HALF], w, None,
                                                  ALU.mult).then_inc(dve_step, 1)
                            else:
                                dve.wait_ge(dve_step, steps)
                                dve.scalar_tensor_tensor(out=tmp[:, 1, :],
                                                         in0=ubuf[:, tap:tap + HALF], scalar=w,
                                                         in1=tmp[:, 1, :], op0=ALU.mult,
                                                         op1=ALU.add).then_inc(dve_step, 1)
                            steps += 1
                    else:
                        dve.wait_ge(dve_step, steps)
                        i = p // 3 - 2
                        if i >= 1:
                            dve.wait_ge(conv_ready, hf * CONV_TILES + i)
                        dve.tensor_tensor(tmp[:, 2, :], ps[:, bank, :], tmp[:, 1, :], ALU.mult)\
                            .then_inc(proj_read, 1)
                        dve.wait_ge(proj_read, reads + 1)
                        dve.sem_inc(conv_done, 1)
                dve.wait_ge(conv_hi_done, (hf + 1) * CONV_TILES)
                dve.tensor_tensor(conv_lo[:, CONV_TILES - 1, :], tmp[:, 2, :],
                                  conv_hi[:, CONV_TILES - 1, :].bitcast(F32), ALU.subtract)\
                    .then_inc(conv_ready, 1)

                mb, tb, gb, cb = ub + PROJ, TL_MIX[hf], GR_MIX[hf], CH_MIX[hf]

                def add_merged(chunk):
                    for m in range(KD):
                        dve.wait_ge(dn_mm, chunk * KD + (m + 1))
                        dve.scalar_tensor_tensor(out=res[:, m, toks], in0=ps[:, 4 + m % 4, :],
                                                 scalar=mod[:, 5, m:m + 1], in1=res[:, m, toks],
                                                 op0=ALU.mult, op1=ALU.add).then_inc(dn_acc, 1)

                def merge_tile(i, s):
                    t = i * 2 + (tb + s)
                    dve.wait_ge(gate_read, i * 4 + (gb + 2 * s + 2))
                    dve.wait_ge(up_mm, i * 6 + (mb + 3 * s + 3))
                    dve.wait_ge(g_ready, t)
                    for b in range(2):
                        dve.tensor_tensor(tmp[:, 2 + b, :], tmp[:, b, :], ps[:, 2 + b, :],
                                          ALU.mult).then_inc(merge_parts, 1)
                    dve.wait_ge(merge_parts, i * 4 + ((tb + s - TL_FFN) * 2 + 2))
                    dve.tensor_tensor(tmp[:, 2, :], tmp[:, 2, :], tmp[:, 3, :], ALU.add)\
                        .then_inc(prod_done, 1)

                def merge_low(i, s):
                    dve.wait_ge(g_hi_done, i * 2 + (tb + s + 1))
                    dve.tensor_tensor(mg_lo[:, s, :], tmp[:, 2, :], mg_hi[:, s, :].bitcast(F32),
                                      ALU.subtract).then_inc(g_ready, 1)

                def merge_step(i):
                    merge_tile(i, 0)
                    add_merged(i + (cb - 1))
                    merge_low(i, 0)
                    split_down(i + cb)
                    merge_tile(i, 1)
                    merge_low(i, 1)

                ln = 1 + hf
                centre_and_square(ln, 0, KD + 2)
                inverse(ln)
                merge_tile(0, 0)
                dve.wait_ge(ln_rstd, ln + 1)
                ln_input(ln, 0, 4)
                merge_low(0, 0)
                split_down(cb)
                ln_input(ln, 4, 7)
                merge_tile(0, 1)
                merge_low(0, 1)
                ln_input(ln, 7, KD + 2)
                if hf == 0:
                    scale_residual(0, coef[:, C_R1S, :], coef[:, C_R1B, :])
                    scale_residual(1, coef[:, C_R1S, :], coef[:, C_R1B, :])
                else:
                    scale_residual(2, coef[:, C_R2S, :], coef[:, C_R2B, :])
                dve.wait_ge(r_scaled, (3, 4)[hf] * KD)
                with dve.Fori(1, MIX_STEPS) as i:
                    merge_step(i)
                add_merged(cb + MIX_STEPS - 1)

            gate = coef[:, C_G3, :]
            u, t, g = UPB_FFN2, TL_FFN2, GR_FFN2
            centre_and_square(3, 0, 4)
            half_product(u, t, g)
            centre_and_square(3, 4, KD + 2)
            half_low(0, t)
            split_down(CH_FFN2)
            inverse(3)
            half_product(u + 2, t + 1, g + 1)
            half_low(1, t + 1)
            for m in range(KD):
                add_half(m, 0, 4 + m % 4, half_mm, KD, gate, half_acc)
                if m >= 2:
                    ln_low_h(3, m - 2)
            for k in range(KD - 2, KD):
                ln_low_h(3, k)
            for n in range(2, 4):
                half_product(u + 2 * n, t + n, g + n)
                half_low(n, t + n)
            scale_residual(3, coef[:, C_R2S, :], coef[:, C_R2B, :])
            dve.wait_ge(r_scaled, 5 * KD)
            ffn_step(1, TL_FFN2 + 2, GR_FFN2 + 2, UPB_FFN2 + 4, CH_FFN2, gate, "half")
            with dve.Fori(2, LAST) as c:
                ffn_step(c, TL_FFN2 + 2, GR_FFN2 + 2, UPB_FFN2 + 4, CH_FFN2, gate, True)

            def sum_pair(m):
                if m in (5, 7):
                    dve.wait_ge(dn_acc, (CH_FFN2 + LAST) * KD + m + 1)
                    r = res[:, :, halves(1)]
                    dve.tensor_tensor(tmp[:, (m - 5) // 2, :], r[:, m - 1, :], r[:, m, :], ALU.add)\
                        .then_inc(ln_pair, 1)
                if m == 7:
                    inverse(4, 1)

            last_step(UPB_FFN2 + 4 + 4 * LAST, TL_FFN2 + 2 + 2 * LAST, GR_FFN2 + 2 + 2 * LAST,
                      CH_FFN2 + LAST, gate, 2 * KD, 4, sum_pair)
            for k in range(KD):
                centre(5, k)
            dve.wait_ge(ln_sq, 6 * KD)
            dve.tensor_tensor(ln_tmp[:, 2, :], ln_tmp[:, 2, :], ln_tmp[:, 3, :], ALU.add)\
                .then_inc(ln_pair, 1)
            inverse(5)
            dve.wait_ge(ln_rstd, 6)
            for k in range(KD):
                r = res[:, k, halves(1)]
                g = PC_LN + 4 * KD + k
                dve.scalar_tensor_tensor(out=r, in0=r, scalar=par[:, g:g + 1], in1=inv_row(5),
                                         op0=ALU.mult, op1=ALU.mult).then_inc(ln_scaled, 1)

        @block.tensor
        def _(pe):
            def passes(w_hi, w_lo, v_hi, v_lo):
                return ((w_hi, v_hi), (w_hi, v_lo), (w_lo, v_hi))

            def up_granule(slot, half_list, out_of, ks=range(KD), v_hi=h_hi, v_lo=h_lo,
                           last=True, tokens=None, ready=None, ready_at=None, k_of=None,
                           begin=0, end=KD - 1):
                for hf in half_list:
                    toks = halves(hf) if tokens is None else tokens
                    for k in ks:
                        if ready is not None:
                            pe.wait_ge(ready, ready_at(hf, k))
                        kv = k if k_of is None else k_of(k)
                        for n, (w, v) in enumerate(passes(up_hi, up_lo, v_hi, v_lo)):
                            mm = pe.matmul(out_of(hf), w[:, slot, k, :], v[:, kv, toks],
                                           start=(k == begin and n == 0),
                                           stop=(k == end and n == 2))
                if last:
                    mm.then_inc(up_mm, 1)

            def up_pair(u, hf, banks, ready_from):
                waited = -1
                for slot, k in PAIR_ORDER:
                    if k > waited:
                        pe.wait_ge(h_ready, ready_from + k + 1)
                        waited = k
                    if (slot, k) == (1, 0):
                        pe.wait_ge(up_lo_done, u + 2)
                    up_granule(slot, [hf], lambda h: ps[:, banks[slot], :], ks=[k],
                               last=(k == KD - 1))

            def down_tile(m, half_list, out_of, v_hi, v_lo, toks_of):
                for hf in half_list:
                    for s in range(2):
                        for n, (w, v) in enumerate(passes(dn_hi, dn_lo, v_hi, v_lo)):
                            mm = pe.matmul(out_of(hf), w[:, s, m * P:(m + 1) * P],
                                           v[:, s, toks_of(hf)], start=(s == 0 and n == 0),
                                           stop=(s == 1 and n == 2))
                mm.then_inc(dn_mm, 1)

            def ffn_down(chunk, more):
                pe.wait_ge(dn_lo_done, chunk * 2 + 2)
                pe.wait_ge(g_ready, chunk * 2 + (2 + more))
                for m in range(KD):
                    if not isinstance(chunk, int) or chunk > 0 or m >= 2:
                        pe.wait_ge(dn_acc, chunk * KD + (m - 1))
                    down_tile(m, range(2), lambda hf: ps[:, 4 + 2 * (m % 2) + hf, :], g_hi, g_lo,
                              halves)

            def half_up(u, n, t, g, mean_at=None, variance_at=None, i=None, ready=None):
                for s in range(2):
                    pe.wait_ge(up_lo_done, u + s + 1)
                    if s == 0:
                        pe.wait_ge(gate_read, g)
                    else:
                        pe.wait_ge(prod_done, t)
                    for k in range(KD):
                        up_granule(s, [n // 2], lambda hf: ps[:, s, :], ks=[k],
                                   ready=None if s else ready,
                                   ready_at=lambda hf, k: 5 * KD + k + 1, last=(k == KD - 1))
                        if (s, k) == mean_at:
                            mean(i)
                        if (s, k) == variance_at:
                            variance(i)

            def half_down(m, hf, ss, bank, mm_sem):
                for s in ss:
                    for j, (w, v) in enumerate(passes(dn_hi, dn_lo, g_hi, g_lo)):
                        mm = pe.matmul(ps[:, bank, :], w[:, s, m * P:(m + 1) * P],
                                       v[:, s, halves(hf)], start=(s == 0 and j == 0),
                                       stop=(s == 1 and j == 2))
                if ss[-1] == 1:
                    mm.then_inc(mm_sem, 1)

            def first_half_down(chunk, t, halves_before, early=0):
                pe.wait_ge(dn_lo_done, chunk * 2 + 2)
                pe.wait_ge(g_ready, t + (1 if early else 2))
                pe.wait_ge(dn_acc, chunk * KD)
                for m in range(early):
                    half_down(m, 0, (0,), 4 + m % 4, half_mm)
                if early:
                    pe.wait_ge(g_ready, t + 2)
                for m in range(KD):
                    if m >= 4:
                        pe.wait_ge(half_acc, halves_before + m - 3)
                    half_down(m, 0, (0, 1) if m >= early else (1,), 4 + m % 4, half_mm)

            def last_step(u, t, g, chunk, more, halves_before, i):
                half_up(u, 0, t, g)
                ffn_down(chunk - 1, more)
                for n in range(1, 3):
                    half_up(u + 2 * n, n, t + n, g + n)
                first_half_down(chunk, t, halves_before)

                half_up(u + 6, 3, t + 3, g + 3, mean_at=(0, 3), i=i)
                pe.wait_ge(half_acc, halves_before + KD)
                for m in range(6):
                    if m == 3:
                        variance(i)
                    if m == 4:
                        pe.wait_ge(prod_done, t + 4)
                    half_down(m, 1, (0,), LAST_BANKS[m], dn_mm)
                pe.wait_ge(g_ready, t + 4)
                for m in range(KD):
                    if m >= 6:
                        pe.wait_ge(dn_acc, chunk * KD + m - 5)
                    half_down(m, 1, (1,) if m < 6 else (0, 1), LAST_BANKS[m % 6], dn_mm)

            def ffn_step(c, ub, tb, gb, cb, down, more=0):
                for s in range(2):
                    t = c * 2 + (tb + s)
                    if isinstance(c, int) and c == 0 and s == 0:
                        for w, k in ([(0, 0)] + [(w, k - w) for k in range(1, KD)
                                                 for w in range(2)] + [(1, KD - 1)]):
                            if k == 0:
                                pe.wait_ge(up_lo_done, w + 1)
                            for hf in range(2):
                                if w == 0:
                                    pe.wait_ge(h_ready, 2 * k + hf + 1)
                                up_granule(w, [hf], lambda h: ps[:, 2 * w + h, :], ks=[k],
                                           last=(k == KD - 1 and hf == 1))
                        continue
                    pe.wait_ge(up_lo_done, c * 4 + (ub + 2 * s + 1))
                    pe.wait_ge(gate_read, c * 2 + (gb + s))
                    if down == "half" and s == 0:
                        up_granule(0, [0], lambda hf: ps[:, hf, :], last=False)
                        pe.wait_ge(prod_done, t)
                        up_granule(0, [1], lambda hf: ps[:, hf, :])
                    else:
                        up_granule(0, range(2), lambda hf: ps[:, hf, :])
                    pe.wait_ge(up_lo_done, c * 4 + (ub + 2 * s + 2))
                    pe.wait_ge(prod_done, t)
                    up_granule(1, range(2), lambda hf: ps[:, 2 + hf, :])
                    if s == 0 and down == "half":
                        chunk = c + (cb - 1)
                        pe.wait_ge(g_ready, TL_FFN2 + 4)
                        for m in range(KD):
                            if m < 4:
                                pe.wait_ge(half_acc, KD + 5 + m)
                            else:
                                pe.wait_ge(dn_acc, chunk * KD + m - 3)
                            half_down(m, 1, (0, 1), 4 + m % 4, dn_mm)
                    elif s == 0 and down:
                        ffn_down(c + (cb - 1), more)

            def mean(i):
                pe.wait_ge(ln_sum, i + 1)
                if i == 5:
                    pe.wait_ge(ln_centred, i * KD)
                parts = [presum[:, i % 2, :]] + ([tmp[:, 0, :], tmp[:, 1, :]] if i == 5 else [])
                for n, part in enumerate(parts):
                    if n:
                        pe.wait_ge(ln_pair, n)
                    mm = pe.matmul(ps[:, LN_BANKS[i][0], :], mean_m[:, :], part, start=(n == 0),
                                   stop=(n == len(parts) - 1))
                mm.then_inc(ln_mean, 1)

            def variance(i):
                pe.wait_ge(ln_sqadd, (i + 1) * (KD - 1))
                if i > 0:
                    pe.wait_ge(ln_std, i)
                pe.matmul(ps[:, LN_BANKS[i][1], :], mean_m[:, :], presum[:, 1 - i % 2, :],
                          start=True, stop=True).then_inc(ln_sqmm, 1)

            def mean_square(i, k):
                if k < KD - 2:
                    pe.wait_ge(ln_sq, i * KD + k + 1)
                else:
                    pe.wait_ge(ln_pair, 3)
                if k == 0:
                    pe.wait_ge(ln_std, i)
                pe.matmul(ps[:, LN_BANKS[i][1], :], mean_m[:, :], ln_tmp[:, k % 4, :],
                          start=(k == 0), stop=(k == KD - 2)).then_inc(ln_sqmm, 1)

            pe.wait_ge(up_lo_done, 1)
            ffn_step(0, 0, 0, 0, 0, False)
            LAST = FF_STEPS - 1
            ffn_step(1, 0, 0, 0, 0, True)
            with pe.Fori(2, LAST) as c:
                ffn_step(c, 0, 0, 0, 0, True)
            pe.wait_ge(tables_in, 48)
            last_step(4 * LAST, 2 * LAST, 2 * LAST, LAST, 0, 0, 0)

            for hf in range(2):
                ub = UPB_MIX[hf]
                acc0 = CH_MIX[hf] * KD

                def project(hf, p):
                    u = UPB_MIX[hf] + p
                    pe.wait_ge(up_lo_done, u + 1)
                    if p >= 4:
                        pe.wait_ge(proj_read, hf * PROJ + p - 3)
                    elif hf == 1 and p == 0:
                        pe.wait_ge(gate_read, GR_MIX[1])
                    elif hf == 1:
                        pe.wait_ge(prod_done, TL_MIX[1])
                    elif p == 2:
                        pe.wait_ge(ln_std, 1)
                    up_granule(u % 2, [hf], lambda h: ps[:, p % 4, :],
                               ready=h_ready if p == 0 else None,
                               ready_at=lambda h, k: (2 + h) * KD + k + 1)

                for p in range(PROJ):
                    m = p - ATT_FIRST
                    if p == 3:
                        pe.wait_ge(proj_read, hf * PROJ + 2)
                        pe.wait_ge(dn_acc, acc0)
                        for n in range(N_CH):
                            mm = pe.transpose(ps[:, 6 + n // 4, (n % 4) * P:(n % 4 + 1) * P],
                                              vT[:, n * CHUNK:n * CHUNK + P], eye[:, :])
                        mm.then_inc(vband_mm, 1)
                    if 0 <= m - LAG_V < N_CH:
                        v = m - LAG_V
                        a = hf * N_CH + v
                        pe.wait_ge(probT_ready, a + 1)
                        pe.wait_ge(vband_ready, hf + 1)
                        if v >= 1:
                            pe.wait_ge(attn_ready, a)
                        for g in range(2):
                            rows = slice(g * HEAD_DIM, (g + 1) * HEAD_DIM)
                            mm = pe.matmul(ps[rows, 7, 0:Q_TILES * CHUNK], vband[:, v, rows],
                                           probT[:, a % 2, :, rows], start=True, stop=True)
                        mm.then_inc(av_mm, 1)
                    if 0 <= m - LAG_T < N_CH:
                        a = hf * N_CH + m - LAG_T
                        pe.wait_ge(probs_ready, a + 1)
                        pe.wait_ge(vband_ready, hf + 1)
                        if a >= 1:
                            pe.wait_ge(probT_ready, a)
                        for j in range(Q_TILES):
                            mm = pe.transpose(ps[:, 6, j * P:(j + 1) * P], prob[:, a % 2, j, :],
                                              eye[:, :])
                        mm.then_inc(probT_mm, 1)
                    if 0 <= m < N_CH:
                        a = hf * N_CH + m
                        pe.wait_ge(qkv_ready, (hf + 1) * (1 + Q_TILES))
                        if a >= 2:
                            pe.wait_ge(exp_done, a - 1)
                        for j in range(Q_TILES):
                            for g in range(2):
                                rows = slice(g * HEAD_DIM, (g + 1) * HEAD_DIM)
                                mm = pe.matmul(ps[rows, 4 + a % 2, j * P:(j + 1) * P],
                                               qT[rows, j, m * CHUNK:(m + 1) * CHUNK],
                                               kT[rows, m * CHUNK:m * CHUNK + P],
                                               start=True, stop=True)
                        mm.then_inc(score_mm, 1)
                    if p == 0 and hf == 0:
                        pe.wait_ge(up_lo_done, ub + 1)
                        pe.wait_ge(dn_acc, acc0 - 2)
                        up_pair(ub, 0, (0, 1), 2 * KD)
                    elif p > hf ^ 1:
                        project(hf, p)

                mb, tb, gb, cb = ub + PROJ, TL_MIX[hf], GR_MIX[hf], CH_MIX[hf]
                ln = 1 + hf

                def merge_down(chunk):
                    pe.wait_ge(dn_lo_done, chunk * 2 + 2)
                    pe.wait_ge(g_ready, chunk * 2 + (2 + TL_MIX[0] - 2 * CH_MIX[0]))
                    for m in range(KD):
                        pe.wait_ge(dn_acc, chunk * KD + (m - 3))
                        down_tile(m, [hf], lambda h: ps[:, 4 + m % 4, :], mg_hi, mg_lo,
                                  lambda h: slice(0, HALF))

                def merge_step(i, down):
                    for s in range(2):
                        t = i * 2 + (tb + s)
                        for b in range(2):
                            slot = (3 * s + b) % 2
                            pe.wait_ge(up_lo_done, i * 6 + (mb + 3 * s + b + 1))
                            pe.wait_ge(gate_read, i * 4 + (gb + 2 * s + b - 1))
                            if s == 0 and not down:
                                pe.wait_ge(proj_read, hf * PROJ + PROJ - 1 + b)
                            if s == 0 and b == 0 and not down:
                                up_granule(slot, [hf], lambda h: ps[:, b, :], ks=range(2),
                                           last=False)
                                pe.wait_ge(attn_ready, (hf + 1) * N_CH)
                                pe.wait_ge(ln_sum, ln + 1)
                                pe.matmul(ps[:, LN_BANKS[ln][0], :], mean_m[:, :], tmp[:, 3, :],
                                          start=True, stop=True).then_inc(ln_mean, 1)
                                up_granule(slot, [hf], lambda h: ps[:, b, :],
                                           ks=range(2, KD))
                            else:
                                up_granule(slot, [hf], lambda h: ps[:, b, :])
                        slot = (3 * s + 2) % 2
                        pe.wait_ge(up_lo_done, i * 6 + (mb + 3 * s + 3))
                        pe.wait_ge(prod_done, t)
                        if isinstance(i, int):
                            pe.wait_ge(attn_ready, (hf + 1) * N_CH)
                            pe.wait_ge(conv_ready, (hf + 1) * CONV_TILES)
                        up_granule(slot, [hf], lambda h: ps[:, 2, :], ks=range(0, 4),
                                   v_hi=conv_hi, v_lo=conv_lo, last=False, tokens=slice(0, HALF),
                                   end=3)
                        if s == 0 and not down:
                            variance(ln)
                        up_granule(slot, [hf], lambda h: ps[:, 3, :], ks=range(4, 8),
                                   v_hi=attn_hi, v_lo=attn_lo, tokens=slice(0, HALF),
                                   k_of=lambda k: k - 4, begin=4)
                        if s == 0 and down:
                            merge_down(i + (cb - 1))

                merge_step(0, False)
                pe.wait_ge(ln_std, 2 + hf)
                with pe.Fori(1, MIX_STEPS) as i:
                    merge_step(i, True)
                if hf == 0:
                    project(1, 0)
                    merge_down(cb + MIX_STEPS - 1)

            u, t, g = UPB_FFN2, TL_FFN2, GR_FFN2
            pe.wait_ge(up_lo_done, u + 1)
            pe.wait_ge(gate_read, g)
            up_granule(0, [0], lambda hf: ps[:, 0, :], ready=h_ready,
                       ready_at=lambda hf, k: 4 * KD + k + 1)
            merge_down(CH_FFN2 - 1)
            pe.wait_ge(up_lo_done, u + 2)
            for k in range(KD):
                up_granule(1, [0], lambda hf: ps[:, 1, :], ks=[k], last=(k == KD - 1))
                if k == 4:
                    mean(3)
            half_up(u + 2, 1, t + 1, g + 1, variance_at=(1, 4), i=3)
            first_half_down(CH_FFN2, t, KD, 4)
            half_up(u + 4, 2, t + 2, g + 2, ready=h_ready)
            half_up(u + 6, 3, t + 3, g + 3)
            ffn_step(1, UPB_FFN2 + 4, TL_FFN2 + 2, GR_FFN2 + 2, CH_FFN2, "half")
            with pe.Fori(2, LAST) as c:
                ffn_step(c, UPB_FFN2 + 4, TL_FFN2 + 2, GR_FFN2 + 2, CH_FFN2, True, more=4)
            last_step(UPB_FFN2 + 4 + 4 * LAST, TL_FFN2 + 2 + 2 * LAST, GR_FFN2 + 2 + 2 * LAST,
                      CH_FFN2 + LAST, 4, 2 * KD, 4)
            mean(5)
            for k in range(KD - 1):
                mean_square(5, k)


def tiles_of(w):
    n = w.shape[1] // P
    return w.reshape(-1, P, n, P).transpose(2, 1, 0, 3).reshape(n, P, -1)


def interleaved(*lists):
    return np.stack(lists, axis=1).reshape(-1, *lists[0].shape[1:])


def kernel(**inputs):
    import concourse.bacc as bacc
    from concourse.bass_utils import run_bass_kernel_spmd

    a = {k: np.asarray(v) for k, v in inputs.items()}
    w = {k: a[k][0] for k in a if k not in ("x", "c", "positions")}
    f32 = np.float32

    def columns(v):
        return v.reshape(-1, P).T

    pair = np.concatenate([np.arange(h * HEAD_DIM, (h + 1) * HEAD_DIM)
                           for j in range(Q_TILES) for h in (j, j + Q_TILES)])
    q_w, kv_w, conv_w3, merge_w = np.split(
        w["w_in"], [Q_HEADS * HEAD_DIM, Q_HEADS * HEAD_DIM + 2 * P,
                    Q_HEADS * HEAD_DIM + 2 * P + 3 * CONV_WIDTH], axis=1)
    gate_b, gate_c, conv_x = np.split(conv_w3, 3, axis=1)
    merge_a, merge_c = np.split(merge_w, 2, axis=1)
    branches = np.concatenate([tiles_of(w["w_branch_conv"]),
                               tiles_of(w["w_branch_attn"][pair])], axis=2)
    up_w = np.concatenate([
        interleaved(tiles_of(w["ffn1_w1"]), tiles_of(w["ffn1_w3"])),
        tiles_of(kv_w), tiles_of(q_w[:, pair]),
        interleaved(tiles_of(gate_c), tiles_of(conv_x), tiles_of(gate_b)),
        interleaved(tiles_of(merge_c), tiles_of(merge_a), branches),
        interleaved(tiles_of(w["ffn2_w1"]), tiles_of(w["ffn2_w3"]))])
    down_w = np.concatenate([w["ffn1_w2"], w["w_out"], w["ffn2_w2"]]).reshape(-1, P, D)
    w_cond = w["w_cond"].T.reshape(N_COND, KD, P, D)
    sinks = np.repeat(w["attn_sinks"].reshape(2, Q_TILES), HEAD_DIM, axis=0)
    half = HEAD_DIM // 2
    freq = (ROPE_THETA ** (-np.arange(half) / half)).astype(f32)
    sign = np.where(np.arange(P) % HEAD_DIM < half, 1.0, -1.0)
    table = np.concatenate(
        [columns(w["b_cond"])]
        + [columns(w[n]) for n in ("ln1_g", "ln1_b", "ln2_g", "ln2_b", "ln3_g", "ln3_b")]
        + [columns(w["conv_w"]), sinks, np.tile(freq, P // half)[:, None],
           sign[:, None].astype(f32), np.ones((P, 1), f32),
           np.full((P, 1), LN_EPS, f32)], axis=1)
    mean_w = np.stack([np.full((P, P), 1.0 / D, f32), np.eye(P, dtype=f32)])
    arrays = {
        "x_t": a["x"][0].T.reshape(KD, P, SEQ).transpose(1, 0, 2),
        "c": a["c"].reshape(1, D), "positions": a["positions"], "table": table, "mean_w": mean_w, "w_cond": w_cond,
        "up_w": up_w, "down_w": down_w,
    }
    arrays = {n: np.ascontiguousarray(v) for n, v in arrays.items()}
    nc = bacc.Bacc("TRN2", target_bir_lowering=False, num_devices=1, dynamic_dma_scratch_size=1024)
    args = [nc.dram_tensor(n, v.shape, mybir.dt.from_np(v.dtype), kind="ExternalInput").ap()
            for n, v in arrays.items()]
    out = nc.dram_tensor("out_t", (P, KD, SEQ), F32, kind="ExternalOutput").ap()
    encoder_block(nc, *args, out)
    got = run_bass_kernel_spmd(nc, [arrays], core_ids=[0]).results[0]["out_t"]
    return got.transpose(2, 1, 0).reshape(1, SEQ, D)
```
